# Optimizing a Trainium2 kernel written in Bass

```python
import jax, jax.numpy as jnp
from jax import lax
import numpy as np

D_MODEL = 1024
BATCH = 1
SEQ = 1024
DEPTH = 1

EPS = 1e-6
RWKV_HEADS = 8
RWKV_HEAD_DIM = 64
D_RWKV = RWKV_HEADS * RWKV_HEAD_DIM
DECAY_LORA = 64
AAA_LORA = 64
GATE_LORA = 128
LN_X_EPS = 64e-5
MLA_HEADS = 8
QK_NOPE_DIM = 64
QK_ROPE_DIM = 32
QK_HEAD_DIM = QK_NOPE_DIM + QK_ROPE_DIM
V_HEAD_DIM = 64
D_MLA = MLA_HEADS * V_HEAD_DIM
Q_LORA = 256
KV_LORA = 128
ROPE_THETA = 10000.0
Q_BLOCK = 128
RWKV_COLS = 3 * D_RWKV + DECAY_LORA + AAA_LORA + GATE_LORA
MLA_COLS = Q_LORA + KV_LORA + QK_ROPE_DIM
N_BRANCHES = 2
D_IN = RWKV_COLS + MLA_COLS + N_BRANCHES * D_MODEL
D_BRANCH = 512
N_GROUPS = 4
EXPERTS_PER_GROUP = 8
N_EXPERTS = N_GROUPS * EXPERTS_PER_GROUP
TOP_K = 2
D_EXPERT = 256

kernel_name = "hybrid_rwkv7_mla_hmoe_adaln_block"

def rmsnorm(x, g):
    xf = x.astype(jnp.float32)
    y = xf * lax.rsqrt(jnp.mean(xf * xf, axis=-1, keepdims=True) + EPS)
    return (y * g.astype(jnp.float32)).astype(x.dtype)

def modulate(h, shift, scale):
    return h * (1 + scale[:, None, :]) + shift[:, None, :]

def token_shift(z):
    return jnp.pad(z, ((0, 0), (1, 0), (0, 0)))[:, :-1]

def rope(x, cos, sin):
    x1, x2 = jnp.split(x, 2, axis=-1)
    return jnp.concatenate([x1 * cos - x2 * sin, x2 * cos + x1 * sin], axis=-1)

def rwkv7_scan(r, w, k, v, kk, b):
    bsz, _, nh, n = r.shape
    xs = tuple(jnp.moveaxis(t.astype(jnp.float32), 1, 0) for t in (r, w, k, v, kk, b))

    def step(state, inp):
        r_t, w_t, k_t, v_t, kk_t, b_t = inp
        sa = jnp.einsum('bhij,bhj->bhi', state, -kk_t)
        state = (state * w_t[:, :, None, :]
                 + sa[..., None] * b_t[:, :, None, :]
                 + v_t[..., None] * k_t[:, :, None, :])
        y = jnp.einsum('bhij,bhj->bhi', state, r_t)
        return state, y

    state0 = jnp.zeros((bsz, nh, n, n), jnp.float32)
    _, ys = lax.scan(step, state0, xs)
    return jnp.moveaxis(ys, 0, 1)

def rwkv7_branch(z, mu, w0, w_decay_up, a0, w_a_up, w_g_up, k_k, k_a, r_k, ln_w, ln_b):
    bsz, s, _ = z.shape
    z = z + (token_shift(z) - z) * mu
    zr, zk, zv, zw, za, zg = jnp.split(
        z, [D_RWKV, 2 * D_RWKV, 3 * D_RWKV, 3 * D_RWKV + DECAY_LORA,
            3 * D_RWKV + DECAY_LORA + AAA_LORA], axis=-1)
    w_log = -jax.nn.softplus(-(w0 + jnp.tanh(zw) @ w_decay_up)) - 0.5
    decay = jnp.exp(-jnp.exp(w_log.astype(jnp.float32)))
    a = jax.nn.sigmoid(a0 + za @ w_a_up)
    g = jax.nn.sigmoid(zg) @ w_g_up

    heads = lambda t: t.reshape(bsz, s, RWKV_HEADS, RWKV_HEAD_DIM)
    kk = heads(zk * k_k).astype(jnp.float32)
    kk = kk / jnp.maximum(jnp.sqrt(jnp.sum(kk * kk, axis=-1, keepdims=True)), 1e-12)
    k = zk * (1 + (a - 1) * k_a)
    r_h, k_h, v_h, a_h = heads(zr), heads(k), heads(zv), heads(a)

    y = rwkv7_scan(r_h, heads(decay), k_h, v_h, kk, kk * a_h)
    mean = jnp.mean(y, axis=-1, keepdims=True)
    var = jnp.mean(jnp.square(y - mean), axis=-1, keepdims=True)
    y = ((y - mean) * lax.rsqrt(var + LN_X_EPS)).reshape(bsz, s, D_RWKV)
    y = (y * ln_w.astype(jnp.float32) + ln_b.astype(jnp.float32)).astype(z.dtype)
    bonus = jnp.sum(r_h * k_h * r_k, axis=-1, keepdims=True) * v_h
    return (y + bonus.reshape(bsz, s, D_RWKV)) * g

def causal_attention(q, k, v):
    bsz, s, nh, dv = v.shape
    q = q.transpose(0, 2, 1, 3)
    k = k.transpose(0, 2, 1, 3)
    v = v.transpose(0, 2, 1, 3)
    scale = QK_HEAD_DIM ** -0.5
    kpos = jnp.arange(s)

    def block(i):
        start = i * Q_BLOCK
        qb = lax.dynamic_slice_in_dim(q, start, Q_BLOCK, axis=2)
        sc = jnp.einsum('bhqd,bhkd->bhqk', qb, k).astype(jnp.float32) * scale
        qpos = start + jnp.arange(Q_BLOCK)
        sc = jnp.where(kpos[None, :] <= qpos[:, None], sc, -jnp.inf)
        p = jax.nn.softmax(sc, axis=-1).astype(v.dtype)
        return jnp.einsum('bhqk,bhkd->bhqd', p, v)

    o = lax.map(block, jnp.arange(s // Q_BLOCK))
    return o.transpose(1, 0, 3, 2, 4).reshape(bsz, s, nh, dv)

def mla_branch(z, cos, sin, g_q_a, w_uq, g_kv_a, w_ukv, q_norm, k_norm):
    bsz, s, _ = z.shape
    zq, zkv, zpe = jnp.split(z, [Q_LORA, Q_LORA + KV_LORA], axis=-1)
    q = (rmsnorm(zq, g_q_a) @ w_uq).reshape(bsz, s, MLA_HEADS, QK_HEAD_DIM)
    kv = (rmsnorm(zkv, g_kv_a) @ w_ukv).reshape(bsz, s, MLA_HEADS, QK_NOPE_DIM + V_HEAD_DIM)
    k_nope, v = jnp.split(kv, [QK_NOPE_DIM], axis=-1)
    k_pe = jnp.broadcast_to(zpe[:, :, None, :], (bsz, s, MLA_HEADS, QK_ROPE_DIM))
    k = jnp.concatenate([k_nope, k_pe], axis=-1)
    q = rmsnorm(q, q_norm)
    k = rmsnorm(k, k_norm)
    q = jnp.concatenate([q[..., :QK_NOPE_DIM], rope(q[..., QK_NOPE_DIM:], cos, sin)], axis=-1)
    k = jnp.concatenate([k[..., :QK_NOPE_DIM], rope(k[..., QK_NOPE_DIM:], cos, sin)], axis=-1)
    o = causal_attention(q, k, v)
    return o.reshape(bsz, s, D_MLA)

def hier_moe(h, w_rg, b_rg, w_re, b_re, w_e_gate, w_e_up, w_e_down):
    bsz, s, d = h.shape
    t = h.reshape(-1, d)
    g_logits = (t @ w_rg).astype(jnp.float32) + b_rg.astype(jnp.float32)
    p_group = jax.nn.softmax(g_logits, axis=-1)
    g_idx = jnp.argmax(g_logits, axis=-1)
    p_g = jnp.take_along_axis(p_group, g_idx[:, None], axis=-1)
    e_logits = ((t @ w_re).astype(jnp.float32) + b_re.astype(jnp.float32)).reshape(
        -1, N_GROUPS, EXPERTS_PER_GROUP)
    e_in_group = jnp.take_along_axis(e_logits, g_idx[:, None, None], axis=1)[:, 0]
    p_e = jax.nn.softmax(e_in_group, axis=-1)
    top_w, top_i = lax.top_k(p_e, TOP_K)
    top_w = top_w / jnp.sum(top_w, axis=-1, keepdims=True) * p_g
    expert_id = g_idx[:, None] * EXPERTS_PER_GROUP + top_i
    combine = jnp.sum(jax.nn.one_hot(expert_id, N_EXPERTS, dtype=jnp.float32)
                      * top_w[..., None], axis=1).astype(t.dtype)
    out = jnp.zeros_like(t)
    for e in range(N_EXPERTS):
        hid = jax.nn.silu(t @ w_e_gate[e]) * (t @ w_e_up[e])
        out = out + combine[:, e:e + 1] * (hid @ w_e_down[e])
    return out.reshape(bsz, s, d)

def setup_inputs(seed: int = 0) -> dict:
    key = jax.random.key(seed)
    ks = iter(jax.random.split(key, 40))
    L = DEPTH
    nrm = lambda shape, scale: jax.random.normal(next(ks), shape, jnp.float32) * scale
    gain = lambda shape: 1.0 + nrm(shape, 0.02)
    x = nrm((BATCH, SEQ, D_MODEL), 1.0)
    c = nrm((BATCH, D_MODEL), 1.0)
    offset = jax.random.randint(next(ks), (BATCH, 1), 0, 4096, dtype=jnp.int32)
    positions = (offset + jnp.arange(SEQ, dtype=jnp.int32)[None, :]).astype(jnp.int32)
    return {
        'x': x,
        'c': c,
        'positions': positions,
        'w_ada': nrm((L, D_MODEL, 6 * D_MODEL), D_MODEL ** -0.5),
        'b_ada': nrm((L, 6 * D_MODEL), 0.01),
        'g_norm_mix': gain((L, D_MODEL)),
        'w_in': nrm((L, D_MODEL, D_IN), D_MODEL ** -0.5),
        'mu_shift': jax.random.uniform(next(ks), (L, RWKV_COLS), jnp.float32),
        'w0': -2.0 + nrm((L, D_RWKV), 0.5),
        'w_decay_up': nrm((L, DECAY_LORA, D_RWKV), 0.5 * DECAY_LORA ** -0.5),
        'a0': nrm((L, D_RWKV), 0.1),
        'w_a_up': nrm((L, AAA_LORA, D_RWKV), AAA_LORA ** -0.5),
        'w_g_up': nrm((L, GATE_LORA, D_RWKV), GATE_LORA ** -0.5),
        'k_k': 0.85 + nrm((L, D_RWKV), 0.05),
        'k_a': 1.0 + nrm((L, D_RWKV), 0.05),
        'r_k': nrm((L, RWKV_HEADS, RWKV_HEAD_DIM), 0.1),
        'ln_x_w': gain((L, D_RWKV)),
        'ln_x_b': nrm((L, D_RWKV), 0.01),
        'g_q_a': gain((L, Q_LORA)),
        'w_uq': nrm((L, Q_LORA, MLA_HEADS * QK_HEAD_DIM), Q_LORA ** -0.5),
        'g_kv_a': gain((L, KV_LORA)),
        'w_ukv': nrm((L, KV_LORA, MLA_HEADS * (QK_NOPE_DIM + V_HEAD_DIM)), KV_LORA ** -0.5),
        'q_norm': gain((L, QK_HEAD_DIM)),
        'k_norm': gain((L, QK_HEAD_DIM)),
        'w_branch': nrm((L, N_BRANCHES, D_BRANCH, D_MODEL), D_BRANCH ** -0.5),
        'w_out': nrm((L, D_MODEL, D_MODEL), D_MODEL ** -0.5),
        'g_norm_ffn': gain((L, D_MODEL)),
        'w_router_group': nrm((L, D_MODEL, N_GROUPS), D_MODEL ** -0.5),
        'b_router_group': nrm((L, N_GROUPS), 0.01),
        'w_router_expert': nrm((L, D_MODEL, N_EXPERTS), D_MODEL ** -0.5),
        'b_router_expert': nrm((L, N_EXPERTS), 0.01),
        'w_e_gate': nrm((L, N_EXPERTS, D_MODEL, D_EXPERT), D_MODEL ** -0.5),
        'w_e_up': nrm((L, N_EXPERTS, D_MODEL, D_EXPERT), D_MODEL ** -0.5),
        'w_e_down': nrm((L, N_EXPERTS, D_EXPERT, D_MODEL), D_EXPERT ** -0.5),
    }

def reference(x, c, positions, w_ada, b_ada, g_norm_mix, w_in, mu_shift, w0, w_decay_up,
              a0, w_a_up, w_g_up, k_k, k_a, r_k, ln_x_w, ln_x_b, g_q_a, w_uq, g_kv_a,
              w_ukv, q_norm, k_norm, w_branch, w_out, g_norm_ffn, w_router_group,
              b_router_group, w_router_expert, b_router_expert, w_e_gate, w_e_up, w_e_down):
    freqs = ROPE_THETA ** (-(jnp.arange(0, QK_ROPE_DIM, 2, dtype=jnp.float32) / QK_ROPE_DIM))
    ang = positions.astype(jnp.float32)[..., None] * freqs
    cos = jnp.cos(ang)[:, :, None, :].astype(x.dtype)
    sin = jnp.sin(ang)[:, :, None, :].astype(x.dtype)
    for l in range(DEPTH):
        mod = jax.nn.silu(c) @ w_ada[l] + b_ada[l]
        sh_m, sc_m, gt_m, sh_f, sc_f, gt_f = jnp.split(mod, 6, axis=-1)

        h = modulate(rmsnorm(x, g_norm_mix[l]), sh_m, sc_m)
        z = h @ w_in[l]
        z_rwkv, z_mla, z_gates = jnp.split(z, [RWKV_COLS, RWKV_COLS + MLA_COLS], axis=-1)
        y_rwkv = rwkv7_branch(z_rwkv, mu_shift[l], w0[l], w_decay_up[l], a0[l], w_a_up[l],
                              w_g_up[l], k_k[l], k_a[l], r_k[l], ln_x_w[l], ln_x_b[l])
        y_mla = mla_branch(z_mla, cos, sin, g_q_a[l], w_uq[l], g_kv_a[l], w_ukv[l],
                           q_norm[l], k_norm[l])
        gate_rwkv, gate_mla = jnp.split(jax.nn.sigmoid(z_gates), N_BRANCHES, axis=-1)
        merged = gate_rwkv * (y_rwkv @ w_branch[l, 0]) + gate_mla * (y_mla @ w_branch[l, 1])
        x = x + gt_m[:, None, :] * (merged @ w_out[l])

        h2 = modulate(rmsnorm(x, g_norm_ffn[l]), sh_f, sc_f)
        x = x + gt_f[:, None, :] * hier_moe(h2, w_router_group[l], b_router_group[l],
                                            w_router_expert[l], b_router_expert[l],
                                            w_e_gate[l], w_e_up[l], w_e_down[l])
    return x


_drawn_inputs = setup_inputs


def setup_inputs(seed=0):
    import zlib

    import numpy as np

    out = dict(_drawn_inputs(seed))
    spreads = {}
    factors = {'g_norm_mix': 2.694,
     'ln_x_w': 26.588,
     'ln_x_b': 53.543,
     'g_q_a': 8.0,
     'g_kv_a': 4.365,
     'q_norm': 7.934,
     'k_norm': 8.0,
     'b_router_group': 64.0,
     'b_router_expert': 25.446,
     'k_k': 6.107,
     'g_norm_ffn': 3.892}
    for name, (base, spread) in spreads.items():
        noise = np.random.default_rng([zlib.crc32(name.encode()), seed]).standard_normal(out[name].shape)
        drawn = base * np.exp(spread * noise) if base else spread * noise
        out[name] = __import__('jax').numpy.asarray(drawn.astype(out[name].dtype))
    for name, factor in factors.items():
        out[name] = (out[name] * factor).astype(out[name].dtype)
    return out
```

```python
import math
from contextlib import ExitStack, contextmanager

import numpy as np

import concourse.bass as bass
from concourse import mybir

P = 128
D = 1024
SEQ = 1024
KD = D // P
NT = SEQ // P
EPS = 1e-6
HEADS = 8
N = 64
D_RWKV = HEADS * N
CT = D_RWKV // P
RWKV_COLS = 3 * D_RWKV + 64 + 64 + 128
RT = RWKV_COLS // P
LN_EPS = 64e-5
Q_LORA, KV_LORA, ROPE = 256, 128, 32
MLA_COLS = Q_LORA + KV_LORA + ROPE
QKD = 96
GATE0 = RWKV_COLS + MLA_COLS
NE, NG, EPG, FE = 32, 4, 8, 256
NBLK = 48
SURE = 2 * SEQ // P
CHUNK = 64
LEVELS = [2, 4, 8, 16, 32]
DECAY = -math.exp(-0.5)
HALF = SEQ // 2

f32 = mybir.dt.float32
i32 = mybir.dt.int32
u32 = mybir.dt.uint32
ALU = mybir.AluOpType
ACT = mybir.ActivationFunctionType
AX = mybir.AxisListType

CONST = {}
_at = 0
for _name, _w in (("ident", P), ("mask4", 4 * P), ("up1", P), ("offt", len(LEVELS) * P), ("causal", P),
                  ("heads", P), ("before", P), ("ones", P), ("keep", P), ("freq", 16), ("iota", NBLK),
                  ("thr", 8), ("id64", N)):
    CONST[_name] = (_at, _at + _w)
    _at += _w
NCONST = _at


def const_table():
    c = np.zeros((P, NCONST), np.float32)
    s, t = np.arange(P)[:, None], np.arange(P)[None, :]
    same = s // CHUNK == t // CHUNK

    def put(name, v):
        a, b = CONST[name]
        c[:, a:b] = v
    put("ident", s == t)
    before, upto = (s < t) & same, (s <= t) & same
    put("mask4", np.concatenate([before, upto, before, upto], 1))
    put("up1", (s // 2 == t // 2) & (s < t))
    put("offt", np.concatenate([(s // (2 * b) == t // (2 * b)) & (s // b < t // b) for b in LEVELS], 1))
    put("causal", np.where(t <= s, 0.0, -1e30))
    put("heads", s // N == t // N)
    put("before", s < t)
    put("ones", 1.0)
    put("keep", np.broadcast_to(t % CHUNK != 0, (P, P)))
    put("freq", (10000.0 ** (-(np.arange(0, ROPE, 2) / ROPE)))[None, :])
    put("iota", np.arange(NBLK)[None, :])
    put("id64", s % N == t[:, :N])
    put("thr", (np.arange(8) * P)[None, :])
    return c


PCOL = {}
_at = 0
for _name, _w in (("mu", RT), ("w0", CT), ("a0", CT), ("k_k", CT), ("k_a", CT), ("r_k", CT), ("ln_w", CT), ("ln_b", CT)):
    PCOL[_name] = (_at, _at + _w)
    _at += _w
NPCOL = _at


def lay_out(inputs):
    a = {n: np.asarray(v) for n, v in inputs.items()}
    o = dict(a)
    cols = [a[n].reshape(-1, P).T for n in
            ("mu_shift", "w0", "a0", "k_k", "k_a", "r_k", "ln_x_w", "ln_x_b")]
    o["pcol"] = np.concatenate(cols, 1)
    w = a["w_in"][0].reshape(KD, P, -1)
    tiles = lambda v: v.reshape(KD, P, -1, P).transpose(2, 1, 0, 3)
    o["w_rwkv"] = tiles(w[:, :, :RWKV_COLS])
    o["w_mla"] = w[:, :, RWKV_COLS:GATE0].transpose(1, 0, 2)
    o["w_gates"] = tiles(w[:, :, GATE0:])
    o["w_br"] = a["w_branch"][0].reshape(2, CT, P, KD, P).transpose(3, 2, 0, 1, 4)
    o["pos"] = a["positions"].reshape(NT, P).T
    o["w_router"] = np.concatenate([a["w_router_group"][0], a["w_router_expert"][0]], 1)\
        .reshape(KD, P, NG + NE).transpose(1, 0, 2)
    o["b_router"] = np.concatenate([a["b_router_group"], a["b_router_expert"]], 1)
    o["qk_gain"] = np.concatenate([a["q_norm"], a["k_norm"]], 1)
    o["consts"], o["tokens"] = const_table(), token_table()
    for n in ("w_in", "mu_shift", "w0", "a0", "k_k", "k_a", "r_k", "ln_x_w", "ln_x_b", "w_branch", "positions",
              "w_router_group", "w_router_expert", "b_router_group", "b_router_expert", "q_norm", "k_norm"):
        del o[n]
    return {n: np.ascontiguousarray(v) for n, v in o.items()}


def token_table():
    return (np.arange(NT)[None, :] * P + np.arange(P)[:, None]).astype(np.int32)


def two_pi_parts():
    rest, parts = 2 * math.pi, []
    for _ in range(3):
        e = math.floor(math.log2(rest)) - 5
        p = math.floor(rest / 2.0 ** e) * 2.0 ** e
        parts.append(p)
        rest -= p
    return parts + [rest]


class Chain:

    def __init__(self, eng, sem, base=0, credit=0):
        self.eng, self.sem, self.base, self.n = eng, sem, base, credit

    def __call__(self, ins):
        self.n += 1
        ins.then_inc(self.sem, 1)
        self.eng.wait_ge(self.sem, self.base + self.n)


def build(nc, x, c, w_ada, b_ada, g_norm_mix, g_norm_ffn, w_decay_up, w_a_up, w_g_up, g_q_a, w_uq, g_kv_a,
          w_ukv, w_out, w_e_gate, w_e_up, w_e_down, pcol, w_rwkv, w_mla, w_gates, w_br, pos, w_router, b_router,
          qk_gain, consts, tokens, out, last_phase=99, debug=None):
    h_dram = nc.dram_tensor("h_spill", (P, KD * SEQ), f32, kind="Internal").ap()
    mod_dram = nc.dram_tensor("mod_rows", (1, 6 * D), f32, kind="Internal").ap()
    zm_dram = nc.dram_tensor("mla_rows", (P, NT * MLA_COLS), f32, kind="Internal").ap()
    yr_dram = nc.dram_tensor("rwkv_rows", (P, CT * SEQ), f32, kind="Internal").ap()
    h2_dram = nc.dram_tensor("h2_rows", (SEQ, D), f32, kind="Internal").ap()
    slot_dram = nc.dram_tensor("slot_token", (NBLK * P, 1), i32, kind="Internal").ap()
    y_dram = nc.dram_tensor("expert_rows", (NBLK * P, D), f32, kind="Internal").ap()
    ctx = ExitStack()
    with ctx:
        def sb(st, name, shape, dt=f32):
            return st.enter_context(nc.sbuf_tensor(name, shape, dt))

        taken = []
        scattered = ctx.enter_context(nc.semaphore("scattered"))
        idx_in = [ctx.enter_context(nc.semaphore(f"idx_in{i}")) for i in range(2)]
        xg_in = [ctx.enter_context(nc.semaphore(f"xg_in{i}")) for i in range(2)]
        r_in = [ctx.enter_context(nc.semaphore(f"r_in{i}")) for i in range(2 * NT)]

        def sem(st, name):
            taken.append(st.enter_context(nc.semaphore(name)))
            return taken[-1]

        def sems(st, *names):
            return [sem(st, n) for n in names]

        def slots(st, name, n):
            return [sem(st, f"{name}{i}") for i in range(n)]

        @contextmanager
        def phase():
            with ExitStack() as st:
                yield st
                with nc.Block() as block:
                    @block.gpsimd
                    def _(pool):
                        for s_ in taken:
                            pool.sem_clear(s_)
                taken.clear()

        ps = ctx.enter_context(nc.psum_tensor("ps", [P, 8, 512], f32))
        cst = sb(ctx, "cst", [P, NCONST])
        pc = sb(ctx, "pc", [P, NPCOL])
        YTM = sb(ctx, "YTM", [P, CT, SEQ])
        zst = ctx.enter_context(ExitStack())
        zT = sb(zst, "zT", [P, RT, SEQ + 1])
        mst = ctx.enter_context(ExitStack())
        mod = sb(mst, "mod", [P, 6 * D])

        def C(name):
            a, b = CONST[name]
            return cst[:, a:b]

        def PC(name, i=None):
            a, b = PCOL[name]
            return pc[:, a:b] if i is None else pc[:, a + i:a + i + 1]

        SH_M, SC_M, GT_M, SH_F, SC_F, GT_F = (mod[:, i * D:(i + 1) * D] for i in range(6))

        with phase() as st:
            NW = 3
            ccol = sb(st, "ccol", [P, KD])
            csig = sb(st, "csig", [P, KD])
            crep = sb(st, "crep", [P, KD, P])
            brow = sb(st, "brow", [P, 6 * D])
            gmix = sb(st, "gmix", [P, D])
            gffn = sb(st, "gffn", [P, D])
            wbuf = sb(st, "wbuf", [P, NW, KD, 512])
            const_in, c_in, b_in, c_sig, c_rep, mod_mm, mod_ev, dch, mod_out = sems(
                st, "const_in", "c_in", "b_in", "c_sig", "c_rep", "mod_mm", "mod_ev", "dch0", "mod_out")
            w_in_s = slots(st, "wada", NW)
            CH = 6 * D // 512
            w_v = w_ada[0].rearrange("(p k) n -> p k n", k=KD)
            with nc.Block() as block:
                @block.sync
                def _(sp):
                    sp.dma_start(ccol[:], c[0].rearrange("(p k) -> p k", k=KD)).then_inc(c_in, 16)
                    sp.dma_start(cst[:], consts).then_inc(const_in, 16)
                    sp.dma_start(pc[:], pcol).then_inc(const_in, 16)
                    for b in range(NW):
                        sp.dma_start(wbuf[:, b], w_v[:, :, b * 512:(b + 1) * 512]).then_inc(w_in_s[b], 16)
                    for dst, src in ((brow, b_ada), (gmix, g_norm_mix), (gffn, g_norm_ffn)):
                        sp.dma_start(dst[:], src.broadcast_to(list(dst.shape))).then_inc(b_in, 16)
                    with sp.Fori(0, CH // NW - 1) as i:
                        for b in range(NW):
                            sp.wait_ge(mod_mm, i * NW + b + 1)
                            sp.dma_start(wbuf[:, b], w_v[:, :, bass.ds(i * NW * 512 + (NW + b) * 512, 512)])\
                              .then_inc(w_in_s[b], 16)
                    sp.wait_ge(dch, 2)
                    sp.dma_start(mod_dram, mod[0:1, :]).then_inc(mod_out, 16)
                    sp.wait_ge(mod_out, 16)
                    sp.wait_ge(const_in, 32)

                @block.scalar
                def _(act):
                    act.wait_ge(c_in, 16)
                    nc.scalar.activation(csig[:], ccol[:], ACT.Sigmoid).then_inc(c_sig, 1)

                @block.vector
                def _(dve):
                    link = Chain(dve, dch)
                    dve.sem_inc(mod_ev, 1)
                    dve.wait_ge(c_sig, 1)
                    link(nc.vector.tensor_tensor(csig[:], csig[:], ccol[:], ALU.mult))
                    nc.vector.tensor_copy(crep[:], csig[:].unsqueeze(2).broadcast_to([P, KD, P])).then_inc(c_rep, 1)
                    dve.wait_ge(b_in, 48)
                    with dve.Fori(0, CH // NW) as i:
                        for b in range(NW):
                            dve.wait_ge(mod_mm, i * NW + b + 1)
                            cols = bass.ds(i * NW * 512 + b * 512, 512)
                            nc.vector.tensor_tensor(mod[:, cols], ps[:, b], brow[:, cols], ALU.add)\
                              .then_inc(mod_ev, 1)
                    dve.wait_ge(mod_ev, CH + 1)
                    nc.vector.scalar_tensor_tensor(SC_M, SC_M, 1.0, gmix[:], ALU.add, ALU.mult)
                    nc.vector.scalar_tensor_tensor(SC_F, SC_F, 1.0, gffn[:], ALU.add, ALU.mult).then_inc(dch, 1)

                @block.tensor
                def _(pe):
                    pe.wait_ge(c_rep, 1)
                    with pe.Fori(0, CH // NW) as i:
                        for b in range(NW):
                            pe.wait_ge(w_in_s[b], i * 16 + 16)
                            if b == 0:
                                pe.wait_ge(mod_ev, i * NW + 1)
                            for k in range(KD):
                                m = nc.tensor.matmul(ps[:, b], crep[:, k], wbuf[:, b, k],
                                                     start=(k == 0), stop=(k == KD - 1))
                            m.then_inc(mod_mm, 1)
        if debug is not None and last_phase == 0:
            return dump(nc, ctx, debug, mod[:])

        with phase() as st:
            hT = sb(st, "hT", [P, KD, SEQ])
            zm = sb(st, "zm", [P, NT, MLA_COLS])
            xt = sb(st, "xt", [P, 4, D])
            hb, junk = YTM[:, 0:2], YTM[:, 2]
            ss = sb(st, "ss", [P, NT])
            rs = sb(st, "rs", [P, NT])
            wr = sb(st, "wr", [P, 2, KD, P])
            wm = sb(st, "wm", [P, KD, MLA_COLS])
            tmp = sb(st, "tmp", [P, 2, SEQ])
            x_in = slots(st, "x_in", 4)
            wr_in = slots(st, "wr_in", 2)
            wm_in, ssq, root, rstd, h_ready, tr, tr_ev, z_mm, z_ev, z_done, dif, mla_mm, mla_ev, dch, \
                h_out, zero = sems(
                    st, "wm_in", "ssq", "root", "rstd", "h_ready", "tr", "tr_ev", "z_mm", "z_ev", "z_done",
                    "dif", "mla_mm", "mla_ev", "dch1", "h_out", "zero")
            x_v = x[0].rearrange("(t p) d -> t p d", p=P)
            with nc.Block() as block:
                @block.sync
                def _(sp):
                    for t in range(NT):
                        if t >= 4:
                            sp.wait_ge(h_ready, t - 3)
                        sp.dma_start(xt[:, t % 4], x_v[t]).then_inc(x_in[t % 4], 16)
                        if t == 3:
                            sp.dma_start(wm[:], w_mla).then_inc(wm_in, 16)
                            for b in range(2):
                                sp.dma_start(wr[:, b], w_rwkv[b]).then_inc(wr_in[b], 16)
                    sp.wait_ge(tr_ev, 2 * NT)
                    sp.dma_start(h_dram, hT[:].rearrange("p k s -> p (k s)")).then_inc(h_out, 16)
                    with sp.Fori(0, RT // 2 - 1) as i:
                        for b in range(2):
                            sp.wait_ge(z_mm, 2 * i + b + 1)
                            sp.dma_start(wr[:, b], w_rwkv[bass.ds(2 * i + 2 + b, 1)].rearrange("a p k n -> (a p) k n"))\
                              .then_inc(wr_in[b], 16)
                    sp.wait_ge(mla_ev, NT)
                    sp.dma_start(zm_dram, zm[:].rearrange("p t n -> p (t n)")).then_inc(h_out, 16)
                    sp.wait_ge(h_out, 32)

                @block.scalar
                def _(act):
                    for t in range(4):
                        act.wait_ge(x_in[t], 16)
                        if t:
                            act.wait_ge(ssq, t)
                        nc.scalar.activation(junk, xt[:, t], ACT.Square, accum_out=ss[:, t:t + 1]).then_inc(ssq, 1)
                    act.wait_ge(rstd, 1)
                    nc.scalar.activation(rs[:, 0:4], rs[:, 0:4], ACT.Sqrt).then_inc(root, 1)
                    for t in range(NT):
                        for g in range(2):
                            act.wait_ge(tr, 2 * t + g + 1)
                            nc.scalar.activation(hT[:, 4 * g:4 * g + 4, t * P:(t + 1) * P],
                                                 ps[:, 2 * (t % 2) + g].rearrange("p (a b) -> p a b", a=4),
                                                 ACT.Copy).then_inc(tr_ev, 1)
                        if t < 4:
                            act.wait_ge(x_in[t], 32)
                            act.wait_ge(ssq, t + 4)
                            nc.scalar.activation(junk, xt[:, t], ACT.Square, accum_out=ss[:, t + 4:t + 5])\
                               .then_inc(ssq, 1)
                        if t == 3:
                            act.wait_ge(rstd, 3)
                            nc.scalar.activation(rs[:, 4:8], rs[:, 4:8], ACT.Sqrt).then_inc(root, 1)
                    for t in range(NT):
                        act.wait_ge(mla_mm, t + 1)
                        nc.scalar.activation(zm[:, t], ps[:, t % 2, 0:MLA_COLS], ACT.Copy).then_inc(mla_ev, 1)
                    with act.Fori(0, RT // 2) as i:
                        for b in range(2):
                            act.wait_ge(z_mm, 2 * i + b + 1)
                            nc.scalar.activation(zT[:, bass.ds(2 * i + b, 1), 1:SEQ + 1],
                                                 ps[:, 4 + 2 * b:6 + 2 * b].rearrange("p a n -> p (a n)").unsqueeze(1),
                                                 ACT.Copy).then_inc(z_ev, 1)

                @block.vector
                def _(dve):
                    link = Chain(dve, dch)
                    nc.vector.memset(zT[:, :, 0:1], 0.0).then_inc(zero, 1)
                    for half in range(2):
                        cols = slice(4 * half, 4 * half + 4)
                        dve.wait_ge(ssq, 4 * half + 4)
                        nc.vector.tensor_scalar(rs[:, cols], ss[:, cols], 1.0 / D, EPS, ALU.mult, ALU.add)\
                          .then_inc(rstd, 1)
                        dve.wait_ge(root, half + 1)
                        nc.vector.reciprocal(rs[:, cols], rs[:, cols]).then_inc(rstd, 1)
                        dve.wait_ge(rstd, 2 * half + 2)
                        for t in range(4 * half, 4 * half + 4):
                            if t >= 2:
                                dve.wait_ge(tr, 2 * t - 2)
                            link(nc.vector.scalar_tensor_tensor(hb[:, t % 2], xt[:, t % 4], rs[:, t:t + 1], SC_M,
                                                                ALU.mult, ALU.mult))
                            nc.vector.tensor_tensor(hb[:, t % 2], hb[:, t % 2], SH_M, ALU.add).then_inc(h_ready, 1)
                    dve.wait_ge(zero, 1)
                    with dve.Fori(0, RT // 2) as i:
                        for b in range(2):
                            dve.wait_ge(z_ev, 2 * i + b + 1)
                            zt = zT[:, bass.ds(2 * i + b, 1), :].rearrange("p a n -> p (a n)")
                            nc.vector.tensor_tensor(tmp[:, b], zt[:, 0:SEQ], zt[:, 1:SEQ + 1], ALU.subtract)\
                              .then_inc(dif, 1)
                            dve.wait_ge(dif, 2 * i + b + 1)
                            nc.vector.scalar_tensor_tensor(zt[:, 1:SEQ + 1], tmp[:, b], pc[:, bass.ds(2 * i + (b + PCOL["mu"][0]), 1)],
                                                           zt[:, 1:SEQ + 1], ALU.mult, ALU.add).then_inc(z_done, 1)

                @block.tensor
                def _(pe):
                    for t in range(NT):
                        pe.wait_ge(h_ready, t + 1)
                        if t >= 2:
                            pe.wait_ge(tr_ev, 2 * t - 2)
                        for g in range(2):
                            for j in range(4):
                                k = 4 * g + j
                                m = nc.tensor.transpose(ps[:, 2 * (t % 2) + g, j * P:(j + 1) * P],
                                                        hb[:, t % 2, k * P:(k + 1) * P], C("ident"))
                            m.then_inc(tr, 1)
                    pe.wait_ge(tr_ev, 2 * NT)
                    pe.wait_ge(wm_in, 16)
                    for t in range(NT):
                        if t >= 2:
                            pe.wait_ge(mla_ev, t - 1)
                        for k in range(KD):
                            m = nc.tensor.matmul(ps[:, t % 2, 0:MLA_COLS], hT[:, k, t * P:(t + 1) * P], wm[:, k],
                                                 start=(k == 0), stop=(k == KD - 1))
                        m.then_inc(mla_mm, 1)

                    def column_tile(b):
                        for n in range(2):
                            for k in range(KD):
                                m = nc.tensor.matmul(ps[:, 4 + 2 * b + n], wr[:, b, k], hT[:, k, n * 512:(n + 1) * 512],
                                                     start=(k == 0), stop=(k == KD - 1))
                        m.then_inc(z_mm, 1)
                    for b in range(2):
                        pe.wait_ge(wr_in[b], 16)
                        column_tile(b)
                    with pe.Fori(1, RT // 2) as i:
                        for b in range(2):
                            pe.wait_ge(wr_in[b], i * 16 + 16)
                            pe.wait_ge(z_ev, 2 * i + b - 1)
                            column_tile(b)
        if debug is not None and last_phase == 1:
            return dump(nc, ctx, debug, zT[:].rearrange("p a b -> p (a b)"))

        mst.close()

        R0, K0, V0, WA, GL = 0, CT, 2 * CT, 3 * CT, 3 * CT + 1
        kst = ctx.enter_context(ExitStack())
        kk = sb(kst, "kk", [P, CT, SEQ])
        aa = sb(kst, "aa", [P, CT, SEQ])
        lw = sb(kst, "lw", [P, CT, SEQ])

        def Z(i):
            return zT[:, i, 1:SEQ + 1]

        with phase() as st:
            wup = sb(st, "wup", [P, D_RWKV])
            sq = sb(st, "sq", [P, 2, SEQ])
            norm = YTM
            one_ka = sb(st, "one_ka", [P, CT])
            up_in, low, up_mm, dec, a_done, kraw, sq_done, ss_mm, nr_ev, dch, kdone, pch = sems(
                st, "up_in", "low", "up_mm", "dec", "a_done", "kraw", "sq_done", "ss_mm", "nr_ev", "dch2",
                "kdone", "pch2")
            with nc.Block() as block:
                @block.sync
                def _(sp):
                    sp.dma_start(wup[0:64], w_decay_up[0]).then_inc(up_in, 16)
                    sp.dma_start(wup[64:128], w_a_up[0]).then_inc(up_in, 16)
                    sp.wait_ge(up_in, 32)

                @block.gpsimd
                def _(pool):
                    for c_ in range(CT):
                        pool.wait_ge(kraw, c_ + 1)
                        if c_ >= 2:
                            pool.wait_ge(ss_mm, c_ - 1)
                        nc.gpsimd.tensor_tensor(sq[:, c_ % 2], kk[:, c_], kk[:, c_], ALU.mult).then_inc(sq_done, 1)

                @block.scalar
                def _(act):
                    nc.scalar.activation(Z(WA)[0:64], Z(WA)[0:64], ACT.Tanh).then_inc(low, 1)
                    nc.scalar.activation(Z(GL), Z(GL), ACT.Sigmoid).then_inc(low, 1)
                    for c_ in range(CT):
                        act.wait_ge(up_mm, 2 * c_ + 1)
                        nc.scalar.activation(lw[:, c_], ps[:, 0:2].rearrange("p a n -> p (a n)"), ACT.Sigmoid,
                                             bias=PC("w0", c_)).then_inc(dec, 1)
                        act.wait_ge(up_mm, 2 * c_ + 2)
                        nc.scalar.activation(aa[:, c_], ps[:, 2:4].rearrange("p a n -> p (a n)"), ACT.Sigmoid,
                                             bias=PC("a0", c_)).then_inc(a_done, 1)
                    for c_ in range(CT):
                        act.wait_ge(ss_mm, c_ + 1)
                        nc.scalar.activation(norm[:, c_], ps[:, 6:8].rearrange("p a n -> p (a n)"), ACT.Sqrt)\
                           .then_inc(nr_ev, 1)

                @block.vector
                def _(dve):
                    link = Chain(dve, dch)
                    for c_ in range(CT):
                        nc.vector.tensor_scalar(kk[:, c_], Z(K0 + c_), PC("k_k", c_), None, ALU.mult).then_inc(kraw, 1)
                    link(nc.vector.tensor_scalar(one_ka[:], PC("k_a"), -1.0, 1.0, ALU.mult, ALU.add))
                    for c_ in range(CT):
                        dve.wait_ge(dec, c_ + 1)
                        nc.vector.tensor_scalar(lw[:, c_], lw[:, c_], DECAY, None, ALU.mult)
                        dve.wait_ge(a_done, c_ + 1)
                        buf = norm[:, c_]
                        link(nc.vector.tensor_scalar(buf, aa[:, c_], PC("k_a", c_), one_ka[:, c_:c_ + 1],
                                                     ALU.mult, ALU.add))
                        nc.vector.tensor_tensor(Z(K0 + c_), Z(K0 + c_), buf, ALU.mult).then_inc(kdone, 1)
                    for c_ in range(CT):
                        dve.wait_ge(nr_ev, c_ + 1)
                        link(nc.vector.tensor_scalar(norm[:, c_], norm[:, c_], 1e-12, None, ALU.max))
                        link(nc.vector.reciprocal(norm[:, c_], norm[:, c_]))
                        link(nc.vector.tensor_tensor(kk[:, c_], kk[:, c_], norm[:, c_], ALU.mult))
                        nc.vector.tensor_tensor(aa[:, c_], aa[:, c_], kk[:, c_], ALU.mult)

                @block.tensor
                def _(pe):
                    pe.wait_ge(up_in, 32)
                    pe.wait_ge(low, 2)
                    for c_ in range(CT):
                        for j, (w, src, done) in enumerate(((wup[0:64], Z(WA)[0:64], dec),
                                                            (wup[64:128], Z(WA)[64:128], a_done))):
                            if c_:
                                pe.wait_ge(done, c_)
                            for n in range(2):
                                m = nc.tensor.matmul(ps[:, 2 * j + n], w[:, c_ * P:(c_ + 1) * P],
                                                     src[:, n * 512:(n + 1) * 512], start=True, stop=True)
                            m.then_inc(up_mm, 1)
                    for c_ in range(CT):
                        pe.wait_ge(sq_done, c_ + 1)
                        if c_:
                            pe.wait_ge(nr_ev, c_)
                        elif CT:
                            pe.wait_ge(kdone, CT)
                        for n in range(2):
                            m = nc.tensor.matmul(ps[:, 6 + n], C("heads"), sq[:, c_ % 2, n * 512:(n + 1) * 512],
                                                 start=True, stop=True)
                        m.then_inc(ss_mm, 1)
        if debug is not None and last_phase == 2:
            return dump(nc, ctx, debug, kk[:].rearrange("p a b -> p (a b)"))

        yrow = YTM[:].rearrange("p c (t n) -> p (c t) n", n=D_RWKV)
        with phase() as st:
            cum = sb(st, "cum", [P, CT, P])
            ex = sb(st, "ex", [P, 4, CT, P])
            nr = sb(st, "nr", [P, CT, 2, P])
            bd = sb(st, "bd", [P, CT, P])
            kd = sb(st, "kd", [P, CT, P])
            ce = sb(st, "ce", [P, 2, CT, P])
            tok = sb(st, "tok", [P, 3, CT, P])
            nb = sb(st, "nb", [P, HEADS, 2, N])
            mats = sb(st, "mats", [P, HEADS, 4, P])
            off = sb(st, "off", [P, 2, 4, P])
            xx = ce[:].rearrange("p a c n -> p (a c) n")
            tt = sb(st, "tt", [P, HEADS, 2, P])
            wu = sb(st, "wu", [P, HEADS, 2, N])
            pt = sb(st, "pt", [P, CT, P])
            mt = sb(st, "mt", [P, 2, CT, P])
            rk = pt
            S = sb(st, "S", [P, 2, CT, P])
            headrk = zT[:, WA, 0:CT * P].rearrange("p (c n) -> p c n", c=CT)
            dg = zT[:, WA, 512:1024].rearrange("p (h c n) -> p h c n", c=CT, h=2)
            vst = sb(st, "vst", [P, CT, P])

            def tok_rows(i, h):
                return tok[:, i, h // 2, 64 * (h % 2):64 * (h % 2) + 64]

            def v_rows(h):
                return tok_rows(2, h)
            PER = dict(cum=4, pre=2, ex=3, vst=1, mul=4, pmul=3, tr=4, tok=1, nb=1, pair=8, pair_ev=8, t0=4, t0_mm=2,
                       t0_ev=2, off=10, x=10, x_ev=10, t=10, t_ev=10, bv=1, bv_ev=1, wu=2, wu_ev=2, pt=1, pt_ev=1,
                       mr=1, mt_ev=2, dg=2, st=2, st_ev=2, y=1, y_ev=1, bon=1, bon_ev=1)
            sm = {n: sem(st, "r_" + n) for n in PER}
            init = sem(st, "r_init")
            over = sem(st, "r_over")
            NL = len(LEVELS)
            assert PER["off"] == 2 * NL

            def head(h):
                return h // 2, slice(64 * (h % 2), 64 * (h % 2) + 64)

            def chunks(ap):
                return ap.rearrange("p c (h n) -> p (c h) n", n=CHUNK)

            XB, DB = (0, 3), (1, 4)
            with nc.Block() as block:
                @block.gpsimd
                def _(pool):
                    with pool.Fori(0, NT) as j:
                        def wait(name, n):
                            pool.wait_ge(sm[name], j * PER[name] + n)
                        seq = bass.ds(j * P, P)
                        zseq = bass.ds(j * P + 1, P)
                        pool.wait_ge(over, j + 1)
                        nc.gpsimd.tensor_copy(vst[:], zT[:, V0:V0 + CT, zseq]).then_inc(sm["vst"], 1)
                        nc.gpsimd.tensor_tensor(rk[:], zT[:, R0:R0 + CT, zseq], zT[:, K0:K0 + CT, zseq], ALU.mult)\
                          .then_inc(sm["pmul"], 1)
                        wait("ex", 1)
                        nc.gpsimd.tensor_tensor(ce[:, 0], aa[:, :, seq], ex[:, 3], ALU.mult).then_inc(sm["pmul"], 1)
                        nc.gpsimd.tensor_tensor(ce[:, 1], zT[:, K0:K0 + CT, zseq], ex[:, 3], ALU.mult)\
                          .then_inc(sm["pmul"], 1)
                        wait("ex", 2)
                        for ch in range(2):
                            end = ex[:, 0, :, (ch + 1) * CHUNK - 1:(ch + 1) * CHUNK]
                            nc.gpsimd.tensor_tensor(dg[:, ch], C("id64").unsqueeze(1).broadcast_to([P, CT, N]),
                                                    end.broadcast_to([P, CT, N]), ALU.mult).then_inc(sm["dg"], 1)
                        for g in range(2):
                            hs = slice(4 * g, 4 * g + 4)
                            wait("pair_ev", 4 * g + 4)
                            nc.gpsimd.tensor_tensor(tt[:, hs, 1], mats[:, hs, 0],
                                                    C("up1").unsqueeze(1).broadcast_to([P, 4, P]), ALU.mult)\
                              .then_inc(sm["t0"], 1)
                            wait("t0", 2 * g + 1)
                            nc.gpsimd.tensor_tensor(tt[:, hs, 1], tt[:, hs, 1],
                                                    C("ident").unsqueeze(1).broadcast_to([P, 4, P]), ALU.add)\
                              .then_inc(sm["t0"], 1)
                        for l in range(NL):
                            a = CONST["offt"][0] + l * P
                            for g in range(2):
                                if l:
                                    wait("x", 2 * (l - 1) + g + 1)
                                nc.gpsimd.tensor_tensor(off[:, g], mats[:, 4 * g:4 * g + 4, 0],
                                                        cst[:, a:a + P].unsqueeze(1).broadcast_to([P, 4, P]), ALU.mult)\
                                  .then_inc(sm["off"], 1)

                @block.scalar
                def _(act):
                    with act.Fori(0, NT) as j:
                        def wait(name, n):
                            act.wait_ge(sm[name], j * PER[name] + n)
                        wait("pre", 2)
                        nc.scalar.activation(ex[:, 2:4], ex[:, 2:4], ACT.Exp).then_inc(sm["ex"], 1)
                        nc.scalar.activation(ex[:, 0], cum[:], ACT.Exp).then_inc(sm["ex"], 1)
                        nc.scalar.activation(ex[:, 1], cum[:], ACT.Exp, scale=-1.0).then_inc(sm["ex"], 1)
                        wait("tr", 4)
                        nc.scalar.activation(tok[:].rearrange("p a c n -> p (a c n)"),
                                             ps[:, 1:4].rearrange("p a n -> p (a n)"), ACT.Copy).then_inc(sm["tok"], 1)
                        nc.scalar.activation(nb[:, :, 0], ps[:, 0].rearrange("p (h n) -> p h n", n=N), ACT.Copy)\
                           .then_inc(sm["nb"], 1)
                        wait("bv", 1)
                        nc.scalar.activation(nb[:, :, 1], ps[:, 6].rearrange("p (h n) -> p h n", n=N), ACT.Copy)\
                           .then_inc(sm["bv_ev"], 1)
                        for g in range(2):
                            wait("t0_mm", g + 1)
                            nc.scalar.activation(tt[:, 4 * g:4 * g + 4, 0],
                                                 ps[:, XB[g]].rearrange("p (h n) -> p h n", n=P), ACT.Copy)\
                               .then_inc(sm["t0_ev"], 1)
                        for l in range(NL):
                            for g in range(2):
                                wait("x", 2 * l + g + 1)
                                nc.scalar.activation(xx[:, 4 * g:4 * g + 4],
                                                     ps[:, XB[g]].rearrange("p (h n) -> p h n", n=P), ACT.Copy)\
                                   .then_inc(sm["x_ev"], 1)
                        for c_ in range(2):
                            wait("st", c_ + 1)
                            if c_ == 1:
                                wait("y", 1)
                            nc.scalar.activation(S[:, 1 - c_].rearrange("p c n -> p (c n)"), ps[:, 4 + c_], ACT.Copy).then_inc(sm["st_ev"], 1)

                @block.vector
                def _(dve):
                    nc.vector.memset(S[:], 0.0).then_inc(init, 1)
                    nc.vector.memset(mt[:], 0.0).then_inc(init, 1)
                    for c_ in range(CT):
                        nc.vector.tensor_scalar(headrk[:, c_], C("heads"), PC("r_k", c_), None, ALU.mult)\
                          .then_inc(init, 1)
                    with dve.Fori(0, NT) as j:
                        def wait(name, n):
                            dve.wait_ge(sm[name], j * PER[name] + n)
                        seq = bass.ds(j * P, P)
                        zseq = bass.ds(j * P + 1, P)
                        for c_ in range(CT):
                            nc.vector.tensor_tensor_scan(cum[:, c_], C("keep"),
                                                         lw[:, c_, seq], 0.0, ALU.mult, ALU.add)\
                              .then_inc(sm["cum"], 1)
                        wait("cum", CT)
                        nc.vector.tensor_tensor(ex[:, 2], cum[:], lw[:, :, seq], ALU.subtract).then_inc(sm["pre"], 1)
                        end = chunks(cum[:])[:, :, CHUNK - 1:CHUNK]
                        nc.vector.tensor_tensor(chunks(ex[:, 3]), end.broadcast_to([P, 2 * CT, CHUNK]),
                                                chunks(cum[:]), ALU.subtract).then_inc(sm["pre"], 1)
                        wait("ex", 1)
                        nc.vector.scalar_tensor_tensor(nr[:, :, 0], kk[:, :, seq], -1.0, ex[:, 2], ALU.mult, ALU.mult)\
                          .then_inc(sm["mul"], 1)
                        wait("ex", 2)
                        nc.vector.tensor_tensor(nr[:, :, 1], zT[:, R0:R0 + CT, zseq], ex[:, 0], ALU.mult)\
                          .then_inc(sm["mul"], 1)
                        wait("ex", 3)
                        nc.vector.tensor_tensor(bd[:], aa[:, :, seq], ex[:, 1], ALU.mult).then_inc(sm["mul"], 1)
                        nc.vector.tensor_tensor(kd[:], zT[:, K0:K0 + CT, zseq], ex[:, 1], ALU.mult)\
                          .then_inc(sm["mul"], 1)
                        for h in range(HEADS):
                            wait("pair", h + 1)
                            nc.vector.tensor_tensor(mats[:, h].rearrange("p a n -> p (a n)"), ps[:, 5 + h % 3],
                                                    C("mask4"), ALU.mult).then_inc(sm["pair_ev"], 1)
                        wait("bon", 1)
                        wait("vst", 1)
                        nc.vector.tensor_tensor(zT[:, V0:V0 + CT, zseq], vst[:],
                                                ps[:, 4].rearrange("p (c n) -> p c n", c=CT), ALU.mult)\
                          .then_inc(sm["bon_ev"], 1)
                        for l in range(NL):
                            for g in range(2):
                                wait("t", 2 * l + g + 1)
                                hs = slice(4 * g, 4 * g + 4)
                                nc.vector.tensor_tensor(tt[:, hs].rearrange("p h a n -> p (h a n)"),
                                                        tt[:, hs].rearrange("p h a n -> p (h a n)"),
                                                        ps[:, DB[g]:DB[g] + 2].rearrange("p a n -> p (a n)"), ALU.add)\
                                  .then_inc(sm["t_ev"], 1)
                        for g in range(2):
                            wait("wu", g + 1)
                            nc.vector.tensor_copy(wu[:, 4 * g:4 * g + 4].rearrange("p h a n -> p (h a n)"),
                                                  ps[:, XB[g]]).then_inc(sm["wu_ev"], 1)
                        wait("dg", 2)
                        wait("mr", 1)
                        for i in range(2):
                            half = slice(64 * i, 64 * i + 64)
                            for ch in range(2):
                                m = nc.vector.tensor_tensor(
                                    mt[half, ch, :, half],
                                    ps[half, 1 + ch].rearrange("p (c n) -> p c n", c=CT)[:, :, half],
                                    dg[half, ch], ALU.add)
                            m.then_inc(sm["mt_ev"], 1)
                        wait("pt", 1)
                        nc.vector.tensor_tensor(pt[:], ps[:, 7].rearrange("p (c n) -> p c n", c=CT), nr[:, :, 1],
                                                ALU.add).then_inc(sm["pt_ev"], 1)
                        wait("y", 1)
                        nc.vector.tensor_copy(yrow[:, bass.ds(j, 1)].rearrange("p a n -> p (a n)"), ps[:, 6])\
                          .then_inc(sm["y_ev"], 1)

                @block.tensor
                def _(pe):
                    pe.wait_ge(init, 2 + CT)
                    pe.sem_inc(over, 1)
                    with pe.Fori(0, NT) as j:
                        def wait(name, n):
                            pe.wait_ge(sm[name], j * PER[name] + n)

                        def four_transposes(bank, src):
                            for c_ in range(CT):
                                m = nc.tensor.transpose(ps[:, bank, c_ * P:(c_ + 1) * P], src[:, c_], C("ident"))
                            m.then_inc(sm["tr"], 1)
                        wait("vst", 1)
                        four_transposes(3, vst)
                        wait("pmul", 1)
                        for c_ in range(CT):
                            m = nc.tensor.matmul(ps[:, 4, c_ * P:(c_ + 1) * P], headrk[:, c_], rk[:, c_],
                                                 start=True, stop=True)
                        m.then_inc(sm["bon"], 1)
                        wait("mul", 1)
                        four_transposes(0, nr[:, :, 0])
                        wait("pmul", 3)
                        four_transposes(1, ce[:, 0])
                        four_transposes(2, ce[:, 1])
                        wait("mul", 4)
                        for h in range(HEADS):
                            c_, half = head(h)
                            if h >= 3:
                                wait("pair_ev", h - 2)
                            bank = ps[:, 5 + h % 3]
                            both = nr[half, c_].rearrange("p a n -> p (a n)")
                            nc.tensor.matmul(bank[:, 0:2 * P], bd[half, c_], both, start=True, stop=True)
                            nc.tensor.matmul(bank[:, 2 * P:4 * P], kd[half, c_], both, start=True, stop=True)\
                              .then_inc(sm["pair"], 1)
                        wait("tok", 1)
                        wait("pair_ev", HEADS)
                        for h in range(HEADS):
                            m = nc.tensor.matmul(ps[:, 6, h * N:(h + 1) * N], mats[:, h, 2], v_rows(h),
                                                 start=True, stop=True)
                        m.then_inc(sm["bv"], 1)
                        wait("nb", 1)
                        for g in range(2):
                            wait("t0", 2 * g + 2)
                            for h in range(4):
                                m = nc.tensor.transpose(ps[:, XB[g], h * P:(h + 1) * P], tt[:, 4 * g + h, 1],
                                                        C("ident"))
                            m.then_inc(sm["t0_mm"], 1)
                        wait("bon_ev", 1)
                        for l in range(NL):
                            for g in range(2):
                                if l == 0:
                                    wait("t0_ev", g + 1)
                                else:
                                    wait("t_ev", 2 * (l - 1) + g + 1)
                                wait("off", 2 * l + g + 1)
                                for h in range(4):
                                    m = nc.tensor.matmul(ps[:, XB[g], h * P:(h + 1) * P], off[:, g, h],
                                                         tt[:, 4 * g + h, 0], start=True, stop=True)
                                m.then_inc(sm["x"], 1)
                            for g in range(2):
                                wait("x_ev", 2 * l + g + 1)
                                for h in range(4):
                                    o = ps[:, DB[g] + h // 2, (h % 2) * 2 * P:(h % 2) * 2 * P + 2 * P]
                                    hh = 4 * g + h
                                    nc.tensor.matmul(o[:, 0:P], tt[:, hh, 1], xx[:, hh], start=True, stop=True)
                                    m = nc.tensor.matmul(o[:, P:2 * P], xx[:, hh], tt[:, hh, 1], start=True, stop=True)
                                m.then_inc(sm["t"], 1)
                        wait("bv_ev", 1)
                        for g in range(2):
                            wait("t_ev", 2 * (NL - 1) + g + 1)
                            for h in range(4):
                                m = nc.tensor.matmul(ps[:, XB[g], h * P:(h + 1) * P], tt[:, 4 * g + h, 1],
                                                     nb[:, 4 * g + h].rearrange("p a n -> p (a n)"),
                                                     start=True, stop=True)
                            m.then_inc(sm["wu"], 1)
                        wait("wu_ev", 2)
                        for h in range(HEADS):
                            o = ps[:, 6, h * N:(h + 1) * N]
                            nc.tensor.matmul(o, mats[:, h, 1], wu[:, h, 1], start=(h == 0), stop=False,
                                             skip_group_check=True)
                            nc.tensor.matmul(o, mats[:, h, 3], v_rows(h), start=False, stop=False,
                                             skip_group_check=True)
                        for ch in range(2):
                            rows = slice(64 * ch, 64 * ch + 64)
                            for h in range(HEADS):
                                c_, half = head(h)
                                at = slice(c_ * P + 64 * (h % 2), c_ * P + 64 * (h % 2) + 64)
                                nc.tensor.matmul(ps[half, 1 + ch, at], wu[rows, h, 0], tok_rows(0, h)[rows],
                                                 start=True, stop=True)
                                nc.tensor.matmul(ps[half, 4 + ch, at], tok_rows(0, h)[rows], wu[rows, h, 1],
                                                 start=(h < 2), stop=False, skip_group_check=True)
                                m = nc.tensor.matmul(ps[half, 4 + ch, at], tok_rows(1, h)[rows], v_rows(h)[rows],
                                                     start=False, stop=False, skip_group_check=True)
                        m.then_inc(sm["mr"], 1)
                        for h in range(HEADS):
                            c_, half = head(h)
                            m = nc.tensor.matmul(ps[half, 7, c_ * P:(c_ + 1) * P], wu[:, h, 0], mats[:, h, 1],
                                                 start=True, stop=True)
                        m.then_inc(sm["pt"], 1)
                        wait("mt_ev", 2)
                        pe.wait_ge(over, j + 1)
                        for ch in range(2):
                            if ch == 1:
                                wait("st_ev", 1)
                            for c_ in range(CT):
                                m = nc.tensor.matmul(ps[:, 4 + ch, c_ * P:(c_ + 1) * P], mt[:, ch, c_], S[:, ch, c_],
                                                     start=False, stop=(c_ == CT - 1), skip_group_check=True)
                            m.then_inc(sm["st"], 1)
                            if ch == 0:
                                wait("pt_ev", 1)
                            rows = slice(64 * ch, 64 * ch + 64)
                            for c_ in range(CT):
                                m = nc.tensor.matmul(ps[rows, 6, c_ * P:(c_ + 1) * P], pt[:, c_, rows], S[:, ch, c_],
                                                     start=False, stop=(c_ == CT - 1), skip_group_check=True)
                            if ch == 1:
                                m.then_inc(sm["y"], 1)
                        wait("y_ev", 1)
                        wait("st_ev", 2)
                        pe.sem_inc(over, 1)
        if debug is not None and last_phase == 3:
            return dump(nc, ctx, debug, YTM[:].rearrange("p a b -> p (a b)"))
        kst.close()

        with phase() as st:
            wg = sb(st, "wg", [P, D_RWKV])
            yc = sb(st, "yc", [P, NT, D_RWKV])
            sq = sb(st, "sq4", [P, 2, D_RWKV])
            mean = sb(st, "mean", [P, NT * HEADS])
            var = sb(st, "var", [P, NT * HEADS])
            part = sb(st, "part", [P, 2, CT, P])
            yT = sb(st, "yT", [P, CT, SEQ])
            wg_in, cent, sq_s, var_s, root, yn, tr, gm, aff, fin, y_out, dch = sems(
                st, "wg_in", "cent", "sq_s", "var_s", "root4", "yn", "tr4", "gm4", "aff", "fin4", "y_out4", "dch4")

            def by_head(ap):
                return ap.rearrange("p (h n) -> p h n", n=N)
            with nc.Block() as block:
                @block.sync
                def _(sp):
                    sp.dma_start(wg[:], w_g_up[0]).then_inc(wg_in, 16)
                    sp.wait_ge(fin, 2 * NT)
                    sp.dma_start(yr_dram, yT[:].rearrange("p c s -> p (c s)")).then_inc(y_out, 16)
                    sp.wait_ge(y_out, 16)

                @block.vector
                def _(dve):
                    link = Chain(dve, dch)
                    for t in range(NT):
                        hs = slice(t * HEADS, (t + 1) * HEADS)
                        link(nc.vector.tensor_reduce(mean[:, hs], by_head(yrow[:, t]), AX.X, ALU.add))
                        link(nc.vector.tensor_scalar(mean[:, hs], mean[:, hs], 1.0 / N, None, ALU.mult))
                        nc.vector.tensor_tensor(by_head(yc[:, t]), by_head(yrow[:, t]),
                                                mean[:, hs].unsqueeze(2).broadcast_to([P, HEADS, N]), ALU.subtract)\
                          .then_inc(cent, 1)
                        if t:
                            dve.wait_ge(sq_s, t)
                            nc.vector.tensor_reduce(var[:, (t - 1) * HEADS:t * HEADS], by_head(sq[:, (t - 1) % 2]),
                                                    AX.X, ALU.add).then_inc(var_s, 1)
                    dve.wait_ge(sq_s, NT)
                    nc.vector.tensor_reduce(var[:, (NT - 1) * HEADS:], by_head(sq[:, (NT - 1) % 2]),
                                            AX.X, ALU.add).then_inc(var_s, 1)
                    dve.wait_ge(var_s, NT)
                    nc.vector.tensor_scalar(var[:], var[:], 1.0 / N, LN_EPS, ALU.mult, ALU.add).then_inc(var_s, 1)
                    dve.wait_ge(root, 1)
                    link(nc.vector.reciprocal(var[:], var[:]))
                    for t in range(NT + 1):
                        if t < NT:
                            hs = slice(t * HEADS, (t + 1) * HEADS)
                            nc.vector.tensor_tensor(by_head(yc[:, t]), by_head(yc[:, t]),
                                                    var[:, hs].unsqueeze(2).broadcast_to([P, HEADS, N]), ALU.mult)\
                              .then_inc(yn, 1)
                        if t:
                            u = t - 1
                            dve.wait_ge(aff, CT * t)
                            pp = part[:, u % 2]
                            nc.vector.tensor_tensor(pp, pp, zT[:, V0:V0 + CT, 1 + u * P:1 + t * P],
                                                    ALU.add).then_inc(fin, 1)
                            dve.wait_ge(fin, 2 * u + 1)
                            dve.wait_ge(gm, t)
                            nc.vector.tensor_tensor(yT[:, :, u * P:t * P], pp,
                                                    ps[:, 2 + u % 2].rearrange("p (c n) -> p c n", c=CT), ALU.mult)\
                              .then_inc(fin, 1)

                @block.scalar
                def _(act):
                    for t in range(NT):
                        act.wait_ge(cent, t + 1)
                        if t >= 2:
                            act.wait_ge(var_s, t - 1)
                        nc.scalar.activation(sq[:, t % 2], yc[:, t], ACT.Square).then_inc(sq_s, 1)
                    act.wait_ge(var_s, NT + 1)
                    nc.scalar.activation(var[:], var[:], ACT.Sqrt).then_inc(root, 1)
                    for t in range(NT):
                        act.wait_ge(tr, t + 1)
                        if t >= 2:
                            act.wait_ge(fin, 2 * (t - 1))
                        for c_ in range(CT):
                            nc.scalar.activation(part[:, t % 2, c_], ps[:, t % 2, c_ * P:(c_ + 1) * P], ACT.Identity,
                                                 scale=PC("ln_w", c_), bias=PC("ln_b", c_)).then_inc(aff, 1)

                @block.tensor
                def _(pe):
                    pe.wait_ge(wg_in, 16)
                    for t in range(NT):
                        pe.wait_ge(yn, t + 1)
                        if t >= 2:
                            pe.wait_ge(aff, CT * (t - 1))
                            pe.wait_ge(fin, 2 * (t - 1))
                        for c_ in range(CT):
                            m = nc.tensor.transpose(ps[:, t % 2, c_ * P:(c_ + 1) * P], yc[:, t, c_ * P:(c_ + 1) * P],
                                                    C("ident"))
                        m.then_inc(tr, 1)
                        for c_ in range(CT):
                            m = nc.tensor.matmul(ps[:, 2 + t % 2, c_ * P:(c_ + 1) * P], wg[:, c_ * P:(c_ + 1) * P],
                                                 Z(GL)[:, t * P:(t + 1) * P], start=True, stop=True)
                        m.then_inc(gm, 1)
        if debug is not None and last_phase == 4:
            with nc.sbuf_tensor("dbgt", [P, CT * SEQ], f32) as d, nc.semaphore("ds") as s:
                with nc.Block() as block:
                    @block.sync
                    def _(sp):
                        sp.dma_start(d[:], yr_dram).then_inc(s, 16)
                        sp.wait_ge(s, 16)
                return dump(nc, ctx, debug, d[:])
        zst.close()

        QK = 2 * HEADS
        with ExitStack() as st5:
            qkT = sb(st5, "qkT", [P, QK, SEQ])
            vv = sb(st5, "vv", [P, NT, HEADS, N])
            with phase() as st:
                zm = sb(st, "zm5", [P, NT, MLA_COLS])
                wuq = sb(st, "wuq", [P, 2, HEADS * QKD])
                wukv = sb(st, "wukv", [P, HEADS * P])
                g_lat = sb(st, "g_lat", [P, Q_LORA + KV_LORA])
                g_row = sb(st, "g_row", [P, 2, QKD])
                gain = sb(st, "gain", [P, QK, QKD])
                posi = sb(st, "posi", [P, NT], i32)
                posf = sb(st, "posf", [P, NT])
                ang = sb(st, "ang", [P, NT, 16])
                turns = sb(st, "turns", [P, NT, 16])
                trig = sb(st, "trig", [P, 2, NT, 16])
                junk = sb(st, "junk5", [P, Q_LORA])
                sl = sb(st, "sl", [P, 2, NT])
                zn = sb(st, "zn", [P, 2, Q_LORA + KV_LORA])
                znT = sb(st, "znT", [P, 2, 3, P])
                qk = sb(st, "qk", [P, 2, QK, QKD])
                sqk = sb(st, "sqk", [P, QK, QKD])
                ssn = sb(st, "ssn", [P, NT, QK])
                rot = sb(st, "rot", [P, 2, 2, QK, 16])
                zrow = sb(st, "zrow", [P, D])
                z_in, z_out, m_in, w_in5, lat, root, dch, ang_s, trig_s, zn_s, trl, trl_ev, up, q_ev, v_ev, k_ev, pe_ev, sq_s, \
                    ssn_s, nroot, nrm, gained, roped, trq, trq_a, trq_d, gain_s = sems(
                        st, "z_in", "z_out", "m_in", "w_in5", "lat", "root5", "dch5", "ang_s", "trig_s", "zn_s", "trl", "trl_ev", "up5",
                        "q_ev", "v_ev", "k_ev", "pe_ev", "sq_s5", "ssn_s", "nroot", "nrm", "gained", "roped", "trq",
                        "trq_a", "trq_d", "gain_s")
                with nc.Block() as block:
                    @block.sync
                    def _(sp):
                        sp.dma_start(zm[:].rearrange("p t n -> p (t n)"), zm_dram).then_inc(m_in, 16)
                        sp.dma_start(posi[:], pos).then_inc(m_in, 16)
                        sp.dma_start(g_row[:].rearrange("p a n -> p (a n)"),
                                     qk_gain.broadcast_to([P, 2 * QKD])).then_inc(m_in, 16)
                        sp.dma_start(g_lat[:, 0:Q_LORA], g_q_a.broadcast_to([P, Q_LORA])).then_inc(m_in, 16)
                        sp.dma_start(g_lat[:, Q_LORA:], g_kv_a.broadcast_to([P, KV_LORA])).then_inc(m_in, 16)
                        sp.dma_start(wuq[:], w_uq[0].rearrange("(k p) n -> p k n", p=P)).then_inc(w_in5, 16)
                        sp.dma_start(wukv[:], w_ukv[0]).then_inc(w_in5, 16)
                        sp.wait_ge(z_in, 1)
                        free = y_dram[SURE * P:].rearrange("(a b p) d -> a p b d", p=P, b=8)
                        for a_ in range(free.shape[0]):
                            sp.dma_start(free[a_], zrow[:].unsqueeze(1).broadcast_to([P, 8, D])).then_inc(z_out, 16)
                        sp.wait_ge(z_out, 16 * free.shape[0])

                    @block.gpsimd
                    def _(pool):
                        nc.gpsimd.memset(zrow[:], 0.0).then_inc(z_in, 1)
                        pool.wait_ge(m_in, 80)
                        for i in range(2):
                            nc.gpsimd.tensor_copy(gain[:, i * HEADS:(i + 1) * HEADS],
                                                  g_row[:, i].unsqueeze(1).broadcast_to([P, HEADS, QKD]))\
                              .then_inc(gain_s, 1)
                        pool.wait_ge(gain_s, 2)
                        for t in range(NT):
                            b = t % 2
                            if t >= 2:
                                pool.wait_ge(trq, 4 * (t - 1))
                            nc.gpsimd.tensor_copy(
                                qk[:, b, HEADS:, N:QKD],
                                zm[:, t, Q_LORA + KV_LORA:].unsqueeze(1).broadcast_to([P, HEADS, ROPE])).then_inc(pe_ev, 1)
                            pool.wait_ge(nrm, t + 1)
                            nc.gpsimd.tensor_tensor(qk[:, b], qk[:, b], gain[:], ALU.mult).then_inc(gained, 1)

                    @block.scalar
                    def _(act):
                        act.wait_ge(m_in, 80)
                        n = 0
                        for t in range(NT):
                            for i, (a, b) in enumerate(((0, Q_LORA), (Q_LORA, Q_LORA + KV_LORA))):
                                if n:
                                    act.wait_ge(lat, n)
                                n += 1
                                nc.scalar.activation(junk[:, 0:b - a], zm[:, t, a:b], ACT.Square,
                                                     accum_out=sl[:, i, t:t + 1]).then_inc(lat, 1)
                        act.wait_ge(ang_s, 1)
                        nc.scalar.activation(trig[:, 0], trig[:, 0], ACT.Sin).then_inc(trig_s, 1)
                        nc.scalar.activation(trig[:, 1], trig[:, 1], ACT.Sin).then_inc(trig_s, 1)
                        act.wait_ge(dch, 2)
                        nc.scalar.activation(sl[:], sl[:], ACT.Sqrt).then_inc(root, 1)
                        for t in range(NT):
                            b = t % 2
                            act.wait_ge(trl, t + 1)
                            nc.scalar.activation(znT[:, b].rearrange("p a n -> p (a n)"), ps[:, b, 0:3 * P], ACT.Copy)\
                               .then_inc(trl_ev, 1)
                            act.wait_ge(up, t + 1)
                            if t >= 2:
                                act.wait_ge(trq, 4 * (t - 1))
                            nc.scalar.activation(qk[:, b, 0:HEADS].rearrange("p (a h) n -> p a (h n)", a=2),
                                                 ps[:, 2:4, 0:4 * QKD], ACT.Copy).then_inc(q_ev, 1)
                            kv = ps[:, 4:6].rearrange("p a n -> p (a n)").rearrange("p (h n) -> p h n", n=P)
                            act.wait_ge(k_ev, t + 1)
                            nc.scalar.activation(vv[:, t], kv[:, :, N:P], ACT.Copy).then_inc(v_ev, 1)
                            act.wait_ge(q_ev, t + 1)
                            act.wait_ge(pe_ev, t + 1)
                            if t:
                                act.wait_ge(ssn_s, 2 * t)
                            nc.scalar.activation(sqk[:], qk[:, b], ACT.Square).then_inc(sq_s, 1)
                            act.wait_ge(ssn_s, 2 * t + 2)
                            nc.scalar.activation(ssn[:, t], ssn[:, t], ACT.Sqrt).then_inc(nroot, 1)
                            for g in (0, 2):
                                act.wait_ge(trq, 4 * t + g + 1)
                                nc.scalar.activation(qkT[0:QKD, 4 * g:4 * g + 4, t * P:(t + 1) * P],
                                                     ps[0:QKD, 6 + g % 2].rearrange("p (h n) -> p h n", h=4), ACT.Copy)\
                                   .then_inc(trq_a, 1)

                    @block.vector
                    def _(dve):
                        link = Chain(dve, dch)
                        dve.wait_ge(lat, 2 * NT)
                        link(nc.vector.tensor_scalar(sl[:, 0], sl[:, 0], 1.0 / Q_LORA, EPS, ALU.mult, ALU.add))
                        link(nc.vector.tensor_scalar(sl[:, 1], sl[:, 1], 1.0 / KV_LORA, EPS, ALU.mult, ALU.add))
                        link(nc.vector.tensor_copy(posf[:], posi[:]))
                        link(nc.vector.tensor_tensor(ang[:], posf[:].unsqueeze(2).broadcast_to([P, NT, 16]),
                                                     C("freq").unsqueeze(1).broadcast_to([P, NT, 16]), ALU.mult))
                        big = 1.5 * 2.0 ** 23
                        for i, shift in enumerate((0.0, 0.25)):
                            link(nc.vector.tensor_scalar(turns[:], ang[:], 1.0 / (2 * math.pi), shift,
                                                         ALU.mult, ALU.add))
                            link(nc.vector.tensor_scalar(turns[:], turns[:], big, None, ALU.add))
                            link(nc.vector.tensor_scalar(turns[:], turns[:], -big, None, ALU.add))
                            src = ang[:]
                            for part_ in two_pi_parts():
                                link(nc.vector.scalar_tensor_tensor(trig[:, i], turns[:], -part_, src,
                                                                    ALU.mult, ALU.add))
                                src = trig[:, i]
                            link(nc.vector.tensor_scalar(trig[:, i], trig[:, i], math.pi / 2 if i else 0.0, 3.1415925,
                                                         ALU.add, ALU.min))
                            link(nc.vector.tensor_scalar(trig[:, i], trig[:, i], -3.1415925, None, ALU.max))
                        nc.vector.tensor_copy(posf[:], posi[:]).then_inc(ang_s, 1)
                        dve.wait_ge(root, 1)
                        link(nc.vector.reciprocal(sl[:], sl[:]))
                        dve.wait_ge(trig_s, 2)

                        def latents(t):
                            if t >= 2:
                                dve.wait_ge(trl, t - 1)
                            nc.vector.scalar_tensor_tensor(zn[:, t % 2, 0:Q_LORA], zm[:, t, 0:Q_LORA], sl[:, 0, t:t + 1],
                                                           g_lat[:, 0:Q_LORA], ALU.mult, ALU.mult).then_inc(zn_s, 1)
                            nc.vector.scalar_tensor_tensor(zn[:, t % 2, Q_LORA:], zm[:, t, Q_LORA:Q_LORA + KV_LORA],
                                                           sl[:, 1, t:t + 1], g_lat[:, Q_LORA:], ALU.mult, ALU.mult)\
                              .then_inc(zn_s, 1)
                        latents(0)
                        for t in range(NT):
                            b = t % 2
                            if t + 1 < NT:
                                latents(t + 1)
                            dve.wait_ge(up, t + 1)
                            if t >= 2:
                                dve.wait_ge(trq, 4 * (t - 1))
                            kv = ps[:, 4:6].rearrange("p a n -> p (a n)").rearrange("p (h n) -> p h n", n=P)
                            nc.vector.tensor_copy(qk[:, b, HEADS:, 0:N], kv[:, :, 0:N]).then_inc(k_ev, 1)
                            dve.wait_ge(sq_s, t + 1)
                            nc.vector.tensor_reduce(ssn[:, t], sqk[:], AX.X, ALU.add).then_inc(ssn_s, 1)
                            dve.wait_ge(ssn_s, 2 * t + 1)
                            nc.vector.tensor_scalar(ssn[:, t], ssn[:, t], 1.0 / QKD, EPS, ALU.mult, ALU.add)\
                              .then_inc(ssn_s, 1)
                            dve.wait_ge(nroot, t + 1)
                            link(nc.vector.reciprocal(ssn[:, t], ssn[:, t]))
                            nc.vector.tensor_tensor(qk[:, b], qk[:, b],
                                                    ssn[:, t].unsqueeze(2).broadcast_to([P, QK, QKD]), ALU.mult)\
                              .then_inc(nrm, 1)
                            dve.wait_ge(gained, t + 1)
                            for i in range(2):
                                tri = trig[:, i, t].unsqueeze(1).broadcast_to([P, QK, 16])
                                for j in range(2):
                                    link(nc.vector.tensor_tensor(rot[:, i, j], qk[:, b, :, N + 16 * j:N + 16 * j + 16],
                                                                 tri, ALU.mult))
                            nc.vector.tensor_tensor(qk[:, b, :, N:N + 16], rot[:, 1, 0], rot[:, 0, 1],
                                                    ALU.subtract).then_inc(roped, 1)
                            nc.vector.tensor_tensor(qk[:, b, :, N + 16:QKD], rot[:, 1, 1], rot[:, 0, 0],
                                                    ALU.add).then_inc(roped, 1)
                            for g in (1, 3):
                                dve.wait_ge(trq, 4 * t + g + 1)
                                nc.vector.tensor_copy(qkT[0:QKD, 4 * g:4 * g + 4, t * P:(t + 1) * P],
                                                      ps[0:QKD, 6 + g % 2].rearrange("p (h n) -> p h n", h=4))\
                                  .then_inc(trq_d, 1)

                    @block.tensor
                    def _(pe):
                        pe.wait_ge(w_in5, 32)

                        def latent_transposes(t):
                            pe.wait_ge(zn_s, 2 * t + 2)
                            if t >= 2:
                                pe.wait_ge(trl_ev, t - 1)
                            for i in range(3):
                                m = nc.tensor.transpose(ps[:, t % 2, i * P:(i + 1) * P],
                                                        zn[:, t % 2, i * P:(i + 1) * P], C("ident"))
                            m.then_inc(trl, 1)
                        latent_transposes(0)
                        for t in range(NT):
                            b = t % 2
                            if t + 1 < NT:
                                latent_transposes(t + 1)
                            pe.wait_ge(trl_ev, t + 1)
                            if t:
                                pe.wait_ge(q_ev, t)
                                pe.wait_ge(k_ev, t)
                                pe.wait_ge(v_ev, t)
                            for i in range(2):
                                for k in range(2):
                                    nc.tensor.matmul(ps[:, 2 + i, 0:4 * QKD], znT[:, b, k],
                                                     wuq[:, k, i * 4 * QKD:(i + 1) * 4 * QKD],
                                                     start=(k == 0), stop=(k == 1))
                            for i in range(2):
                                m = nc.tensor.matmul(ps[:, 4 + i], znT[:, b, 2], wukv[:, i * 512:(i + 1) * 512],
                                                     start=True, stop=True)
                            m.then_inc(up, 1)
                            pe.wait_ge(roped, 2 * t + 2)
                            for g in range(4):
                                done = trq_d if g % 2 else trq_a
                                if 2 * t + g // 2:
                                    pe.wait_ge(done, 2 * t + g // 2)
                                for i in range(4):
                                    m = nc.tensor.transpose(ps[0:QKD, 6 + g % 2, i * P:(i + 1) * P],
                                                            qk[:, b, 4 * g + i], C("ident"))
                                m.then_inc(trq, 1)

            with phase() as st:
                prob = sb(st, "prob", [P, 2, SEQ])
                pT = sb(st, "pT", [P, 2, NT, P])
                orow = sb(st, "orow", [P, NT, D_RWKV])
                nmax = sb(st, "nmax", [P, HEADS * NT])
                rsum = sb(st, "rsum", [P, HEADS * NT])
                s_mm, mx, nm, e_s, rec, tp, tp_d, tp_a, av, o_ev, tf, tf_ev = sems(
                    st, "s_mm", "mx", "nm", "e_s", "rec", "tp", "tp_d", "tp_a", "av", "o_ev", "tf", "tf_ev")
                items = [(h, i) for h in range(HEADS) for i in range(NT)]
                wide = [n for n, (h, i) in enumerate(items) if i >= 4]
                SCALE = QKD ** -0.5

                def wides(n):
                    return sum(w < n for w in wide)
                with nc.Block() as block:
                    @block.tensor
                    def _(pe):
                        def scores(n):
                            h, i = items[n]
                            if n >= 2:
                                pe.wait_ge(e_s, n - 1)
                            bank = 2 * (n % 2)
                            q = qkT[0:QKD, h, i * P:(i + 1) * P]
                            kT_ = qkT[0:QKD, HEADS + h]
                            for a in range(0, i * P, 512):
                                w_ = min(512, i * P - a)
                                nc.tensor.matmul(ps[:, bank + a // 512, 0:w_], q, kT_[:, a:a + w_], start=True, stop=True)
                            at = (i % 4) * P
                            o = ps[:, bank + i // 4, at:at + P]
                            nc.tensor.matmul(o, q, kT_[:, i * P:(i + 1) * P], start=True, stop=False)
                            nc.tensor.matmul(o, C("ident"), C("causal"), start=False, stop=True).then_inc(s_mm, 1)

                        def turn(n):
                            h, i = items[n]
                            pe.wait_ge(e_s, n + 1)
                            if n:
                                pe.wait_ge(tp_d, n)
                            if wides(n):
                                pe.wait_ge(tp_a, wides(n))
                            for k in range(i + 1):
                                m = nc.tensor.transpose(ps[:, 4 + k // 4, (k % 4) * P:(k % 4 + 1) * P],
                                                        prob[:, n % 2, k * P:(k + 1) * P], C("ident"))
                            m.then_inc(tp, 1)

                        def values(n):
                            h, i = items[n]
                            pe.wait_ge(tp_d, n + 1)
                            if wides(n + 1):
                                pe.wait_ge(tp_a, wides(n + 1))
                            if n >= 2:
                                pe.wait_ge(o_ev, n - 1)
                            for k in range(i + 1):
                                m = nc.tensor.matmul(ps[:, 6 + n % 2, 0:N], pT[:, n % 2, k], vv[:, k, h],
                                                     start=(k == 0), stop=(k == i))
                            m.then_inc(av, 1)
                        scores(0)
                        for n in range(len(items)):
                            if n + 1 < len(items):
                                scores(n + 1)
                            turn(n)
                            if n:
                                values(n - 1)
                        values(len(items) - 1)
                        pe.wait_ge(o_ev, len(items))
                        for t in range(NT):
                            if t >= 2:
                                pe.wait_ge(tf_ev, t - 1)
                            for c_ in range(CT):
                                m = nc.tensor.transpose(ps[:, t % 2, c_ * P:(c_ + 1) * P],
                                                        orow[:, t, c_ * P:(c_ + 1) * P], C("ident"))
                            m.then_inc(tf, 1)

                    @block.scalar
                    def _(act):
                        for n, (h, i) in enumerate(items):
                            act.wait_ge(nm, n + 1)
                            if n >= 2:
                                act.wait_ge(tp, n - 1)
                            bank = 2 * (n % 2)
                            s_ = ps[:, bank:bank + 2].rearrange("p a n -> p (a n)")[:, 0:(i + 1) * P]
                            nc.scalar.activation(prob[:, n % 2, 0:(i + 1) * P], s_, ACT.Exp, bias=nmax[:, n:n + 1],
                                                 scale=SCALE, accum_out=rsum[:, n:n + 1]).then_inc(e_s, 1)
                            if i >= 4:
                                act.wait_ge(tp, n + 1)
                                if n >= 2:
                                    act.wait_ge(av, n - 1)
                                nc.scalar.activation(pT[:, n % 2, 4:i + 1].rearrange("p k n -> p (k n)"),
                                                     ps[:, 5, 0:(i - 3) * P], ACT.Copy).then_inc(tp_a, 1)

                    @block.vector
                    def _(dve):
                        def peak(n):
                            h, i = items[n]
                            dve.wait_ge(s_mm, n + 1)
                            bank = 2 * (n % 2)
                            s_ = ps[:, bank:bank + 2].rearrange("p a n -> p (a n)")[:, 0:(i + 1) * P]
                            nc.vector.tensor_reduce(nmax[:, n:n + 1], s_, AX.X, ALU.max).then_inc(mx, 1)
                            dve.wait_ge(mx, n + 1)
                            nc.vector.tensor_scalar(nmax[:, n:n + 1], nmax[:, n:n + 1], -SCALE, None, ALU.mult)\
                              .then_inc(nm, 1)

                        def out_rows(n):
                            h, i = items[n]
                            dve.wait_ge(rec, n + 1)
                            dve.wait_ge(av, n + 1)
                            nc.vector.tensor_scalar(orow[:, i, h * N:(h + 1) * N], ps[:, 6 + n % 2, 0:N],
                                                    rsum[:, n:n + 1], None, ALU.mult).then_inc(o_ev, 1)
                        peak(0)
                        for n, (h, i) in enumerate(items):
                            if n + 1 < len(items):
                                peak(n + 1)
                            dve.wait_ge(e_s, n + 1)
                            nc.vector.reciprocal(rsum[:, n:n + 1], rsum[:, n:n + 1]).then_inc(rec, 1)
                            dve.wait_ge(tp, n + 1)
                            if n >= 2:
                                dve.wait_ge(av, n - 1)
                            k = min(4, i + 1)
                            nc.vector.tensor_copy(pT[:, n % 2, 0:k].rearrange("p k n -> p (k n)"), ps[:, 4, 0:k * P])\
                              .then_inc(tp_d, 1)
                            if n:
                                out_rows(n - 1)
                        out_rows(len(items) - 1)
                        for t in range(NT):
                            dve.wait_ge(tf, t + 1)
                            nc.vector.tensor_copy(YTM[:, :, t * P:(t + 1) * P],
                                                  ps[:, t % 2].rearrange("p (c n) -> p c n", c=CT)).then_inc(tf_ev, 1)
        if debug is not None and last_phase == 6:
            return dump(nc, ctx, debug, YTM[:].rearrange("p a b -> p (a b)"))

        x1 = sb(ctx, "x1", [P, NT, D])
        with phase() as st:
            hT = sb(st, "hT7", [P, KD, SEQ])
            yT = sb(st, "yT7", [P, CT, SEQ])
            mT = sb(st, "mT", [P, KD, SEQ])
            wo = sb(st, "wo", [P, KD, D])
            wg = sb(st, "wg7", [P, 2, 2, KD, P])
            wb = sb(st, "wb7", [P, 2, 2, CT, P])
            gate = sb(st, "gate", [P, 2, SEQ])
            gt = sb(st, "gt7", [P, D])
            a_in, wo_in, gt_in, x_in7, g_mm, g_ev, b_mm, mer, o_mm, o_ev, o_add = sems(
                st, "a_in7", "wo_in", "gt_in7", "x_in7", "g_mm", "g_ev", "b_mm", "mer", "o_mm", "o_ev7", "o_add")
            wg_in = slots(st, "wg_in", 2)
            branches = (yT, YTM)
            with nc.Block() as block:
                @block.sync
                def _(sp):
                    def weights(b, ft):
                        if isinstance(ft, int):
                            pick = lambda v: v[ft]
                        else:
                            pick = lambda v: v[bass.ds(ft, 1)]
                        for br in range(2):
                            src = w_gates[ft + br * KD] if isinstance(ft, int) else \
                                w_gates[bass.ds(ft + br * KD, 1)].rearrange("a p k n -> (a p) k n")
                            sp.dma_start(wg[:, b, br], src).then_inc(wg_in[b], 16)
                        src = w_br[ft] if isinstance(ft, int) else \
                            w_br[bass.ds(ft, 1)].rearrange("a p b k n -> (a p) b k n")
                        sp.dma_start(wb[:, b], src).then_inc(wg_in[b], 16)
                    weights(0, 0)
                    sp.dma_start(hT[:].rearrange("p k s -> p (k s)"), h_dram).then_inc(a_in, 16)
                    sp.dma_start(yT[:].rearrange("p k s -> p (k s)"), yr_dram).then_inc(a_in, 16)
                    weights(1, 1)
                    sp.dma_start(wo[:], w_out[0].rearrange("(k p) n -> p k n", p=P)).then_inc(wo_in, 16)
                    sp.dma_start(gt[:], mod_dram[:, 2 * D:3 * D].broadcast_to([P, D])).then_inc(gt_in, 16)
                    sp.dma_start(x1[:], x[0].rearrange("(t p) d -> p t d", p=P)).then_inc(x_in7, 16)
                    with sp.Fori(0, KD // 2 - 1) as i:
                        for b in range(2):
                            sp.wait_ge(b_mm, 2 * (2 * i + b) + 2)
                            weights(b, 2 * i + (b + 2))

                @block.tensor
                def _(pe):
                    pe.wait_ge(a_in, 32)
                    with pe.Fori(0, KD // 2) as i:
                        for b in range(2):
                            pe.wait_ge(wg_in[b], i * 48 + 48)
                            for br in range(2):
                                pe.wait_ge(g_ev, 2 * (2 * i + b) + 1)
                                for n in range(2):
                                    for k in range(KD):
                                        m = nc.tensor.matmul(ps[:, 4 * br + n], wg[:, b, br, k],
                                                             hT[:, k, n * 512:(n + 1) * 512],
                                                             start=(k == 0), stop=(k == KD - 1))
                                m.then_inc(g_mm, 1)
                                pe.wait_ge(mer, 3 * (2 * i + b) + 1)
                                for n in range(2):
                                    for k in range(CT):
                                        m = nc.tensor.matmul(ps[:, 4 * br + 2 + n], wb[:, b, br, k],
                                                             branches[br][:, k, n * 512:(n + 1) * 512],
                                                             start=(k == 0), stop=(k == CT - 1))
                                m.then_inc(b_mm, 1)
                    pe.wait_ge(wo_in, 16)
                    pe.wait_ge(mer, 3 * KD + 1)
                    for t in range(NT):
                        if t >= 4:
                            pe.wait_ge(o_ev, t - 3)
                        for n in range(2):
                            for k in range(KD):
                                m = nc.tensor.matmul(ps[:, 2 * (t % 4) + n], mT[:, k, t * P:(t + 1) * P],
                                                     wo[:, k, n * 512:(n + 1) * 512],
                                                     start=(k == 0), stop=(k == KD - 1))
                        m.then_inc(o_mm, 1)

                @block.scalar
                def _(act):
                    act.sem_inc(g_ev, 1)
                    with act.Fori(0, KD) as i:
                        for br in range(2):
                            act.wait_ge(g_mm, 2 * i + br + 1)
                            act.wait_ge(mer, 3 * i + 1)
                            nc.scalar.activation(gate[:, br], ps[:, 4 * br:4 * br + 2].rearrange("p a n -> p (a n)"),
                                                 ACT.Sigmoid).then_inc(g_ev, 1)

                @block.vector
                def _(dve):
                    dve.sem_inc(mer, 1)
                    with dve.Fori(0, KD) as i:
                        out_t = mT[:, bass.ds(i, 1)].rearrange("p a n -> p (a n)")
                        for br in range(2):
                            dve.wait_ge(g_ev, 2 * i + br + 2)
                            dve.wait_ge(b_mm, 2 * i + br + 1)
                            dst = gate[:, 1] if br else out_t
                            m = nc.vector.tensor_tensor(dst, gate[:, br],
                                                        ps[:, 4 * br + 2:4 * br + 4].rearrange("p a n -> p (a n)"),
                                                        ALU.mult)
                            m.then_inc(mer, 1)
                            if br == 0:
                                continue
                            dve.wait_ge(mer, 3 * i + 3)
                            nc.vector.tensor_tensor(out_t, out_t, gate[:, 1], ALU.add).then_inc(mer, 1)
                    dve.wait_ge(gt_in, 16)
                    dve.wait_ge(x_in7, 16)
                    for t in range(NT):
                        dve.wait_ge(o_mm, t + 1)
                        if t >= 2:
                            dve.wait_ge(o_add, t - 1)
                        tmp = gate[:, t % 2]
                        nc.vector.tensor_tensor(tmp, ps[:, 2 * (t % 4):2 * (t % 4) + 2].rearrange("p a n -> p (a n)"),
                                                gt[:], ALU.mult).then_inc(o_ev, 1)
                        dve.wait_ge(o_ev, t + 1)
                        nc.vector.tensor_tensor(x1[:, t], x1[:, t], tmp, ALU.add).then_inc(o_add, 1)
        if debug is not None and last_phase == 7:
            return dump(nc, ctx, debug, x1[:].rearrange("p a b -> p (a b)"))

        top = sb(ctx, "top", [P, 2, NT])
        place = sb(ctx, "place", [P, 2, NT], i32)
        table = sb(ctx, "table", [1, NBLK + 2], i32)
        with phase() as st:
            shf = sb(st, "shf", [P, D])
            scf = sb(st, "scf", [P, D])
            wr = sb(st, "wr8", [P, KD, NG + NE])
            br_ = sb(st, "br8", [P, NG + NE])
            tok_i = sb(st, "tok_i", [P, NT], i32)
            zero_i = sb(st, "zero_i", [P, NBLK], i32)
            h2 = sb(st, "h2", [P, 3, D])
            junk = sb(st, "junk8", [P, D])
            h2T = sb(st, "h2T", [P, 2, KD, P])
            ss = sb(st, "ss8", [P, NT])
            lg = sb(st, "lg", [P, NT, NG + NE])
            g1 = sb(st, "g1", [P, NT, NG])
            gsum = sb(st, "gsum", [P, NT])
            e1 = sb(st, "e1", [P, NT, NE])
            e2 = sb(st, "e2", [P, NT, NE])
            hot = sb(st, "hot", [P, 2, NT, NE])
            both = sb(st, "both", [P, NT, NE])
            rank = sb(st, "rank", [P, NT, NE])
            run = sb(st, "run", [P, NT + 1, NE])
            blk = sb(st, "blk", [P, NE])
            inc = sb(st, "inc", [P, NE])
            cmp_ = sb(st, "cmp", [P, NE * NBLK])
            m1 = sb(st, "m1", [P, 4, NT])
            tbf = sb(st, "tbf", [1, NBLK + 2])
            mods, ssq, msq, root, h2_s, h2_mid, tr, tr_ev, lmm, lg_s, dch, ge, gx, mm8, z_s, plc, tb_s = sems(
                st, "mods", "ssq8", "msq", "root8", "h2_s", "h2_mid", "tr8", "tr_ev8", "lmm", "lg_s", "dch8", "ge",
                "gx", "mm8", "z_s", "plc", "tb_s")
            h2_out = slots(st, "h2_out", 3)
            h2_v = h2_dram.rearrange("(t p) d -> t p d", p=P)
            with nc.Block() as block:
                @block.sync
                def _(sp):
                    sp.dma_start(scf[:], mod_dram[:, 4 * D:5 * D].broadcast_to([P, D])).then_inc(mods, 16)
                    sp.dma_start(shf[:], mod_dram[:, 3 * D:4 * D].broadcast_to([P, D])).then_inc(mods, 16)
                    sp.dma_start(wr[:], w_router).then_inc(mods, 16)
                    sp.dma_start(br_[:], b_router.broadcast_to([P, NG + NE])).then_inc(mods, 16)
                    sp.dma_start(tok_i[:], tokens).then_inc(mods, 16)
                    for t in range(NT):
                        sp.wait_ge(h2_s, t + 1)
                        sp.dma_start(h2_v[t], h2[:, t % 3]).then_inc(h2_out[t % 3], 16)
                    for b in range(3):
                        sp.wait_ge(h2_out[b], 16 * len(range(b, NT, 3)))

                @block.gpsimd
                def _(pool):
                    nc.gpsimd.memset(zero_i[:], 0).then_inc(z_s, 1)
                    pool.wait_ge(z_s, 1)
                    pool.dma_start(slot_dram.rearrange("(p b) a -> p (b a)", p=P), zero_i[:]).then_inc(scattered, 16)
                    pool.wait_ge(scattered, 16)
                    pool.wait_ge(mods, 80)
                    pool.wait_ge(plc, 2)
                    for i in range(2):
                        for t in range(NT):
                            pool.indirect_dma_start(
                                out=slot_dram, in_=tok_i[:, t:t + 1], in_offset=None,
                                out_offset=bass.IndirectOffsetOnAxis(ap=place[:, i, t:t + 1].bitcast(u32), axis=0),
                            ).then_inc(scattered, 16)
                    pool.wait_ge(scattered, 16 + 2 * NT * 16)

                @block.scalar
                def _(act):
                    for t in range(NT):
                        if t:
                            act.wait_ge(ssq, t)
                        nc.scalar.activation(junk[:], x1[:, t], ACT.Square, accum_out=ss[:, t:t + 1]).then_inc(ssq, 1)
                    act.wait_ge(msq, 1)
                    nc.scalar.activation(ss[:], ss[:], ACT.Sqrt).then_inc(root, 1)
                    for t in range(NT):
                        for g in range(2):
                            act.wait_ge(tr, 2 * t + g + 1)
                            if t >= 2:
                                act.wait_ge(lmm, t - 1)
                            nc.scalar.activation(h2T[:, t % 2, 4 * g:4 * g + 4].rearrange("p a b -> p (a b)"),
                                                 ps[:, 2 * (t % 2) + g], ACT.Copy).then_inc(tr_ev, 1)
                    act.wait_ge(ge, 1)
                    nc.scalar.activation(g1[:], g1[:], ACT.Exp).then_inc(gx, 1)
                    act.wait_ge(ge, 2)
                    nc.scalar.activation(m1[:, 2], m1[:, 2], ACT.Exp).then_inc(gx, 1)

                @block.vector
                def _(dve):
                    V = nc.vector
                    link = Chain(dve, dch)
                    dve.wait_ge(mods, 80)
                    dve.wait_ge(ssq, NT)
                    V.tensor_scalar(ss[:], ss[:], 1.0 / D, EPS, ALU.mult, ALU.add).then_inc(msq, 1)
                    dve.wait_ge(root, 1)
                    link(V.reciprocal(ss[:], ss[:]))
                    for t in range(NT + 1):
                        if t < NT:
                            b = t % 3
                            if t >= 3:
                                dve.wait_ge(h2_out[b], 16 * (t // 3))
                                dve.wait_ge(tr, 2 * (t - 2))
                            V.scalar_tensor_tensor(h2[:, b], x1[:, t], ss[:, t:t + 1], scf[:], ALU.mult, ALU.mult)\
                             .then_inc(h2_mid, 1)
                            dve.wait_ge(h2_mid, t + 1)
                            V.tensor_tensor(h2[:, b], h2[:, b], shf[:], ALU.add).then_inc(h2_s, 1)
                        if t:
                            dve.wait_ge(lmm, t)
                            V.tensor_tensor(lg[:, t - 1], ps[:, 4 + (t - 1) % 2, 0:NG + NE], br_[:], ALU.add)\
                             .then_inc(lg_s, 1)
                    dve.wait_ge(lg_s, NT)
                    G, E = lg[:, :, 0:NG], lg[:, :, NG:]

                    def wide(ap, n):
                        return ap.unsqueeze(2).broadcast_to([P, NT, n])

                    def iota(n):
                        return C("iota")[:, 0:n].unsqueeze(1).broadcast_to([P, NT, n])

                    def first_hot(dst, vals, peak, n):
                        link(V.tensor_tensor(dst, vals, wide(peak, n), ALU.not_equal))
                        link(V.scalar_tensor_tensor(dst, dst, 1000.0, iota(n), ALU.mult, ALU.add))
                        link(V.tensor_reduce(m1[:, 3], dst, AX.X, ALU.min))
                        link(V.tensor_tensor(dst, iota(n), wide(m1[:, 3], n), ALU.is_equal))
                    link(V.tensor_reduce(gsum[:], G, AX.X, ALU.max))
                    V.tensor_tensor(g1[:], G, wide(gsum[:], NG), ALU.subtract).then_inc(ge, 1)
                    first_hot(e1[:, :, 0:NG], G, gsum[:], NG)
                    link(V.tensor_copy(both[:].rearrange("p t (g e) -> p t g e", g=NG),
                                       e1[:, :, 0:NG].unsqueeze(3).broadcast_to([P, NT, NG, EPG])))
                    link(V.tensor_tensor(e2[:], E, both[:], ALU.mult))
                    link(V.tensor_scalar(both[:], both[:], -1.0, 1e30, ALU.add, ALU.mult))
                    link(V.tensor_tensor(e2[:], e2[:], both[:], ALU.add))
                    link(V.tensor_reduce(m1[:, 0], e2[:], AX.X, ALU.max))
                    first_hot(hot[:, 0], e2[:], m1[:, 0], NE)
                    link(V.scalar_tensor_tensor(e2[:], hot[:, 0], -2e30, e2[:], ALU.mult, ALU.add))
                    link(V.tensor_reduce(m1[:, 1], e2[:], AX.X, ALU.max))
                    V.tensor_tensor(m1[:, 2], m1[:, 1], m1[:, 0], ALU.subtract).then_inc(ge, 1)
                    first_hot(hot[:, 1], e2[:], m1[:, 1], NE)
                    V.tensor_tensor(both[:], hot[:, 0], hot[:, 1], ALU.add).then_inc(ge, 1)
                    dve.wait_ge(gx, 2)
                    link(V.tensor_reduce(gsum[:], g1[:], AX.X, ALU.add))
                    link(V.tensor_scalar(m1[:, 0], m1[:, 2], 1.0, None, ALU.add))
                    link(V.tensor_tensor(gsum[:], gsum[:], m1[:, 0], ALU.mult))
                    link(V.reciprocal(top[:, 0], gsum[:]))
                    link(V.tensor_tensor(top[:, 1], top[:, 0], m1[:, 2], ALU.mult))
                    dve.wait_ge(mm8, 1)
                    link(V.memset(run[:, 0], 0.0))
                    for t in range(NT):
                        link(V.tensor_tensor(run[:, t + 1], run[:, t], ps[:, 7, t * NE:(t + 1) * NE], ALU.add))
                    link(V.tensor_tensor(rank[:], run[:, 0:NT], ps[:, 6, 0:NT * NE].rearrange("p (t e) -> p t e", t=NT),
                                         ALU.add))
                    c3 = cmp_[:, 0:NE * 8].rearrange("p (e m) -> p e m", m=8)
                    link(V.tensor_tensor(c3, run[:, NT].unsqueeze(2).broadcast_to([P, NE, 8]),
                                         C("thr").unsqueeze(1).broadcast_to([P, NE, 8]), ALU.is_gt))
                    link(V.tensor_reduce(blk[:], c3, AX.X, ALU.add))
                    link(V.tensor_tensor_scan(inc[:], C("ones")[:, 0:NE], blk[:], 0.0, ALU.mult, ALU.add))
                    link(V.tensor_tensor(blk[:], inc[:], blk[:], ALU.subtract))
                    link(V.scalar_tensor_tensor(rank[:], blk[:].unsqueeze(1).broadcast_to([P, NT, NE]), float(P),
                                                rank[:], ALU.mult, ALU.add))
                    for i in range(2):
                        link(V.tensor_tensor(e1[:], hot[:, i], rank[:], ALU.mult))
                        link(V.tensor_reduce(m1[:, i], e1[:], AX.X, ALU.add))
                        V.tensor_copy(place[:, i], m1[:, i]).then_inc(plc, 1)
                    c2 = cmp_[0:1].rearrange("p (b e) -> p b e", e=NE)
                    link(V.tensor_tensor(c2, inc[0:1].unsqueeze(1).broadcast_to([1, NBLK, NE]),
                                         C("iota")[0:1].unsqueeze(2).broadcast_to([1, NBLK, NE]), ALU.is_le))
                    link(V.tensor_reduce(tbf[:, 0:NBLK], c2, AX.X, ALU.add))
                    link(V.tensor_scalar(tbf[:, 0:NBLK], tbf[:, 0:NBLK], float(NE - 1), None, ALU.min))
                    link(V.tensor_scalar(cmp_[0:1, 0:NBLK // 2], C("iota")[0:1, 0:NBLK // 2], 2.0, None, ALU.mult))
                    link(V.tensor_tensor(cmp_[0:1, 0:NBLK // 2], inc[0:1, NE - 1:NE].broadcast_to([1, NBLK // 2]),
                                         cmp_[0:1, 0:NBLK // 2], ALU.is_gt))
                    link(V.tensor_reduce(tbf[:, NBLK:NBLK + 1], cmp_[0:1, 0:NBLK // 2], AX.X, ALU.add))
                    link(V.memset(tbf[:, NBLK + 1:], 0.0))
                    V.tensor_copy(table[:], tbf[:]).then_inc(tb_s, 1)
                    dve.wait_ge(tb_s, 1)

                @block.tensor
                def _(pe):
                    pe.wait_ge(mods, 80)
                    for t in range(NT + 1):
                        if t < NT:
                            pe.wait_ge(h2_s, t + 1)
                            if t >= 2:
                                pe.wait_ge(tr_ev, 2 * (t - 1))
                            for g in range(2):
                                for j in range(4):
                                    k = 4 * g + j
                                    m = nc.tensor.transpose(ps[:, 2 * (t % 2) + g, j * P:(j + 1) * P],
                                                            h2[:, t % 3, k * P:(k + 1) * P], C("ident"))
                                m.then_inc(tr, 1)
                        if t:
                            u = t - 1
                            pe.wait_ge(tr_ev, 2 * t)
                            if u >= 2:
                                pe.wait_ge(lg_s, u - 1)
                            for k in range(KD):
                                m = nc.tensor.matmul(ps[:, 4 + u % 2, 0:NG + NE], h2T[:, u % 2, k], wr[:, k],
                                                     start=(k == 0), stop=(k == KD - 1))
                            m.then_inc(lmm, 1)
                    pe.wait_ge(ge, 3)
                    sel = both[:].rearrange("p t e -> p (t e)")
                    nc.tensor.matmul(ps[:, 6, 0:NT * NE], C("before"), sel, start=True, stop=True)
                    nc.tensor.matmul(ps[:, 7, 0:NT * NE], C("ones"), sel, start=True, stop=True).then_inc(mm8, 1)

        with phase() as st:
            gu = sb(st, "gu", [P, 2, 2, KD, FE])
            dn = sb(st, "dn", [P, 2, 2, D])
            idx = sb(st, "idx", [P, 2], i32)
            xg = sb(st, "xg", [P, 2, D])
            xT = sb(st, "xT", [P, 2, KD, P])
            sg = sb(st, "sg", [P, 2, FE])
            hid = sb(st, "hid", [P, 2, FE])
            hidT = sb(st, "hidT", [P, 2, 2, P])
            yo = sb(st, "yo", [P, 2, D])
            gt = sb(st, "gt9", [P, D])
            gt_in, used, dn_used, xt_s, xt_ev, gmm, sg_s, hid_mid, hid_s, ht, ht_ev, dmm, y_ev, stored, listed = sems(
                st, "gt_in9", "gu_used", "dn_used", "xt_s", "xt_ev", "gmm", "sg_s9", "hid_mid", "hid_s", "ht", "ht_ev",
                "dmm", "y_ev9", "stored", "listed")
            gu_in, dn_in, y_out = (slots(st, n, 2) for n in ("gu_in", "dn_in", "y_out9"))
            wg_v = w_e_gate[0].rearrange("e (p k) n -> e p k n", k=KD)
            wu_v = w_e_up[0].rearrange("e (p k) n -> e p k n", k=KD)
            wd_v = w_e_down[0].rearrange("e (p k) n -> e p k n", k=2)

            def pairs(eng):
                return eng.value_load(table[0:1, NBLK:NBLK + 1], min_val=1, max_val=NBLK // 2)
            with nc.Block() as block:
                @block.sync
                def _(sp):
                    sp.dma_start(gt[:], mod_dram[:, 5 * D:6 * D].broadcast_to([P, D])).then_inc(gt_in, 16)
                    n = pairs(sp)

                    with sp.Fori(0, n) as i:
                        for b in range(2):
                            e = sp.value_load(table[0:1, bass.ds(2 * i + b, 1)], min_val=0, max_val=NE - 1)
                            one = lambda v: v[bass.ds(e, 1)].rearrange("a p k n -> (a p) k n")
                            sp.wait_ge(gmm, 2 * i + 1)
                            sp.dma_start(gu[:, b, 0], one(wg_v)).then_inc(gu_in[b], 16)
                            sp.dma_start(gu[:, b, 1], one(wu_v)).then_inc(gu_in[b], 16)
                            sp.wait_ge(dmm, 2 * i + 1)
                            sp.dma_start(dn[:, b], one(wd_v)).then_inc(dn_in[b], 16)

                @block.gpsimd
                def _(pool):
                    n = pairs(pool)
                    with pool.Fori(0, n) as i:
                        for b in range(2):
                            pool.wait_ge(xt_s, 2 * (2 * i) + 1)
                            pool.dma_start(idx[:, b:b + 1], slot_dram[bass.ds((2 * i + b) * P, P), :])\
                                .then_inc(idx_in[b], 16)
                            pool.wait_ge(idx_in[b], i * 16 + 16)
                            pool.sem_inc(listed, 1)
                            pool.indirect_dma_start(
                                out=xg[:, b], out_offset=None, in_=h2_dram,
                                in_offset=bass.IndirectOffsetOnAxis(ap=idx[:, b:b + 1].bitcast(u32), axis=0))\
                                .then_inc(xg_in[b], 16)

                @block.tensor
                def _(pe):
                    n = pairs(pe)
                    for s_ in (gmm, dmm, xt_s, ht):
                        pe.sem_inc(s_, 1)
                    with pe.Fori(0, n) as i:
                        for b in range(2):
                            pe.wait_ge(xg_in[b], i * 16 + 16)
                            rows = xg[:, b].rearrange("p (q k) -> p k q", k=KD)
                            for g in range(2):
                                pe.wait_ge(xt_ev, 2 * (2 * i + b) + 1)
                                for j in range(4):
                                    m = nc.tensor.transpose(ps[:, g, j * P:(j + 1) * P], rows[:, 4 * g + j], C("ident"))
                                m.then_inc(xt_s, 1)
                        for b in range(2):
                            pe.wait_ge(xt_ev, 2 * (2 * i + b) + 3)
                            pe.wait_ge(gu_in[b], i * 32 + 32)
                            pe.wait_ge(hid_s, 2 * i + 1)
                            for k in range(KD):
                                m = nc.tensor.matmul(ps[:, 2 + b], xT[:, b, k], gu[:, b, :, k],
                                                     start=(k == 0), stop=(k == KD - 1))
                            m.then_inc(gmm, 1)
                        for b in range(2):
                            pe.wait_ge(hid_s, 2 * i + b + 2)
                            hrows = hid[:, b].rearrange("p (q k) -> p k q", k=2)
                            pe.wait_ge(ht_ev, 2 * i + b + 1)
                            for k in range(2):
                                m = nc.tensor.transpose(ps[:, 4, k * P:(k + 1) * P], hrows[:, k], C("ident"))
                            m.then_inc(ht, 1)
                            pe.wait_ge(ht_ev, 2 * i + b + 2)
                            pe.wait_ge(dn_in[b], i * 16 + 16)
                            pe.wait_ge(y_ev, 2 * i + b + 1)
                            for c_ in range(2):
                                for k in range(2):
                                    m = nc.tensor.matmul(ps[:, 6 + c_], hidT[:, b, k], dn[:, b, k, c_ * 512:(c_ + 1) * 512],
                                                         start=(k == 0), stop=(k == 1))
                            m.then_inc(dmm, 1)

                @block.scalar
                def _(act):
                    n = pairs(act)
                    for s_ in (xt_ev, ht_ev):
                        act.sem_inc(s_, 1)
                    for s_ in y_out:
                        act.sem_inc(s_, 16)
                    with act.Fori(0, n) as i:
                        for b in range(2):
                            for g in range(2):
                                act.wait_ge(xt_s, 2 * (2 * i + b) + g + 2)
                                act.wait_ge(gmm, 2 * i + 1)
                                nc.scalar.activation(xT[:, b, 4 * g:4 * g + 4].rearrange("p a n -> p (a n)"), ps[:, g],
                                                     ACT.Copy).then_inc(xt_ev, 1)
                        for b in range(2):
                            act.wait_ge(gmm, 2 * i + b + 2)
                            nc.scalar.activation(sg[:, b], ps[:, 2 + b, 0:FE], ACT.Sigmoid).then_inc(sg_s, 1)
                        for b in range(2):
                            act.wait_ge(ht, 2 * i + b + 2)
                            nc.scalar.activation(hidT[:, b].rearrange("p a n -> p (a n)"), ps[:, 4, 0:2 * P], ACT.Copy)\
                               .then_inc(ht_ev, 1)
                            act.wait_ge(y_ev, 2 * i + b + 2)
                            act.dma_start(y_dram[bass.ds((2 * i + b) * P, P), :], yo[:, b]).then_inc(y_out[b], 16)
                    for b in range(2):
                        act.wait_ge(y_out[b], n * 16 + 16)
                    act.sem_inc(stored, 1)

                @block.vector
                def _(dve):
                    n = pairs(dve)
                    for s_ in (hid_s, y_ev):
                        dve.sem_inc(s_, 1)
                    dve.wait_ge(gt_in, 16)
                    with dve.Fori(0, n) as i:
                        for b in range(2):
                            dve.wait_ge(sg_s, 2 * i + b + 1)
                            dve.wait_ge(ht, 2 * i + 1)
                            nc.vector.tensor_tensor(sg[:, b], sg[:, b], ps[:, 2 + b, 0:FE], ALU.mult).then_inc(hid_mid, 1)
                            dve.wait_ge(hid_mid, 2 * i + b + 1)
                            nc.vector.tensor_tensor(hid[:, b], sg[:, b], ps[:, 2 + b, FE:2 * FE], ALU.mult)\
                              .then_inc(hid_s, 1)
                        for b in range(2):
                            dve.wait_ge(dmm, 2 * i + b + 2)
                            dve.wait_ge(y_out[b], i * 16 + 16)
                            nc.vector.tensor_tensor(yo[:, b], ps[:, 6:8].rearrange("p a n -> p (a n)"), gt[:], ALU.mult)\
                              .then_inc(y_ev, 1)

        with phase() as st:
            rows = sb(st, "rows", [P, 2 * NT, D])
            acc, acc2, = sems(st, "acc", "acc2")
            o_out = sem(st, "o_out")
            out_v = out[0].rearrange("(t p) d -> t p d", p=P)
            with nc.Block() as block:
                @block.gpsimd
                def _(pool):
                    for t in range(NT):
                        for i in range(2):
                            pool.indirect_dma_start(
                                out=rows[:, 2 * t + i], out_offset=None, in_=y_dram,
                                in_offset=bass.IndirectOffsetOnAxis(ap=place[:, i, t:t + 1].bitcast(u32), axis=0))\
                                .then_inc(r_in[2 * t + i], 16)

                @block.vector
                def _(dve):
                    for t in range(NT):
                        for i in range(2):
                            dve.wait_ge(r_in[2 * t + i], 16)
                            if i:
                                dve.wait_ge(acc, 2 * t + 1)
                            nc.vector.scalar_tensor_tensor(x1[:, t], rows[:, 2 * t + i], top[:, i, t:t + 1], x1[:, t],
                                                           ALU.mult, ALU.add).then_inc(acc, 1)

                @block.sync
                def _(sp):
                    for t in range(NT):
                        sp.wait_ge(acc, 2 * t + 2)
                        sp.dma_start(out_v[t], x1[:, t]).then_inc(o_out, 16)
                    sp.wait_ge(o_out, 16 * NT)


def dump(nc, ctx, debug, ap):
    with nc.semaphore("dbg") as s, nc.Block() as block:
        @block.sync
        def _(sp):
            sp.dma_start(debug, ap).then_inc(s, 16)
            sp.wait_ge(s, 16)


OUT_SHAPE = (1, SEQ, D)


def kernel(**inputs):
    import concourse.bacc as bacc
    from concourse.bass_utils import run_bass_kernel_spmd

    arrays = lay_out(inputs)
    nc = bacc.Bacc("TRN2", target_bir_lowering=False, num_devices=1)
    args = {n: nc.dram_tensor(n, a.shape, mybir.dt.from_np(a.dtype), kind="ExternalInput").ap()
            for n, a in arrays.items()}
    out = nc.dram_tensor("out", OUT_SHAPE, f32, kind="ExternalOutput").ap()
    build(nc, **args, out=out)
    r = run_bass_kernel_spmd(nc, [arrays], core_ids=[0])
    return r.results[0]["out"]
```

```python
import math
from contextlib import ExitStack, contextmanager

import numpy as np

import concourse.bass as bass
from concourse import mybir

P = 128
D = 1024
SEQ = 1024
KD = D // P
NT = SEQ // P
EPS = 1e-6
HEADS = 8
N = 64
D_RWKV = HEADS * N
CT = D_RWKV // P
RWKV_COLS = 3 * D_RWKV + 64 + 64 + 128
RT = RWKV_COLS // P
LN_EPS = 64e-5
Q_LORA, KV_LORA, ROPE = 256, 128, 32
MLA_COLS = Q_LORA + KV_LORA + ROPE
QKD = 96
GATE0 = RWKV_COLS + MLA_COLS
NE, NG, EPG, FE = 32, 4, 8, 256
B = 3
NW = 3
NBLK = 48
SURE = 2 * SEQ // P
CHUNK = 64
LEVELS = [2, 4, 8, 16, 32]
DECAY = -math.exp(-0.5)
HALF = SEQ // 2

f32r = mybir.dt.float32r
f32 = mybir.dt.float32
i32 = mybir.dt.int32
u32 = mybir.dt.uint32
ALU = mybir.AluOpType
ACT = mybir.ActivationFunctionType
AX = mybir.AxisListType

CONST = {}
_at = 0
for _name, _w in (("ident", P), ("mask4", 4 * P), ("up1", P), ("offt", len(LEVELS) * P), ("causal", P),
                  ("heads", P), ("before", P), ("ones", P), ("keep", P), ("freq", 16), ("iota", NBLK + 1),
                  ("thr", 8), ("id64", N)):
    CONST[_name] = (_at, _at + _w)
    _at += _w
NCONST = _at


def const_table():
    c = np.zeros((P, NCONST), np.float32)
    s, t = np.arange(P)[:, None], np.arange(P)[None, :]
    same = s // CHUNK == t // CHUNK

    def put(name, v):
        a, b = CONST[name]
        c[:, a:b] = v
    put("ident", s == t)
    before, upto = (s < t) & same, (s <= t) & same
    put("mask4", np.concatenate([before, upto, before, upto], 1))
    put("up1", (s // 2 == t // 2) & (s < t))
    put("offt", np.concatenate([(s // (2 * b) == t // (2 * b)) & (s // b < t // b) for b in LEVELS], 1))
    put("causal", np.where(t <= s, 0.0, -1e30))
    put("heads", s // N == t // N)
    put("before", s < t)
    put("ones", 1.0)
    put("keep", np.broadcast_to(t % CHUNK != 0, (P, P)))
    put("freq", (10000.0 ** (-(np.arange(0, ROPE, 2) / ROPE)))[None, :])
    put("iota", np.arange(NBLK + 1)[None, :])
    put("id64", s % N == t[:, :N])
    put("thr", (np.arange(8) * P)[None, :])
    return c


PCOL = {}
_at = 0
for _name, _w in (("mu", RT), ("w0", CT), ("a0", CT), ("k_k", CT), ("k_a", CT), ("r_k", CT), ("ln_w", CT), ("ln_b", CT)):
    PCOL[_name] = (_at, _at + _w)
    _at += _w
NPCOL = _at


def lay_out(inputs):
    a = {n: np.asarray(v) for n, v in inputs.items()}
    o = dict(a)
    cols = [a[n].reshape(-1, P).T for n in
            ("mu_shift", "w0", "a0", "k_k", "k_a", "r_k", "ln_x_w", "ln_x_b")]
    o["pcol"] = np.concatenate(cols, 1)
    w = a["w_in"][0].reshape(KD, P, -1)
    tiles = lambda v: v.reshape(KD, P, -1, P).transpose(2, 1, 0, 3)
    o["w_rwkv"] = tiles(w[:, :, :RWKV_COLS])
    o["w_mla"] = w[:, :, RWKV_COLS:GATE0].transpose(1, 0, 2)
    o["w_gates"] = tiles(w[:, :, GATE0:])
    o["w_br"] = a["w_branch"][0].reshape(2, CT, P, KD, P).transpose(3, 2, 0, 1, 4)
    o["pos"] = a["positions"].reshape(NT, P).T
    o["w_router"] = np.concatenate([a["w_router_group"][0], a["w_router_expert"][0]], 1)\
        .reshape(KD, P, NG + NE).transpose(1, 0, 2)
    o["b_router"] = np.concatenate([a["b_router_group"], a["b_router_expert"]], 1)
    o["qk_gain"] = np.concatenate([a["q_norm"], a["k_norm"]], 1)
    o["consts"], o["tokens"] = const_table(), token_table()
    for n in ("w_in", "mu_shift", "w0", "a0", "k_k", "k_a", "r_k", "ln_x_w", "ln_x_b", "w_branch", "positions",
              "w_router_group", "w_router_expert", "b_router_group", "b_router_expert", "q_norm", "k_norm"):
        del o[n]
    return {n: np.ascontiguousarray(v) for n, v in o.items()}


def token_table():
    return (np.arange(NT)[None, :] * P + np.arange(P)[:, None]).astype(np.int32)


def two_pi_parts():
    rest, parts = 2 * math.pi, []
    for _ in range(3):
        e = math.floor(math.log2(rest)) - 5
        p = math.floor(rest / 2.0 ** e) * 2.0 ** e
        parts.append(p)
        rest -= p
    return parts + [rest]


class Chain:

    def __init__(self, eng, sem, base=0, credit=0):
        self.eng, self.sem, self.base, self.n = eng, sem, base, credit

    def __call__(self, ins):
        self.n += 1
        ins.then_inc(self.sem, 1)
        self.eng.wait_ge(self.sem, self.base + self.n)


def build(nc, x, c, w_ada, b_ada, g_norm_mix, g_norm_ffn, w_decay_up, w_a_up, w_g_up, g_q_a, w_uq, g_kv_a,
          w_ukv, w_out, w_e_gate, w_e_up, w_e_down, pcol, w_rwkv, w_mla, w_gates, w_br, pos, w_router, b_router,
          qk_gain, consts, tokens, out, last_phase=99, debug=None):
    h_dram = nc.dram_tensor("h_spill", (P, KD * SEQ), f32, kind="Internal").ap()
    mod_dram = nc.dram_tensor("mod_rows", (1, 6 * D), f32, kind="Internal").ap()
    zm_dram = nc.dram_tensor("mla_rows", (P, NT * MLA_COLS), f32, kind="Internal").ap()
    yr_dram = nc.dram_tensor("rwkv_rows", (P, CT * SEQ), f32, kind="Internal").ap()
    x1_dram = nc.dram_tensor("x1_rows", (P, NT * D), f32, kind="Internal").ap()
    h2_dram = nc.dram_tensor("h2_rows", (SEQ, D), f32, kind="Internal").ap()
    slot_dram = nc.dram_tensor("slot_token", ((NBLK + 1) * P, 1), i32, kind="Internal").ap()
    y_dram = nc.dram_tensor("expert_rows", (NBLK * P, D), f32, kind="Internal").ap()
    ctx = ExitStack()
    with ctx:
        def sb(st, name, shape, dt=f32):
            return st.enter_context(nc.sbuf_tensor(name, shape, dt))

        taken = []
        scattered = ctx.enter_context(nc.semaphore("scattered"))
        idx_in = [ctx.enter_context(nc.semaphore(f"idx_in{i}")) for i in range(B)]
        xg_in = [ctx.enter_context(nc.semaphore(f"xg_in{i}")) for i in range(B)]
        r_in = [ctx.enter_context(nc.semaphore(f"r_in{i}")) for i in range(2 * NT)]

        def alias(name, shape):
            with ExitStack() as st:
                return sb(st, name, shape, f32r)

        def sem(st, name):
            taken.append(st.enter_context(nc.semaphore(name)))
            return taken[-1]

        def sems(st, *names):
            return [sem(st, n) for n in names]

        def slots(st, name, n):
            return [sem(st, f"{name}{i}") for i in range(n)]

        @contextmanager
        def phase():
            with ExitStack() as st:
                yield st
                with nc.Block() as block:
                    @block.gpsimd
                    def _(pool):
                        for s_ in taken:
                            pool.sem_clear(s_)
                taken.clear()

        ps = ctx.enter_context(nc.psum_tensor("ps", [P, 8, 512], f32))
        cst = sb(ctx, "cst", [P, NCONST])
        pc = sb(ctx, "pc", [P, NPCOL])
        top = sb(ctx, "top", [P, 2, NT])
        place = sb(ctx, "place", [P, 2, NT], i32)
        table = sb(ctx, "table", [1, NBLK + 2], i32)
        v_lo7 = alias("v_lo7", [P, CT, SEQ])
        YTM = sb(ctx, "YTM", [P, CT, SEQ])
        csig = sb(ctx, "csig", [P, KD])
        zst = ctx.enter_context(ExitStack())
        zT = sb(zst, "zT", [P, RT, SEQ + 1])
        mst = ctx.enter_context(ExitStack())
        mod = sb(mst, "mod", [P, 2 * D])

        def C(name):
            a, b = CONST[name]
            return cst[:, a:b]

        def PC(name, i=None):
            a, b = PCOL[name]
            return pc[:, a:b] if i is None else pc[:, a + i:a + i + 1]

        SH_M, SC_M = mod[:, 0:D], mod[:, D:2 * D]

        CH = 2 * D // 512
        w_ada_v = w_ada[0].rearrange("(p k) n -> p k n", k=KD)

        class Rows:

            def __init__(self, st, col, bank):
                self.col, self.bank = col, bank
                self.crep = sb(st, f"crep{col}", [P, KD, P])
                self.wbuf = sb(st, f"wada{col}", [P, NW, KD, 512])
                self.row = sb(st, f"arow{col}", [1, 2 * D])
                self.b_in, self.rep_s, self.mm, self.done, self.out = sems(
                    st, f"ab_in{col}", f"arep{col}", f"amm{col}", f"adone{col}", f"aout{col}")
                self.w_in = slots(st, f"aw_in{col}", NW)

            def load(self, sp):
                sp.dma_start(self.row[:], b_ada[:, self.col:self.col + 2 * D]).then_inc(self.b_in, 16)
                for j in range(CH):
                    if j >= NW:
                        sp.wait_ge(self.mm, j - NW + 1)
                    cols = slice(self.col + j * 512, self.col + (j + 1) * 512)
                    sp.dma_start(self.wbuf[:, j % NW], w_ada_v[:, :, cols]).then_inc(self.w_in[j % NW], 16)

            def replicate(self, eng):
                eng.tensor_copy(self.crep[:], csig[:].unsqueeze(2).broadcast_to([P, KD, P])).then_inc(self.rep_s, 1)

            def products(self, pe, a, b):
                for n in range(a, b):
                    j, k = divmod(n, KD)
                    if n == 0:
                        pe.wait_ge(self.rep_s, 1)
                    if k == 0:
                        pe.wait_ge(self.w_in[j % NW], 16 * (j // NW + 1))
                    m = nc.tensor.matmul(ps[:, self.bank + j], self.crep[:, k], self.wbuf[:, j % NW, k],
                                         start=(k == 0), stop=(k == KD - 1))
                    if k == KD - 1:
                        m.then_inc(self.mm, 1)

            def add_bias(self, dve, loads):
                dve.wait_ge(self.b_in, 16 * loads)
                dve.wait_ge(self.mm, CH)
                got = ps[0:1, self.bank:self.bank + CH].rearrange("p a n -> p (a n)")
                nc.vector.tensor_tensor(self.row[:], self.row[:], got, ALU.add).then_inc(self.done, 1)

            def store(self, sp, count):
                sp.wait_ge(self.done, count)
                sp.dma_start(mod_dram[:, self.col:self.col + 2 * D], self.row[:]).then_inc(self.out, 16)
                sp.wait_ge(self.out, 16)

        with phase() as st:
            ccol = sb(st, "ccol", [P, KD])
            crep = sb(st, "crep", [P, KD, P])
            brow = sb(st, "brow", [P, 2 * D])
            gmix = sb(st, "gmix", [P, D])
            wbuf = sb(st, "wbuf", [P, CH, KD, 512])
            const_in, c_in, b_in, c_sig, c_rep, mod_mm, mod_ev, dch = sems(
                st, "const_in", "c_in", "b_in", "c_sig", "c_rep", "mod_mm", "mod_ev", "dch0")
            w_in_s = slots(st, "wada", CH)
            with nc.Block() as block:
                @block.sync
                def _(sp):
                    sp.dma_start(ccol[:], c[0].rearrange("(p k) -> p k", k=KD)).then_inc(c_in, 16)
                    for b in range(CH):
                        sp.dma_start(wbuf[:, b], w_ada_v[:, :, b * 512:(b + 1) * 512]).then_inc(w_in_s[b], 16)
                    for dst, src in ((brow, b_ada[:, 0:2 * D]), (gmix, g_norm_mix)):
                        sp.dma_start(dst[:], src.broadcast_to(list(dst.shape))).then_inc(b_in, 16)
                    sp.dma_start(cst[:], consts).then_inc(const_in, 16)
                    sp.dma_start(pc[:], pcol).then_inc(const_in, 16)
                    sp.wait_ge(const_in, 32)

                @block.scalar
                def _(act):
                    act.wait_ge(c_in, 16)
                    nc.scalar.activation(csig[:], ccol[:], ACT.Sigmoid).then_inc(c_sig, 1)

                @block.vector
                def _(dve):
                    link = Chain(dve, dch)
                    dve.wait_ge(c_sig, 1)
                    link(nc.vector.tensor_tensor(csig[:], csig[:], ccol[:], ALU.mult))
                    nc.vector.tensor_copy(crep[:], csig[:].unsqueeze(2).broadcast_to([P, KD, P])).then_inc(c_rep, 1)
                    dve.wait_ge(b_in, 32)
                    for b in range(CH):
                        dve.wait_ge(mod_mm, b + 1)
                        cols = slice(b * 512, (b + 1) * 512)
                        nc.vector.tensor_tensor(mod[:, cols], ps[:, b], brow[:, cols], ALU.add).then_inc(mod_ev, 1)
                    dve.wait_ge(mod_ev, CH)
                    nc.vector.scalar_tensor_tensor(SC_M, SC_M, 1.0, gmix[:], ALU.add, ALU.mult).then_inc(dch, 1)

                @block.tensor
                def _(pe):
                    pe.wait_ge(c_rep, 1)
                    for b in range(CH):
                        pe.wait_ge(w_in_s[b], 16)
                        for k in range(KD):
                            m = nc.tensor.matmul(ps[:, b], crep[:, k], wbuf[:, b, k],
                                                 start=(k == 0), stop=(k == KD - 1))
                        m.then_inc(mod_mm, 1)
        if debug is not None and last_phase == 0:
            return dump(nc, ctx, debug, mod[:])

        with phase() as st:
            hT = sb(st, "hT", [P, KD, SEQ])
            zm = sb(st, "zm", [P, NT, MLA_COLS])
            xt = sb(st, "xt", [P, 4, D])
            hb, junk = YTM[:, 0:2], YTM[:, 2]
            ss = sb(st, "ss", [P, NT])
            rs = sb(st, "rs", [P, NT])
            wr = sb(st, "wr", [P, 2, KD, P])
            wm = sb(st, "wm", [P, KD, MLA_COLS])
            tmp = sb(st, "tmp", [P, 2, SEQ])
            x_in = slots(st, "x_in", 4)
            wr_in = slots(st, "wr_in", 2)
            wm_in, ssq, root, rstd, h_ready, tr, tr_ev, z_mm, z_ev, z_done, dif, mla_mm, mla_ev, dch, \
                h_out, zero = sems(
                    st, "wm_in", "ssq", "root", "rstd", "h_ready", "tr", "tr_ev", "z_mm", "z_ev", "z_done",
                    "dif", "mla_mm", "mla_ev", "dch1", "h_out", "zero")
            x_v = x[0].rearrange("(t p) d -> t p d", p=P)
            with nc.Block() as block:
                @block.sync
                def _(sp):
                    for t in range(NT):
                        if t >= 4:
                            sp.wait_ge(h_ready, t - 3)
                        sp.dma_start(xt[:, t % 4], x_v[t]).then_inc(x_in[t % 4], 16)
                        if t == 3:
                            sp.dma_start(wm[:], w_mla).then_inc(wm_in, 16)
                            for b in range(2):
                                sp.dma_start(wr[:, b], w_rwkv[b]).then_inc(wr_in[b], 16)
                    sp.wait_ge(tr_ev, 2 * NT)
                    sp.dma_start(h_dram, hT[:].rearrange("p k s -> p (k s)")).then_inc(h_out, 16)
                    with sp.Fori(0, RT // 2 - 1) as i:
                        for b in range(2):
                            sp.wait_ge(z_mm, 2 * i + b + 1)
                            sp.dma_start(wr[:, b], w_rwkv[bass.ds(2 * i + 2 + b, 1)].rearrange("a p k n -> (a p) k n"))\
                              .then_inc(wr_in[b], 16)
                    sp.wait_ge(mla_ev, NT)
                    sp.dma_start(zm_dram, zm[:].rearrange("p t n -> p (t n)")).then_inc(h_out, 16)
                    sp.wait_ge(h_out, 32)

                @block.scalar
                def _(act):
                    for t in range(4):
                        act.wait_ge(x_in[t], 16)
                        if t:
                            act.wait_ge(ssq, t)
                        nc.scalar.activation(junk, xt[:, t], ACT.Square, accum_out=ss[:, t:t + 1]).then_inc(ssq, 1)
                    act.wait_ge(rstd, 1)
                    nc.scalar.activation(rs[:, 0:4], rs[:, 0:4], ACT.Sqrt).then_inc(root, 1)
                    for t in range(NT):
                        for g in range(2):
                            act.wait_ge(tr, 2 * t + g + 1)
                            nc.scalar.activation(hT[:, 4 * g:4 * g + 4, t * P:(t + 1) * P],
                                                 ps[:, 2 * (t % 2) + g].rearrange("p (a b) -> p a b", a=4),
                                                 ACT.Copy).then_inc(tr_ev, 1)
                        if t < 4:
                            act.wait_ge(x_in[t], 32)
                            act.wait_ge(ssq, t + 4)
                            nc.scalar.activation(junk, xt[:, t], ACT.Square, accum_out=ss[:, t + 4:t + 5])\
                               .then_inc(ssq, 1)
                        if t == 3:
                            act.wait_ge(rstd, 3)
                            nc.scalar.activation(rs[:, 4:8], rs[:, 4:8], ACT.Sqrt).then_inc(root, 1)
                    for t in range(NT):
                        act.wait_ge(mla_mm, t + 1)
                        nc.scalar.activation(zm[:, t], ps[:, t % 2, 0:MLA_COLS], ACT.Copy).then_inc(mla_ev, 1)
                    with act.Fori(0, RT // 2) as i:
                        for b in range(2):
                            act.wait_ge(z_mm, 2 * i + b + 1)
                            nc.scalar.activation(zT[:, bass.ds(2 * i + b, 1), 1:SEQ + 1],
                                                 ps[:, 4 + 2 * b:6 + 2 * b].rearrange("p a n -> p (a n)").unsqueeze(1),
                                                 ACT.Copy).then_inc(z_ev, 1)

                @block.vector
                def _(dve):
                    link = Chain(dve, dch)
                    nc.vector.memset(zT[:, :, 0:1], 0.0).then_inc(zero, 1)
                    for half in range(2):
                        cols = slice(4 * half, 4 * half + 4)
                        dve.wait_ge(ssq, 4 * half + 4)
                        nc.vector.tensor_scalar(rs[:, cols], ss[:, cols], 1.0 / D, EPS, ALU.mult, ALU.add)\
                          .then_inc(rstd, 1)
                        dve.wait_ge(root, half + 1)
                        nc.vector.reciprocal(rs[:, cols], rs[:, cols]).then_inc(rstd, 1)
                        dve.wait_ge(rstd, 2 * half + 2)
                        for t in range(4 * half, 4 * half + 4):
                            if t >= 2:
                                dve.wait_ge(tr, 2 * t - 2)
                            link(nc.vector.scalar_tensor_tensor(hb[:, t % 2], xt[:, t % 4], rs[:, t:t + 1], SC_M,
                                                                ALU.mult, ALU.mult))
                            nc.vector.tensor_tensor(hb[:, t % 2], hb[:, t % 2], SH_M, ALU.add).then_inc(h_ready, 1)
                    dve.wait_ge(zero, 1)
                    with dve.Fori(0, RT // 2) as i:
                        for b in range(2):
                            dve.wait_ge(z_ev, 2 * i + b + 1)
                            zt = zT[:, bass.ds(2 * i + b, 1), :].rearrange("p a n -> p (a n)")
                            nc.vector.tensor_tensor(tmp[:, b], zt[:, 0:SEQ], zt[:, 1:SEQ + 1], ALU.subtract)\
                              .then_inc(dif, 1)
                            dve.wait_ge(dif, 2 * i + b + 1)
                            nc.vector.scalar_tensor_tensor(zt[:, 1:SEQ + 1], tmp[:, b], pc[:, bass.ds(2 * i + (b + PCOL["mu"][0]), 1)],
                                                           zt[:, 1:SEQ + 1], ALU.mult, ALU.add).then_inc(z_done, 1)

                @block.tensor
                def _(pe):
                    for t in range(NT):
                        pe.wait_ge(h_ready, t + 1)
                        if t >= 2:
                            pe.wait_ge(tr_ev, 2 * t - 2)
                        for g in range(2):
                            for j in range(4):
                                k = 4 * g + j
                                m = nc.tensor.transpose(ps[:, 2 * (t % 2) + g, j * P:(j + 1) * P],
                                                        hb[:, t % 2, k * P:(k + 1) * P], C("ident"))
                            m.then_inc(tr, 1)
                    pe.wait_ge(tr_ev, 2 * NT)
                    pe.wait_ge(wm_in, 16)
                    for t in range(NT):
                        if t >= 2:
                            pe.wait_ge(mla_ev, t - 1)
                        for k in range(KD):
                            m = nc.tensor.matmul(ps[:, t % 2, 0:MLA_COLS], hT[:, k, t * P:(t + 1) * P], wm[:, k],
                                                 start=(k == 0), stop=(k == KD - 1))
                        m.then_inc(mla_mm, 1)

                    def column_tile(b):
                        for n in range(2):
                            for k in range(KD):
                                m = nc.tensor.matmul(ps[:, 4 + 2 * b + n], wr[:, b, k], hT[:, k, n * 512:(n + 1) * 512],
                                                     start=(k == 0), stop=(k == KD - 1))
                        m.then_inc(z_mm, 1)
                    for b in range(2):
                        pe.wait_ge(wr_in[b], 16)
                        column_tile(b)
                    with pe.Fori(1, RT // 2) as i:
                        for b in range(2):
                            pe.wait_ge(wr_in[b], i * 16 + 16)
                            pe.wait_ge(z_ev, 2 * i + b - 1)
                            column_tile(b)
        if debug is not None and last_phase == 1:
            return dump(nc, ctx, debug, zT[:].rearrange("p a b -> p (a b)"))

        mst.close()

        R0, K0, V0, WA, GL = 0, CT, 2 * CT, 3 * CT, 3 * CT + 1
        kst = ctx.enter_context(ExitStack())
        kk = sb(kst, "kk", [P, CT, SEQ])
        aa = sb(kst, "aa", [P, CT, SEQ])
        lw = sb(kst, "lw", [P, CT, SEQ])

        def Z(i):
            return zT[:, i, 1:SEQ + 1]

        with phase() as st:
            wup = sb(st, "wup", [P, D_RWKV])
            sq = sb(st, "sq", [P, 2, SEQ])
            norm = YTM
            one_ka = sb(st, "one_ka", [P, CT])
            rows2 = Rows(st, 2 * D, 0)
            up_in, low, up_mm, dec, a_done, kraw, sq_done, ss_mm, nr_ev, dch, kdone, pch = sems(
                st, "up_in", "low", "up_mm", "dec", "a_done", "kraw", "sq_done", "ss_mm", "nr_ev", "dch2",
                "kdone", "pch2")
            with nc.Block() as block:
                @block.sync
                def _(sp):
                    sp.dma_start(wup[0:64], w_decay_up[0]).then_inc(up_in, 16)
                    sp.dma_start(wup[64:128], w_a_up[0]).then_inc(up_in, 16)
                    rows2.load(sp)
                    rows2.store(sp, 1)
                    sp.wait_ge(up_in, 32)

                @block.gpsimd
                def _(pool):
                    rows2.replicate(nc.gpsimd)
                    for c_ in range(CT):
                        pool.wait_ge(kraw, c_ + 1)
                        if c_ >= 2:
                            pool.wait_ge(ss_mm, c_ - 1)
                        nc.gpsimd.tensor_tensor(sq[:, c_ % 2], kk[:, c_], kk[:, c_], ALU.mult).then_inc(sq_done, 1)

                @block.scalar
                def _(act):
                    nc.scalar.activation(Z(WA)[0:64], Z(WA)[0:64], ACT.Tanh).then_inc(low, 1)
                    nc.scalar.activation(Z(GL), Z(GL), ACT.Sigmoid).then_inc(low, 1)
                    for c_ in range(CT):
                        act.wait_ge(up_mm, 2 * c_ + 1)
                        nc.scalar.activation(lw[:, c_], ps[:, 0:2].rearrange("p a n -> p (a n)"), ACT.Sigmoid,
                                             bias=PC("w0", c_)).then_inc(dec, 1)
                        act.wait_ge(up_mm, 2 * c_ + 2)
                        nc.scalar.activation(aa[:, c_], ps[:, 2:4].rearrange("p a n -> p (a n)"), ACT.Sigmoid,
                                             bias=PC("a0", c_)).then_inc(a_done, 1)
                    for c_ in range(CT):
                        act.wait_ge(ss_mm, c_ + 1)
                        nc.scalar.activation(norm[:, c_], ps[:, 6:8].rearrange("p a n -> p (a n)"), ACT.Sqrt)\
                           .then_inc(nr_ev, 1)

                @block.vector
                def _(dve):
                    link = Chain(dve, dch)
                    for c_ in range(CT):
                        nc.vector.tensor_scalar(kk[:, c_], Z(K0 + c_), PC("k_k", c_), None, ALU.mult).then_inc(kraw, 1)
                    link(nc.vector.tensor_scalar(one_ka[:], PC("k_a"), -1.0, 1.0, ALU.mult, ALU.add))
                    for c_ in range(CT):
                        dve.wait_ge(dec, c_ + 1)
                        nc.vector.tensor_scalar(lw[:, c_], lw[:, c_], DECAY, None, ALU.mult)
                        dve.wait_ge(a_done, c_ + 1)
                        buf = norm[:, c_]
                        link(nc.vector.tensor_scalar(buf, aa[:, c_], PC("k_a", c_), one_ka[:, c_:c_ + 1],
                                                     ALU.mult, ALU.add))
                        nc.vector.tensor_tensor(Z(K0 + c_), Z(K0 + c_), buf, ALU.mult).then_inc(kdone, 1)
                    for c_ in range(CT):
                        dve.wait_ge(nr_ev, c_ + 1)
                        link(nc.vector.tensor_scalar(norm[:, c_], norm[:, c_], 1e-12, None, ALU.max))
                        link(nc.vector.reciprocal(norm[:, c_], norm[:, c_]))
                        link(nc.vector.tensor_tensor(kk[:, c_], kk[:, c_], norm[:, c_], ALU.mult))
                        nc.vector.tensor_tensor(aa[:, c_], aa[:, c_], kk[:, c_], ALU.mult)
                    rows2.add_bias(dve, 1)

                @block.tensor
                def _(pe):
                    pe.wait_ge(up_in, 32)
                    pe.wait_ge(low, 2)
                    for c_ in range(CT):
                        for j, (w, src, done) in enumerate(((wup[0:64], Z(WA)[0:64], dec),
                                                            (wup[64:128], Z(WA)[64:128], a_done))):
                            if c_:
                                pe.wait_ge(done, c_)
                            for n in range(2):
                                m = nc.tensor.matmul(ps[:, 2 * j + n], w[:, c_ * P:(c_ + 1) * P],
                                                     src[:, n * 512:(n + 1) * 512], start=True, stop=True)
                            m.then_inc(up_mm, 1)
                    for c_ in range(CT):
                        pe.wait_ge(sq_done, c_ + 1)
                        if c_:
                            pe.wait_ge(nr_ev, c_)
                        elif CT:
                            pe.wait_ge(kdone, CT)
                        for n in range(2):
                            m = nc.tensor.matmul(ps[:, 6 + n], C("heads"), sq[:, c_ % 2, n * 512:(n + 1) * 512],
                                                 start=True, stop=True)
                        m.then_inc(ss_mm, 1)
                    pe.wait_ge(dec, CT)
                    pe.wait_ge(a_done, CT)
                    rows2.products(pe, 0, CH * KD)
        if debug is not None and last_phase == 2:
            return dump(nc, ctx, debug, kk[:].rearrange("p a b -> p (a b)"))

        yrow = YTM[:].rearrange("p c (t n) -> p (c t) n", n=D_RWKV)
        with phase() as st:
            cum = sb(st, "cum", [P, CT, P])
            ex = sb(st, "ex", [P, 4, CT, P])
            nr = sb(st, "nr", [P, CT, 2, P])
            bd = sb(st, "bd", [P, CT, P])
            kd = sb(st, "kd", [P, CT, P])
            ce = sb(st, "ce", [P, 2, CT, P])
            tok = sb(st, "tok", [P, 3, CT, P])
            nb = sb(st, "nb", [P, HEADS, 2, N])
            mats = sb(st, "mats", [P, HEADS, 4, P])
            off = sb(st, "off", [P, 2, 4, P])
            xx = ce[:].rearrange("p a c n -> p (a c) n")
            tt = sb(st, "tt", [P, HEADS, 2, P])
            wu = sb(st, "wu", [P, HEADS, 2, N])
            pt = sb(st, "pt", [P, CT, P])
            mt = sb(st, "mt", [P, 2, CT, P])
            rk = pt
            S = sb(st, "S", [P, 2, CT, P])
            headrk = zT[:, WA, 0:CT * P].rearrange("p (c n) -> p c n", c=CT)
            dg = zT[:, WA, 512:1024].rearrange("p (h c n) -> p h c n", c=CT, h=2)
            vst = sb(st, "vst", [P, CT, P])

            def tok_rows(i, h):
                return tok[:, i, h // 2, 64 * (h % 2):64 * (h % 2) + 64]

            def v_rows(h):
                return tok_rows(2, h)
            PER = dict(cum=4, pre=2, ex=3, vst=1, mul=4, pmul=3, tr=4, tok=1, nb=1, pair=8, pair_ev=8, t0=4, t0_mm=2,
                       t0_ev=2, off=10, x=10, x_ev=10, t=10, t_ev=10, bv=1, bv_ev=1, wu=2, wu_ev=2, pt=1, pt_ev=1,
                       mr=1, mt_ev=2, dg=2, st=2, st_ev=2, y=1, y_ev=1, bon=1, bon_ev=1)
            sm = {n: sem(st, "r_" + n) for n in PER}
            init = sem(st, "r_init")
            over = sem(st, "r_over")
            NL = len(LEVELS)
            assert PER["off"] == 2 * NL

            def head(h):
                return h // 2, slice(64 * (h % 2), 64 * (h % 2) + 64)

            def chunks(ap):
                return ap.rearrange("p c (h n) -> p (c h) n", n=CHUNK)

            XB, DB = (0, 3), (1, 4)
            with nc.Block() as block:
                @block.gpsimd
                def _(pool):
                    with pool.Fori(0, NT) as j:
                        def wait(name, n):
                            pool.wait_ge(sm[name], j * PER[name] + n)
                        seq = bass.ds(j * P, P)
                        zseq = bass.ds(j * P + 1, P)
                        pool.wait_ge(over, j + 1)
                        nc.gpsimd.tensor_copy(vst[:], zT[:, V0:V0 + CT, zseq]).then_inc(sm["vst"], 1)
                        nc.gpsimd.tensor_tensor(rk[:], zT[:, R0:R0 + CT, zseq], zT[:, K0:K0 + CT, zseq], ALU.mult)\
                          .then_inc(sm["pmul"], 1)
                        wait("ex", 1)
                        nc.gpsimd.tensor_tensor(ce[:, 0], aa[:, :, seq], ex[:, 3], ALU.mult).then_inc(sm["pmul"], 1)
                        nc.gpsimd.tensor_tensor(ce[:, 1], zT[:, K0:K0 + CT, zseq], ex[:, 3], ALU.mult)\
                          .then_inc(sm["pmul"], 1)
                        wait("ex", 2)
                        for ch in range(2):
                            end = ex[:, 0, :, (ch + 1) * CHUNK - 1:(ch + 1) * CHUNK]
                            nc.gpsimd.tensor_tensor(dg[:, ch], C("id64").unsqueeze(1).broadcast_to([P, CT, N]),
                                                    end.broadcast_to([P, CT, N]), ALU.mult).then_inc(sm["dg"], 1)
                        for g in range(2):
                            hs = slice(4 * g, 4 * g + 4)
                            wait("pair_ev", 4 * g + 4)
                            nc.gpsimd.tensor_tensor(tt[:, hs, 1], mats[:, hs, 0],
                                                    C("up1").unsqueeze(1).broadcast_to([P, 4, P]), ALU.mult)\
                              .then_inc(sm["t0"], 1)
                            wait("t0", 2 * g + 1)
                            nc.gpsimd.tensor_tensor(tt[:, hs, 1], tt[:, hs, 1],
                                                    C("ident").unsqueeze(1).broadcast_to([P, 4, P]), ALU.add)\
                              .then_inc(sm["t0"], 1)
                        for l in range(NL):
                            a = CONST["offt"][0] + l * P
                            for g in range(2):
                                if l:
                                    wait("x", 2 * (l - 1) + g + 1)
                                nc.gpsimd.tensor_tensor(off[:, g], mats[:, 4 * g:4 * g + 4, 0],
                                                        cst[:, a:a + P].unsqueeze(1).broadcast_to([P, 4, P]), ALU.mult)\
                                  .then_inc(sm["off"], 1)

                @block.scalar
                def _(act):
                    with act.Fori(0, NT) as j:
                        def wait(name, n):
                            act.wait_ge(sm[name], j * PER[name] + n)
                        wait("pre", 2)
                        nc.scalar.activation(ex[:, 2:4], ex[:, 2:4], ACT.Exp).then_inc(sm["ex"], 1)
                        nc.scalar.activation(ex[:, 0], cum[:], ACT.Exp).then_inc(sm["ex"], 1)
                        nc.scalar.activation(ex[:, 1], cum[:], ACT.Exp, scale=-1.0).then_inc(sm["ex"], 1)
                        wait("tr", 4)
                        nc.scalar.activation(tok[:].rearrange("p a c n -> p (a c n)"),
                                             ps[:, 1:4].rearrange("p a n -> p (a n)"), ACT.Copy).then_inc(sm["tok"], 1)
                        nc.scalar.activation(nb[:, :, 0], ps[:, 0].rearrange("p (h n) -> p h n", n=N), ACT.Copy)\
                           .then_inc(sm["nb"], 1)
                        wait("bv", 1)
                        nc.scalar.activation(nb[:, :, 1], ps[:, 6].rearrange("p (h n) -> p h n", n=N), ACT.Copy)\
                           .then_inc(sm["bv_ev"], 1)
                        for g in range(2):
                            wait("t0_mm", g + 1)
                            nc.scalar.activation(tt[:, 4 * g:4 * g + 4, 0],
                                                 ps[:, XB[g]].rearrange("p (h n) -> p h n", n=P), ACT.Copy)\
                               .then_inc(sm["t0_ev"], 1)
                        for l in range(NL):
                            for g in range(2):
                                wait("x", 2 * l + g + 1)
                                nc.scalar.activation(xx[:, 4 * g:4 * g + 4],
                                                     ps[:, XB[g]].rearrange("p (h n) -> p h n", n=P), ACT.Copy)\
                                   .then_inc(sm["x_ev"], 1)
                        for c_ in range(2):
                            wait("st", c_ + 1)
                            if c_ == 1:
                                wait("y", 1)
                            nc.scalar.activation(S[:, 1 - c_].rearrange("p c n -> p (c n)"), ps[:, 4 + c_], ACT.Copy).then_inc(sm["st_ev"], 1)

                @block.vector
                def _(dve):
                    nc.vector.memset(S[:], 0.0).then_inc(init, 1)
                    nc.vector.memset(mt[:], 0.0).then_inc(init, 1)
                    for c_ in range(CT):
                        nc.vector.tensor_scalar(headrk[:, c_], C("heads"), PC("r_k", c_), None, ALU.mult)\
                          .then_inc(init, 1)
                    with dve.Fori(0, NT) as j:
                        def wait(name, n):
                            dve.wait_ge(sm[name], j * PER[name] + n)
                        seq = bass.ds(j * P, P)
                        zseq = bass.ds(j * P + 1, P)
                        for c_ in range(CT):
                            nc.vector.tensor_tensor_scan(cum[:, c_], C("keep"),
                                                         lw[:, c_, seq], 0.0, ALU.mult, ALU.add)\
                              .then_inc(sm["cum"], 1)
                        wait("cum", CT)
                        nc.vector.tensor_tensor(ex[:, 2], cum[:], lw[:, :, seq], ALU.subtract).then_inc(sm["pre"], 1)
                        end = chunks(cum[:])[:, :, CHUNK - 1:CHUNK]
                        nc.vector.tensor_tensor(chunks(ex[:, 3]), end.broadcast_to([P, 2 * CT, CHUNK]),
                                                chunks(cum[:]), ALU.subtract).then_inc(sm["pre"], 1)
                        wait("ex", 1)
                        nc.vector.scalar_tensor_tensor(nr[:, :, 0], kk[:, :, seq], -1.0, ex[:, 2], ALU.mult, ALU.mult)\
                          .then_inc(sm["mul"], 1)
                        wait("ex", 2)
                        nc.vector.tensor_tensor(nr[:, :, 1], zT[:, R0:R0 + CT, zseq], ex[:, 0], ALU.mult)\
                          .then_inc(sm["mul"], 1)
                        wait("ex", 3)
                        nc.vector.tensor_tensor(bd[:], aa[:, :, seq], ex[:, 1], ALU.mult).then_inc(sm["mul"], 1)
                        nc.vector.tensor_tensor(kd[:], zT[:, K0:K0 + CT, zseq], ex[:, 1], ALU.mult)\
                          .then_inc(sm["mul"], 1)
                        for h in range(HEADS):
                            wait("pair", h + 1)
                            nc.vector.tensor_tensor(mats[:, h].rearrange("p a n -> p (a n)"), ps[:, 5 + h % 3],
                                                    C("mask4"), ALU.mult).then_inc(sm["pair_ev"], 1)
                        wait("bon", 1)
                        wait("vst", 1)
                        nc.vector.tensor_tensor(zT[:, V0:V0 + CT, zseq], vst[:],
                                                ps[:, 4].rearrange("p (c n) -> p c n", c=CT), ALU.mult)\
                          .then_inc(sm["bon_ev"], 1)
                        for l in range(NL):
                            for g in range(2):
                                wait("t", 2 * l + g + 1)
                                hs = slice(4 * g, 4 * g + 4)
                                nc.vector.tensor_tensor(tt[:, hs].rearrange("p h a n -> p (h a n)"),
                                                        tt[:, hs].rearrange("p h a n -> p (h a n)"),
                                                        ps[:, DB[g]:DB[g] + 2].rearrange("p a n -> p (a n)"), ALU.add)\
                                  .then_inc(sm["t_ev"], 1)
                        for g in range(2):
                            wait("wu", g + 1)
                            nc.vector.tensor_copy(wu[:, 4 * g:4 * g + 4].rearrange("p h a n -> p (h a n)"),
                                                  ps[:, XB[g]]).then_inc(sm["wu_ev"], 1)
                        wait("dg", 2)
                        wait("mr", 1)
                        for i in range(2):
                            half = slice(64 * i, 64 * i + 64)
                            for ch in range(2):
                                m = nc.vector.tensor_tensor(
                                    mt[half, ch, :, half],
                                    ps[half, 1 + ch].rearrange("p (c n) -> p c n", c=CT)[:, :, half],
                                    dg[half, ch], ALU.add)
                            m.then_inc(sm["mt_ev"], 1)
                        wait("pt", 1)
                        nc.vector.tensor_tensor(pt[:], ps[:, 7].rearrange("p (c n) -> p c n", c=CT), nr[:, :, 1],
                                                ALU.add).then_inc(sm["pt_ev"], 1)
                        wait("y", 1)
                        nc.vector.tensor_copy(yrow[:, bass.ds(j, 1)].rearrange("p a n -> p (a n)"), ps[:, 6])\
                          .then_inc(sm["y_ev"], 1)

                @block.tensor
                def _(pe):
                    pe.wait_ge(init, 2 + CT)
                    pe.sem_inc(over, 1)
                    with pe.Fori(0, NT) as j:
                        def wait(name, n):
                            pe.wait_ge(sm[name], j * PER[name] + n)

                        def four_transposes(bank, src):
                            for c_ in range(CT):
                                m = nc.tensor.transpose(ps[:, bank, c_ * P:(c_ + 1) * P], src[:, c_], C("ident"))
                            m.then_inc(sm["tr"], 1)
                        wait("vst", 1)
                        four_transposes(3, vst)
                        wait("pmul", 1)
                        for c_ in range(CT):
                            m = nc.tensor.matmul(ps[:, 4, c_ * P:(c_ + 1) * P], headrk[:, c_], rk[:, c_],
                                                 start=True, stop=True)
                        m.then_inc(sm["bon"], 1)
                        wait("mul", 1)
                        four_transposes(0, nr[:, :, 0])
                        wait("pmul", 3)
                        four_transposes(1, ce[:, 0])
                        four_transposes(2, ce[:, 1])
                        wait("mul", 4)
                        for h in range(HEADS):
                            c_, half = head(h)
                            if h >= 3:
                                wait("pair_ev", h - 2)
                            bank = ps[:, 5 + h % 3]
                            both = nr[half, c_].rearrange("p a n -> p (a n)")
                            nc.tensor.matmul(bank[:, 0:2 * P], bd[half, c_], both, start=True, stop=True)
                            nc.tensor.matmul(bank[:, 2 * P:4 * P], kd[half, c_], both, start=True, stop=True)\
                              .then_inc(sm["pair"], 1)
                        wait("tok", 1)
                        wait("pair_ev", HEADS)
                        for h in range(HEADS):
                            m = nc.tensor.matmul(ps[:, 6, h * N:(h + 1) * N], mats[:, h, 2], v_rows(h),
                                                 start=True, stop=True)
                        m.then_inc(sm["bv"], 1)
                        wait("nb", 1)
                        for g in range(2):
                            wait("t0", 2 * g + 2)
                            for h in range(4):
                                m = nc.tensor.transpose(ps[:, XB[g], h * P:(h + 1) * P], tt[:, 4 * g + h, 1],
                                                        C("ident"))
                            m.then_inc(sm["t0_mm"], 1)
                        wait("bon_ev", 1)
                        for l in range(NL):
                            for g in range(2):
                                if l == 0:
                                    wait("t0_ev", g + 1)
                                else:
                                    wait("t_ev", 2 * (l - 1) + g + 1)
                                wait("off", 2 * l + g + 1)
                                for h in range(4):
                                    m = nc.tensor.matmul(ps[:, XB[g], h * P:(h + 1) * P], off[:, g, h],
                                                         tt[:, 4 * g + h, 0], start=True, stop=True)
                                m.then_inc(sm["x"], 1)
                            for g in range(2):
                                wait("x_ev", 2 * l + g + 1)
                                for h in range(4):
                                    o = ps[:, DB[g] + h // 2, (h % 2) * 2 * P:(h % 2) * 2 * P + 2 * P]
                                    hh = 4 * g + h
                                    nc.tensor.matmul(o[:, 0:P], tt[:, hh, 1], xx[:, hh], start=True, stop=True)
                                    m = nc.tensor.matmul(o[:, P:2 * P], xx[:, hh], tt[:, hh, 1], start=True, stop=True)
                                m.then_inc(sm["t"], 1)
                        wait("bv_ev", 1)
                        for g in range(2):
                            wait("t_ev", 2 * (NL - 1) + g + 1)
                            for h in range(4):
                                m = nc.tensor.matmul(ps[:, XB[g], h * P:(h + 1) * P], tt[:, 4 * g + h, 1],
                                                     nb[:, 4 * g + h].rearrange("p a n -> p (a n)"),
                                                     start=True, stop=True)
                            m.then_inc(sm["wu"], 1)
                        wait("wu_ev", 2)
                        for h in range(HEADS):
                            o = ps[:, 6, h * N:(h + 1) * N]
                            nc.tensor.matmul(o, mats[:, h, 1], wu[:, h, 1], start=(h == 0), stop=False,
                                             skip_group_check=True)
                            nc.tensor.matmul(o, mats[:, h, 3], v_rows(h), start=False, stop=False,
                                             skip_group_check=True)
                        for ch in range(2):
                            rows = slice(64 * ch, 64 * ch + 64)
                            for h in range(HEADS):
                                c_, half = head(h)
                                at = slice(c_ * P + 64 * (h % 2), c_ * P + 64 * (h % 2) + 64)
                                nc.tensor.matmul(ps[half, 1 + ch, at], wu[rows, h, 0], tok_rows(0, h)[rows],
                                                 start=True, stop=True)
                                nc.tensor.matmul(ps[half, 4 + ch, at], tok_rows(0, h)[rows], wu[rows, h, 1],
                                                 start=(h < 2), stop=False, skip_group_check=True)
                                m = nc.tensor.matmul(ps[half, 4 + ch, at], tok_rows(1, h)[rows], v_rows(h)[rows],
                                                     start=False, stop=False, skip_group_check=True)
                        m.then_inc(sm["mr"], 1)
                        for h in range(HEADS):
                            c_, half = head(h)
                            m = nc.tensor.matmul(ps[half, 7, c_ * P:(c_ + 1) * P], wu[:, h, 0], mats[:, h, 1],
                                                 start=True, stop=True)
                        m.then_inc(sm["pt"], 1)
                        wait("mt_ev", 2)
                        pe.wait_ge(over, j + 1)
                        for ch in range(2):
                            if ch == 1:
                                wait("st_ev", 1)
                            for c_ in range(CT):
                                m = nc.tensor.matmul(ps[:, 4 + ch, c_ * P:(c_ + 1) * P], mt[:, ch, c_], S[:, ch, c_],
                                                     start=False, stop=(c_ == CT - 1), skip_group_check=True)
                            m.then_inc(sm["st"], 1)
                            if ch == 0:
                                wait("pt_ev", 1)
                            rows = slice(64 * ch, 64 * ch + 64)
                            for c_ in range(CT):
                                m = nc.tensor.matmul(ps[rows, 6, c_ * P:(c_ + 1) * P], pt[:, c_, rows], S[:, ch, c_],
                                                     start=False, stop=(c_ == CT - 1), skip_group_check=True)
                            if ch == 1:
                                m.then_inc(sm["y"], 1)
                        wait("y_ev", 1)
                        wait("st_ev", 2)
                        pe.sem_inc(over, 1)
        if debug is not None and last_phase == 3:
            return dump(nc, ctx, debug, YTM[:].rearrange("p a b -> p (a b)"))
        kst.close()

        with phase() as st:
            wg = sb(st, "wg", [P, D_RWKV])
            yc = sb(st, "yc", [P, NT, D_RWKV])
            sq = sb(st, "sq4", [P, 2, D_RWKV])
            mean = sb(st, "mean", [P, NT * HEADS])
            var = sb(st, "var", [P, NT * HEADS])
            part = sb(st, "part", [P, 2, CT, P])
            yT = sb(st, "yT", [P, CT, SEQ])
            gffn = sb(st, "gffn", [1, D])
            rows4 = Rows(st, 4 * D, 4)
            wg_in, cent, sq_s, var_s, root, yn, tr, gm, aff, fin, y_out, dch = sems(
                st, "wg_in", "cent", "sq_s", "var_s", "root4", "yn", "tr4", "gm4", "aff", "fin4", "y_out4", "dch4")

            def by_head(ap):
                return ap.rearrange("p (h n) -> p h n", n=N)
            with nc.Block() as block:
                @block.sync
                def _(sp):
                    sp.dma_start(wg[:], w_g_up[0]).then_inc(wg_in, 16)
                    sp.dma_start(gffn[:], g_norm_ffn).then_inc(rows4.b_in, 16)
                    rows4.load(sp)
                    rows4.store(sp, 2)
                    sp.wait_ge(fin, 2 * NT)
                    sp.dma_start(yr_dram, yT[:].rearrange("p c s -> p (c s)")).then_inc(y_out, 16)
                    sp.wait_ge(y_out, 16)

                @block.vector
                def _(dve):
                    link = Chain(dve, dch)
                    for t in range(NT):
                        hs = slice(t * HEADS, (t + 1) * HEADS)
                        link(nc.vector.tensor_reduce(mean[:, hs], by_head(yrow[:, t]), AX.X, ALU.add))
                        link(nc.vector.tensor_scalar(mean[:, hs], mean[:, hs], 1.0 / N, None, ALU.mult))
                        nc.vector.tensor_tensor(by_head(yc[:, t]), by_head(yrow[:, t]),
                                                mean[:, hs].unsqueeze(2).broadcast_to([P, HEADS, N]), ALU.subtract)\
                          .then_inc(cent, 1)
                        if t:
                            dve.wait_ge(sq_s, t)
                            nc.vector.tensor_reduce(var[:, (t - 1) * HEADS:t * HEADS], by_head(sq[:, (t - 1) % 2]),
                                                    AX.X, ALU.add).then_inc(var_s, 1)
                    dve.wait_ge(sq_s, NT)
                    nc.vector.tensor_reduce(var[:, (NT - 1) * HEADS:], by_head(sq[:, (NT - 1) % 2]),
                                            AX.X, ALU.add).then_inc(var_s, 1)
                    dve.wait_ge(var_s, NT)
                    nc.vector.tensor_scalar(var[:], var[:], 1.0 / N, LN_EPS, ALU.mult, ALU.add).then_inc(var_s, 1)
                    dve.wait_ge(root, 1)
                    link(nc.vector.reciprocal(var[:], var[:]))
                    for t in range(NT + 1):
                        if t < NT:
                            hs = slice(t * HEADS, (t + 1) * HEADS)
                            nc.vector.tensor_tensor(by_head(yc[:, t]), by_head(yc[:, t]),
                                                    var[:, hs].unsqueeze(2).broadcast_to([P, HEADS, N]), ALU.mult)\
                              .then_inc(yn, 1)
                        if t:
                            u = t - 1
                            dve.wait_ge(aff, CT * t)
                            pp = part[:, u % 2]
                            nc.vector.tensor_tensor(pp, pp, zT[:, V0:V0 + CT, 1 + u * P:1 + t * P],
                                                    ALU.add).then_inc(fin, 1)
                            dve.wait_ge(fin, 2 * u + 1)
                            dve.wait_ge(gm, t)
                            nc.vector.tensor_tensor(yT[:, :, u * P:t * P], pp,
                                                    ps[:, 2 + u % 2].rearrange("p (c n) -> p c n", c=CT), ALU.mult)\
                              .then_inc(fin, 1)
                    rows4.add_bias(dve, 2)
                    dve.wait_ge(rows4.done, 1)
                    nc.vector.scalar_tensor_tensor(rows4.row[:, 0:D], rows4.row[:, 0:D], 1.0, gffn[:], ALU.add, ALU.mult)\
                      .then_inc(rows4.done, 1)

                @block.gpsimd
                def _(pool):
                    rows4.replicate(nc.gpsimd)

                @block.scalar
                def _(act):
                    for t in range(NT):
                        act.wait_ge(cent, t + 1)
                        if t >= 2:
                            act.wait_ge(var_s, t - 1)
                        nc.scalar.activation(sq[:, t % 2], yc[:, t], ACT.Square).then_inc(sq_s, 1)
                    act.wait_ge(var_s, NT + 1)
                    nc.scalar.activation(var[:], var[:], ACT.Sqrt).then_inc(root, 1)
                    for t in range(NT):
                        act.wait_ge(tr, t + 1)
                        if t >= 2:
                            act.wait_ge(fin, 2 * (t - 1))
                        for c_ in range(CT):
                            nc.scalar.activation(part[:, t % 2, c_], ps[:, t % 2, c_ * P:(c_ + 1) * P], ACT.Identity,
                                                 scale=PC("ln_w", c_), bias=PC("ln_b", c_)).then_inc(aff, 1)

                @block.tensor
                def _(pe):
                    pe.wait_ge(wg_in, 16)
                    rows4.products(pe, 0, KD)
                    each = (CH - 1) * KD // NT
                    for t in range(NT):
                        pe.wait_ge(yn, t + 1)
                        if t >= 2:
                            pe.wait_ge(aff, CT * (t - 1))
                            pe.wait_ge(fin, 2 * (t - 1))
                        for c_ in range(CT):
                            m = nc.tensor.transpose(ps[:, t % 2, c_ * P:(c_ + 1) * P], yc[:, t, c_ * P:(c_ + 1) * P],
                                                    C("ident"))
                        m.then_inc(tr, 1)
                        for c_ in range(CT):
                            m = nc.tensor.matmul(ps[:, 2 + t % 2, c_ * P:(c_ + 1) * P], wg[:, c_ * P:(c_ + 1) * P],
                                                 Z(GL)[:, t * P:(t + 1) * P], start=True, stop=True)
                        m.then_inc(gm, 1)
                        rows4.products(pe, KD + each * t, KD + each * (t + 1))
        if debug is not None and last_phase == 4:
            with nc.sbuf_tensor("dbgt", [P, CT * SEQ], f32) as d, nc.semaphore("ds") as s:
                with nc.Block() as block:
                    @block.sync
                    def _(sp):
                        sp.dma_start(d[:], yr_dram).then_inc(s, 16)
                        sp.wait_ge(s, 16)
                return dump(nc, ctx, debug, d[:])
        zst.close()

        QK, QB = 2 * HEADS, 3
        with ExitStack() as st5:
            qkT = sb(st5, "qkT", [P, QK, SEQ])
            vv = sb(st5, "vv", [P, NT, HEADS, N])
            with phase() as st:
                zm = sb(st, "zm5", [P, NT, MLA_COLS])
                wuq = sb(st, "wuq", [P, 2, HEADS * QKD])
                wukv = sb(st, "wukv", [P, HEADS * P])
                g_lat = sb(st, "g_lat", [P, Q_LORA + KV_LORA])
                g_row = sb(st, "g_row", [P, 2, QKD])
                gain = sb(st, "gain", [P, QK, QKD])
                posi = sb(st, "posi", [P, NT], i32)
                posf = sb(st, "posf", [P, NT])
                ang = sb(st, "ang", [P, NT, 16])
                turns = sb(st, "turns", [P, NT, 16])
                trig = sb(st, "trig", [P, 2, NT, 16])
                junk = sb(st, "junk5", [P, Q_LORA])
                sl = sb(st, "sl", [P, 2, NT])
                zn = sb(st, "zn", [P, 2, Q_LORA + KV_LORA])
                znT = sb(st, "znT", [P, 2, 3, P])
                qk = sb(st, "qk", [P, QB, QK, QKD])
                sqk = sb(st, "sqk", [P, QK, QKD])
                ssn = sb(st, "ssn", [P, NT, QK])
                rot = sb(st, "rot", [P, 2, 2, QK, 16])
                zrow = sb(st, "zrow", [P, D])
                z_in, z_out, m_in, w_in5, lat, root, dch, ang_s, trig_s, zn_s, trl, trl_ev, up, q_ev, v_ev, k_ev, pe_ev, sq_s, \
                    ssn_s, nroot, nrm, gained, roped, trq, trq_a, trq_d, gain_s = sems(
                        st, "z_in", "z_out", "m_in", "w_in5", "lat", "root5", "dch5", "ang_s", "trig_s", "zn_s", "trl", "trl_ev", "up5",
                        "q_ev", "v_ev", "k_ev", "pe_ev", "sq_s5", "ssn_s", "nroot", "nrm", "gained", "roped", "trq",
                        "trq_a", "trq_d", "gain_s")
                with nc.Block() as block:
                    @block.sync
                    def _(sp):
                        sp.dma_start(zm[:].rearrange("p t n -> p (t n)"), zm_dram).then_inc(m_in, 16)
                        sp.dma_start(posi[:], pos).then_inc(m_in, 16)
                        sp.dma_start(g_row[:].rearrange("p a n -> p (a n)"),
                                     qk_gain.broadcast_to([P, 2 * QKD])).then_inc(m_in, 16)
                        sp.dma_start(g_lat[:, 0:Q_LORA], g_q_a.broadcast_to([P, Q_LORA])).then_inc(m_in, 16)
                        sp.dma_start(g_lat[:, Q_LORA:], g_kv_a.broadcast_to([P, KV_LORA])).then_inc(m_in, 16)
                        sp.dma_start(wuq[:], w_uq[0].rearrange("(k p) n -> p k n", p=P)).then_inc(w_in5, 16)
                        sp.dma_start(wukv[:], w_ukv[0]).then_inc(w_in5, 16)
                        sp.wait_ge(z_in, 1)
                        free = y_dram[SURE * P:].rearrange("(a b p) d -> a p b d", p=P, b=8)
                        for a_ in range(free.shape[0]):
                            sp.dma_start(free[a_], zrow[:].unsqueeze(1).broadcast_to([P, 8, D])).then_inc(z_out, 16)
                        sp.wait_ge(z_out, 16 * free.shape[0])

                    @block.gpsimd
                    def _(pool):
                        nc.gpsimd.memset(zrow[:], 0.0).then_inc(z_in, 1)
                        pool.wait_ge(m_in, 80)
                        for i in range(2):
                            nc.gpsimd.tensor_copy(gain[:, i * HEADS:(i + 1) * HEADS],
                                                  g_row[:, i].unsqueeze(1).broadcast_to([P, HEADS, QKD]))\
                              .then_inc(gain_s, 1)
                        pool.wait_ge(gain_s, 2)

                        def rope_keys(t):
                            if t >= QB:
                                pool.wait_ge(trq, 4 * (t - QB + 1))
                            nc.gpsimd.tensor_copy(
                                qk[:, t % QB, HEADS:, N:QKD],
                                zm[:, t, Q_LORA + KV_LORA:].unsqueeze(1).broadcast_to([P, HEADS, ROPE])).then_inc(pe_ev, 1)
                        rope_keys(0)
                        for t in range(NT):
                            if t + 1 < NT:
                                rope_keys(t + 1)
                            pool.wait_ge(nrm, t + 1)
                            nc.gpsimd.tensor_tensor(qk[:, t % QB], qk[:, t % QB], gain[:], ALU.mult)\
                              .then_inc(gained, 1)

                    @block.scalar
                    def _(act):
                        act.wait_ge(m_in, 80)
                        n = 0
                        for t in range(NT):
                            for i, (a, b) in enumerate(((0, Q_LORA), (Q_LORA, Q_LORA + KV_LORA))):
                                if n:
                                    act.wait_ge(lat, n)
                                n += 1
                                nc.scalar.activation(junk[:, 0:b - a], zm[:, t, a:b], ACT.Square,
                                                     accum_out=sl[:, i, t:t + 1]).then_inc(lat, 1)
                        act.wait_ge(ang_s, 1)
                        nc.scalar.activation(trig[:, 0], trig[:, 0], ACT.Sin).then_inc(trig_s, 1)
                        nc.scalar.activation(trig[:, 1], trig[:, 1], ACT.Sin).then_inc(trig_s, 1)
                        act.wait_ge(dch, 2)
                        nc.scalar.activation(sl[:], sl[:], ACT.Sqrt).then_inc(root, 1)

                        def latents_out(t):
                            act.wait_ge(trl, t + 1)
                            nc.scalar.activation(znT[:, t % 2].rearrange("p a n -> p (a n)"), ps[:, t % 2, 0:3 * P],
                                                 ACT.Copy).then_inc(trl_ev, 1)

                        def queries_out(t):
                            act.wait_ge(up, t + 1)
                            if t >= QB:
                                act.wait_ge(trq, 4 * (t - QB + 1))
                            nc.scalar.activation(qk[:, t % QB, 0:HEADS].rearrange("p (a h) n -> p a (h n)", a=2),
                                                 ps[:, 2:4, 0:4 * QKD], ACT.Copy).then_inc(q_ev, 1)
                            act.wait_ge(k_ev, t + 1)
                            act.wait_ge(q_ev, t + 1)
                            act.wait_ge(pe_ev, t + 1)
                            if t:
                                act.wait_ge(ssn_s, 2 * t)
                            nc.scalar.activation(sqk[:], qk[:, t % QB], ACT.Square).then_inc(sq_s, 1)

                        def values_out(t):
                            kv = ps[:, 4:6].rearrange("p a n -> p (a n)").rearrange("p (h n) -> p h n", n=P)
                            nc.scalar.activation(vv[:, t], kv[:, :, N:P], ACT.Copy).then_inc(v_ev, 1)

                        def norms(t):
                            act.wait_ge(ssn_s, 2 * t + 2)
                            nc.scalar.activation(ssn[:, t], ssn[:, t], ACT.Sqrt).then_inc(nroot, 1)
                        latents_out(0)
                        queries_out(0)
                        latents_out(1)
                        values_out(0)
                        norms(0)
                        for t in range(NT):
                            if t + 1 < NT:
                                queries_out(t + 1)
                                if t + 2 < NT:
                                    latents_out(t + 2)
                                values_out(t + 1)
                                norms(t + 1)
                            for g in (0, 2):
                                act.wait_ge(trq, 4 * t + g + 1)
                                nc.scalar.activation(qkT[0:QKD, 4 * g:4 * g + 4, t * P:(t + 1) * P],
                                                     ps[0:QKD, 6 + g % 2].rearrange("p (h n) -> p h n", h=4), ACT.Copy)\
                                   .then_inc(trq_a, 1)

                    @block.vector
                    def _(dve):
                        link = Chain(dve, dch)
                        dve.wait_ge(lat, 2 * NT)
                        link(nc.vector.tensor_scalar(sl[:, 0], sl[:, 0], 1.0 / Q_LORA, EPS, ALU.mult, ALU.add))
                        link(nc.vector.tensor_scalar(sl[:, 1], sl[:, 1], 1.0 / KV_LORA, EPS, ALU.mult, ALU.add))
                        link(nc.vector.tensor_copy(posf[:], posi[:]))
                        link(nc.vector.tensor_tensor(ang[:], posf[:].unsqueeze(2).broadcast_to([P, NT, 16]),
                                                     C("freq").unsqueeze(1).broadcast_to([P, NT, 16]), ALU.mult))
                        big = 1.5 * 2.0 ** 23
                        for i, shift in enumerate((0.0, 0.25)):
                            link(nc.vector.tensor_scalar(turns[:], ang[:], 1.0 / (2 * math.pi), shift,
                                                         ALU.mult, ALU.add))
                            link(nc.vector.tensor_scalar(turns[:], turns[:], big, None, ALU.add))
                            link(nc.vector.tensor_scalar(turns[:], turns[:], -big, None, ALU.add))
                            src = ang[:]
                            for part_ in two_pi_parts():
                                link(nc.vector.scalar_tensor_tensor(trig[:, i], turns[:], -part_, src,
                                                                    ALU.mult, ALU.add))
                                src = trig[:, i]
                            link(nc.vector.tensor_scalar(trig[:, i], trig[:, i], math.pi / 2 if i else 0.0, 3.1415925,
                                                         ALU.add, ALU.min))
                            link(nc.vector.tensor_scalar(trig[:, i], trig[:, i], -3.1415925, None, ALU.max))
                        nc.vector.tensor_copy(posf[:], posi[:]).then_inc(ang_s, 1)
                        dve.wait_ge(root, 1)
                        link(nc.vector.reciprocal(sl[:], sl[:]))
                        dve.wait_ge(trig_s, 2)

                        def latents(t):
                            if t >= 2:
                                dve.wait_ge(trl, t - 1)
                            nc.vector.scalar_tensor_tensor(zn[:, t % 2, 0:Q_LORA], zm[:, t, 0:Q_LORA], sl[:, 0, t:t + 1],
                                                           g_lat[:, 0:Q_LORA], ALU.mult, ALU.mult).then_inc(zn_s, 1)
                            nc.vector.scalar_tensor_tensor(zn[:, t % 2, Q_LORA:], zm[:, t, Q_LORA:Q_LORA + KV_LORA],
                                                           sl[:, 1, t:t + 1], g_lat[:, Q_LORA:], ALU.mult, ALU.mult)\
                              .then_inc(zn_s, 1)

                        def keys_out(t):
                            dve.wait_ge(up, t + 1)
                            if t >= QB:
                                dve.wait_ge(trq, 4 * (t - QB + 1))
                            kv = ps[:, 4:6].rearrange("p a n -> p (a n)").rearrange("p (h n) -> p h n", n=P)
                            nc.vector.tensor_copy(qk[:, t % QB, HEADS:, 0:N], kv[:, :, 0:N]).then_inc(k_ev, 1)

                        def mean_squares(t):
                            dve.wait_ge(sq_s, t + 1)
                            nc.vector.tensor_reduce(ssn[:, t], sqk[:], AX.X, ALU.add).then_inc(ssn_s, 1)
                            dve.wait_ge(ssn_s, 2 * t + 1)
                            nc.vector.tensor_scalar(ssn[:, t], ssn[:, t], 1.0 / QKD, EPS, ALU.mult, ALU.add)\
                              .then_inc(ssn_s, 1)

                        def transposed_out(t, g):
                            dve.wait_ge(trq, 4 * t + g + 1)
                            nc.vector.tensor_copy(qkT[0:QKD, 4 * g:4 * g + 4, t * P:(t + 1) * P],
                                                  ps[0:QKD, 6 + g % 2].rearrange("p (h n) -> p h n", h=4))\
                              .then_inc(trq_d, 1)
                        latents(0)
                        latents(1)
                        keys_out(0)
                        mean_squares(0)
                        for t in range(NT):
                            b = t % QB
                            dve.wait_ge(nroot, t + 1)
                            link(nc.vector.reciprocal(ssn[:, t], ssn[:, t]))
                            nc.vector.tensor_tensor(qk[:, b], qk[:, b],
                                                    ssn[:, t].unsqueeze(2).broadcast_to([P, QK, QKD]), ALU.mult)\
                              .then_inc(nrm, 1)
                            if t:
                                transposed_out(t - 1, 1)
                            if t + 2 < NT:
                                latents(t + 2)
                            if t:
                                transposed_out(t - 1, 3)
                            if t + 1 < NT:
                                keys_out(t + 1)
                            dve.wait_ge(gained, t + 1)
                            if t:
                                dve.wait_ge(roped, 2 * t)
                            for i in range(2):
                                tri = trig[:, i, t].unsqueeze(1).broadcast_to([P, QK, 16])
                                for j in range(2):
                                    link(nc.vector.tensor_tensor(rot[:, i, j], qk[:, b, :, N + 16 * j:N + 16 * j + 16],
                                                                 tri, ALU.mult))
                            nc.vector.tensor_tensor(qk[:, b, :, N:N + 16], rot[:, 1, 0], rot[:, 0, 1],
                                                    ALU.subtract).then_inc(roped, 1)
                            nc.vector.tensor_tensor(qk[:, b, :, N + 16:QKD], rot[:, 1, 1], rot[:, 0, 0],
                                                    ALU.add).then_inc(roped, 1)
                            if t + 1 < NT:
                                mean_squares(t + 1)
                        transposed_out(NT - 1, 1)
                        transposed_out(NT - 1, 3)

                    @block.tensor
                    def _(pe):
                        pe.wait_ge(w_in5, 32)

                        def latent_transposes(t):
                            pe.wait_ge(zn_s, 2 * t + 2)
                            if t >= 2:
                                pe.wait_ge(trl_ev, t - 1)
                            for i in range(3):
                                m = nc.tensor.transpose(ps[:, t % 2, i * P:(i + 1) * P],
                                                        zn[:, t % 2, i * P:(i + 1) * P], C("ident"))
                            m.then_inc(trl, 1)

                        def up_projections(t):
                            pe.wait_ge(trl_ev, t + 1)
                            if t:
                                pe.wait_ge(q_ev, t)
                                pe.wait_ge(k_ev, t)
                                pe.wait_ge(v_ev, t)
                            for i in range(2):
                                for k in range(2):
                                    nc.tensor.matmul(ps[:, 2 + i, 0:4 * QKD], znT[:, t % 2, k],
                                                     wuq[:, k, i * 4 * QKD:(i + 1) * 4 * QKD],
                                                     start=(k == 0), stop=(k == 1))
                            for i in range(2):
                                m = nc.tensor.matmul(ps[:, 4 + i], znT[:, t % 2, 2], wukv[:, i * 512:(i + 1) * 512],
                                                     start=True, stop=True)
                            m.then_inc(up, 1)
                        for t in range(2):
                            latent_transposes(t)
                            up_projections(t)
                        for t in range(NT):
                            if t + 2 < NT:
                                latent_transposes(t + 2)
                                up_projections(t + 2)
                            pe.wait_ge(roped, 2 * t + 2)
                            for g in range(4):
                                done = trq_d if g % 2 else trq_a
                                if 2 * t + g // 2:
                                    pe.wait_ge(done, 2 * t + g // 2)
                                for i in range(4):
                                    m = nc.tensor.transpose(ps[0:QKD, 6 + g % 2, i * P:(i + 1) * P],
                                                            qk[:, t % QB, 4 * g + i], C("ident"))
                                m.then_inc(trq, 1)

            if debug is not None and last_phase == 5:
                return dump(nc, ctx, debug, YTM[:].rearrange("p a b -> p (a b)"))

            with phase() as st:
                prob = sb(st, "prob", [P, 2, SEQ])
                pT = sb(st, "pT", [P, 2, NT, P])
                orow = sb(st, "orow", [P, NT, D_RWKV])
                nmax = sb(st, "nmax", [P, HEADS * NT])
                rsum = sb(st, "rsum", [P, HEADS * NT])
                s_mm, mx, nm, e_s, rec, tp, tp_d, tp_a, av, o_ev, tf, tf_ev = sems(
                    st, "s_mm", "mx", "nm", "e_s", "rec", "tp", "tp_d", "tp_a", "av", "o_ev", "tf", "tf_ev")
                items = [(h, i) for h in range(HEADS) for i in range(NT)]
                wide = [n for n, (h, i) in enumerate(items) if i >= 4]
                SCALE = QKD ** -0.5

                def wides(n):
                    return sum(w < n for w in wide)
                with nc.Block() as block:
                    @block.tensor
                    def _(pe):
                        def scores(n):
                            h, i = items[n]
                            if n >= 2:
                                pe.wait_ge(e_s, n - 1)
                            bank = 2 * (n % 2)
                            q = qkT[0:QKD, h, i * P:(i + 1) * P]
                            kT_ = qkT[0:QKD, HEADS + h]
                            for a in range(0, i * P, 512):
                                w_ = min(512, i * P - a)
                                nc.tensor.matmul(ps[:, bank + a // 512, 0:w_], q, kT_[:, a:a + w_], start=True, stop=True)
                            at = (i % 4) * P
                            o = ps[:, bank + i // 4, at:at + P]
                            nc.tensor.matmul(o, q, kT_[:, i * P:(i + 1) * P], start=True, stop=False)
                            nc.tensor.matmul(o, C("ident"), C("causal"), start=False, stop=True).then_inc(s_mm, 1)

                        def turn(n):
                            h, i = items[n]
                            pe.wait_ge(e_s, n + 1)
                            if n:
                                pe.wait_ge(tp_d, n)
                            if wides(n):
                                pe.wait_ge(tp_a, wides(n))
                            for k in range(i + 1):
                                m = nc.tensor.transpose(ps[:, 4 + k // 4, (k % 4) * P:(k % 4 + 1) * P],
                                                        prob[:, n % 2, k * P:(k + 1) * P], C("ident"))
                            m.then_inc(tp, 1)

                        def values(n):
                            h, i = items[n]
                            pe.wait_ge(tp_d, n + 1)
                            if wides(n + 1):
                                pe.wait_ge(tp_a, wides(n + 1))
                            if n >= 2:
                                pe.wait_ge(o_ev, n - 1)
                            for k in range(i + 1):
                                m = nc.tensor.matmul(ps[:, 6 + n % 2, 0:N], pT[:, n % 2, k], vv[:, k, h],
                                                     start=(k == 0), stop=(k == i))
                            m.then_inc(av, 1)
                        scores(0)
                        for n in range(len(items)):
                            if n + 1 < len(items):
                                scores(n + 1)
                            turn(n)
                            if n:
                                values(n - 1)
                        values(len(items) - 1)
                        pe.wait_ge(o_ev, len(items))
                        for t in range(NT):
                            if t >= 2:
                                pe.wait_ge(tf_ev, t - 1)
                            for c_ in range(CT):
                                m = nc.tensor.transpose(ps[:, t % 2, c_ * P:(c_ + 1) * P],
                                                        orow[:, t, c_ * P:(c_ + 1) * P], C("ident"))
                            m.then_inc(tf, 1)

                    @block.scalar
                    def _(act):
                        for n, (h, i) in enumerate(items):
                            act.wait_ge(nm, n + 1)
                            if n >= 2:
                                act.wait_ge(tp, n - 1)
                            bank = 2 * (n % 2)
                            s_ = ps[:, bank:bank + 2].rearrange("p a n -> p (a n)")[:, 0:(i + 1) * P]
                            nc.scalar.activation(prob[:, n % 2, 0:(i + 1) * P], s_, ACT.Exp, bias=nmax[:, n:n + 1],
                                                 scale=SCALE, accum_out=rsum[:, n:n + 1]).then_inc(e_s, 1)
                            if i >= 4:
                                act.wait_ge(tp, n + 1)
                                if n >= 2:
                                    act.wait_ge(av, n - 1)
                                nc.scalar.activation(pT[:, n % 2, 4:i + 1].rearrange("p k n -> p (k n)"),
                                                     ps[:, 5, 0:(i - 3) * P], ACT.Copy).then_inc(tp_a, 1)

                    @block.vector
                    def _(dve):
                        def peak(n):
                            h, i = items[n]
                            dve.wait_ge(s_mm, n + 1)
                            bank = 2 * (n % 2)
                            s_ = ps[:, bank:bank + 2].rearrange("p a n -> p (a n)")[:, 0:(i + 1) * P]
                            nc.vector.tensor_reduce(nmax[:, n:n + 1], s_, AX.X, ALU.max).then_inc(mx, 1)
                            dve.wait_ge(mx, n + 1)
                            nc.vector.tensor_scalar(nmax[:, n:n + 1], nmax[:, n:n + 1], -SCALE, None, ALU.mult)\
                              .then_inc(nm, 1)

                        def out_rows(n):
                            h, i = items[n]
                            dve.wait_ge(rec, n + 1)
                            dve.wait_ge(av, n + 1)
                            nc.vector.tensor_scalar(orow[:, i, h * N:(h + 1) * N], ps[:, 6 + n % 2, 0:N],
                                                    rsum[:, n:n + 1], None, ALU.mult).then_inc(o_ev, 1)
                        peak(0)
                        for n, (h, i) in enumerate(items):
                            if n + 1 < len(items):
                                peak(n + 1)
                            dve.wait_ge(e_s, n + 1)
                            nc.vector.reciprocal(rsum[:, n:n + 1], rsum[:, n:n + 1]).then_inc(rec, 1)
                            dve.wait_ge(tp, n + 1)
                            if n >= 2:
                                dve.wait_ge(av, n - 1)
                            k = min(4, i + 1)
                            nc.vector.tensor_copy(pT[:, n % 2, 0:k].rearrange("p k n -> p (k n)"), ps[:, 4, 0:k * P])\
                              .then_inc(tp_d, 1)
                            if n:
                                out_rows(n - 1)
                        out_rows(len(items) - 1)
                        for t in range(NT):
                            dve.wait_ge(tf, t + 1)
                            nc.vector.tensor_copy(YTM[:, :, t * P:(t + 1) * P],
                                                  ps[:, t % 2].rearrange("p (c n) -> p c n", c=CT)).then_inc(tf_ev, 1)
        if debug is not None and last_phase == 6:
            return dump(nc, ctx, debug, YTM[:].rearrange("p a b -> p (a b)"))

        xst = ctx.enter_context(ExitStack())
        yr = alias("yr7", [P, NT, D])
        x1 = sb(xst, "x1", [P, NT, D])
        with phase() as st:
            M = alias("M", [P, 2, KD, SEQ])
            G = sb(st, "G", [P, 2, KD, SEQ])
            hs = alias("hs", [P, 2, KD, SEQ])
            hraw = sb(st, "hraw", [P, 2, KD, SEQ])
            wh = alias("wh7", [P, 2, 1024])
            gt = sb(st, "gt7", [P, 2, 1024])[:, 0]
            wl = alias("wl7", [P, 2, 1024])
            wraw = sb(st, "wraw7", [P, 2, 1024])
            hh, hl = hs[:, 0], hs[:, 1]
            yl, yh = yr[:, 0:CT], yr[:, CT:2 * CT]
            ml, mh = M[:, 0], M[:, 1]
            vh = hs[:, 0, 0:CT]
            wo_l = hs[:, 1]
            PIECE = 2

            def wo_h(k):
                return hs[:, 0, (k + CT) % KD]
            y_in, wo_in, gt_in, x_in7, w_hi, w_lo, h_hi, h_lo, y_hi, y_lo, v_hi, v_lo, g_mm, g_ev, b_mm, mer, m_add, \
                m_hi, m_lo, wo_hi, wo_lo, o_mm, o_ev, o_add = sems(
                    st, "y_in7", "wo_in", "gt_in7", "x_in7", "w_hi", "w_lo", "h_hi", "h_lo", "y_hi", "y_lo", "v_hi",
                    "v_lo", "g_mm", "g_ev", "b_mm", "mer", "m_add", "m_hi", "m_lo", "wo_hi", "wo_lo", "o_mm",
                    "o_ev7", "o_add")
            w_in = slots(st, "w_in7", 2)
            h_in = slots(st, "h_in7", KD // PIECE)
            h_v = h_dram.rearrange("p (k s) -> p k s", k=KD)
            N_GATES = 2 * KD

            def flat(ap):
                return ap.rearrange("p a n -> p (a n)")

            def high(dst, src):
                return nc.scalar.activation(dst, src, ACT.Copy)

            def low(dst, src, hi):
                return nc.vector.tensor_tensor(dst, src, hi.bitcast(f32), ALU.subtract)
            with nc.Block() as block:
                @block.sync
                def _(sp):
                    def gate_weights(i, br):
                        src = w_gates[bass.ds(i + br * KD, 1)].rearrange("a p k n -> (a p) (k n)")
                        sp.dma_start(wraw[:, br], src).then_inc(w_in[br], 16)

                    def branch_weights(i, b):
                        src = w_br[bass.ds(i, 1)].rearrange("a p b k n -> (a p) (b k n)")
                        sp.dma_start(wraw[:, b], src).then_inc(w_in[b], 16)
                    gate_weights(0, 0)
                    for j in range(KD // PIECE):
                        rows = slice(PIECE * j, PIECE * (j + 1))
                        sp.dma_start(hraw[:, 1, rows], h_v[:, rows]).then_inc(h_in[j], 16)
                        if j == 0:
                            gate_weights(0, 1)
                    sp.dma_start(flat(x1[:, 0:CT]), yr_dram).then_inc(y_in, 16)
                    with sp.Fori(0, KD - 1) as i:
                        for br in range(2):
                            sp.wait_ge(g_mm, 2 * i + (br + 1))
                            gate_weights(i + 1, br)
                    for b in range(2):
                        sp.wait_ge(g_mm, N_GATES - 1 + b)
                        branch_weights(b, b)
                    sp.dma_start(hraw[:, 1], w_out[0].rearrange("(k p) n -> p k n", p=P)).then_inc(wo_in, 16)
                    with sp.Fori(0, KD // 2 - 1) as i:
                        for b in range(2):
                            sp.wait_ge(b_mm, 4 * i + (2 * b + 2))
                            branch_weights(2 * i + (2 + b), b)
                    sp.wait_ge(b_mm, 2 * KD)
                    sp.dma_start(x1[:], x[0].rearrange("(t p) d -> p t d", p=P)).then_inc(x_in7, 16)
                    sp.dma_start(gt, mod_dram[:, 2 * D:3 * D].broadcast_to([P, D])).then_inc(gt_in, 16)

                @block.tensor
                def _(pe):
                    def three(out, wt, mov, k, kn):
                        nc.tensor.matmul(out, wt[0], mov[0], start=(k == 0), stop=False)
                        nc.tensor.matmul(out, wt[0], mov[1], start=False, stop=False)
                        return nc.tensor.matmul(out, wt[1], mov[0], start=False, stop=(k == kn - 1))

                    def gate_tile(i, br, first):
                        pe.wait_ge(w_lo, 2 * i + (br + 1))
                        if not first:
                            pe.wait_ge(g_ev, 2 * i + (br - 1))
                        for k in range(KD):
                            if first and br == 0 and k % PIECE == 0:
                                pe.wait_ge(h_lo, k // PIECE + 1)
                            cols = slice(k * P, (k + 1) * P)
                            for n in range(2):
                                at = slice(n * 512, (n + 1) * 512)
                                m = three(ps[:, 4 * br + n], (wh[:, br, cols], wl[:, br, cols]),
                                          (hh[:, k, at], hl[:, k, at]), k, KD)
                        m.then_inc(g_mm, 1)
                    for br in range(2):
                        gate_tile(0, br, True)
                    with pe.Fori(1, KD) as i:
                        for br in range(2):
                            gate_tile(i, br, False)

                    def branch_tile(i, b, first):
                        pe.wait_ge(w_lo, 2 * i + (b + 1 + N_GATES))
                        for br, mov in enumerate(((yh, yl), (vh, v_lo7))):
                            if first:
                                pe.wait_ge(v_lo if br else y_lo, 1)
                                if br == 0:
                                    pe.wait_ge(g_ev, N_GATES - 1 + b)
                            else:
                                pe.wait_ge(mer, 4 * i + (2 * b + br - 3))
                            for n in range(2):
                                at = slice(n * 512, (n + 1) * 512)
                                for k in range(CT):
                                    cols = slice((br * CT + k) * P, (br * CT + k + 1) * P)
                                    m = three(ps[:, 4 * b + 2 * br + n], (wh[:, b, cols], wl[:, b, cols]),
                                              (mov[0][:, k, at], mov[1][:, k, at]), k, CT)
                            m.then_inc(b_mm, 1)
                    for b in range(2):
                        branch_tile(0, b, True)
                    with pe.Fori(1, KD // 2) as i:
                        for b in range(2):
                            branch_tile(i, b, False)
                    pe.wait_ge(mer, 2 * KD - 2)
                    for t in range(NT):
                        if t >= 4:
                            pe.wait_ge(o_ev, t - 3)
                        rows = slice(t * P, (t + 1) * P)
                        for k in range(KD):
                            if t == 0:
                                pe.wait_ge(m_lo, k + 1)
                                pe.wait_ge(wo_lo, k + 1)
                            for n in range(2):
                                at = slice(n * 512, (n + 1) * 512)
                                m = three(ps[:, 2 * (t % 4) + n], (mh[:, k, rows], ml[:, k, rows]),
                                          (wo_h(k)[:, at], wo_l[:, k, at]), k, KD)
                        m.then_inc(o_mm, 1)

                @block.scalar
                def _(act):
                    def weights(b, count):
                        act.wait_ge(w_in[b], count)
                        high(wh[:, b], wraw[:, b]).then_inc(w_hi, 1)
                    weights(0, 16)
                    for j in range(KD // PIECE):
                        rows = slice(PIECE * j, PIECE * (j + 1))
                        act.wait_ge(h_in[j], 16)
                        high(hh[:, rows], hraw[:, 1, rows]).then_inc(h_hi, 1)
                        if j == 1:
                            weights(1, 16)
                    act.wait_ge(y_in, 16)
                    high(yh, x1[:, 0:CT]).then_inc(y_hi, 1)

                    def gate(i, br):
                        act.wait_ge(g_mm, 2 * i + (br + 1))
                        out_t = G[:, br, bass.ds(i, 1)].rearrange("p a n -> p (a n)")
                        nc.scalar.activation(out_t, flat(ps[:, 4 * br:4 * br + 2]), ACT.Sigmoid).then_inc(g_ev, 1)
                    with act.Fori(0, KD - 1) as i:
                        for br in range(2):
                            gate(i, br)
                            weights(br, i * 16 + 32)
                    for br in range(2):
                        gate(KD - 1, br)
                        if br:
                            high(vh, YTM[:]).then_inc(v_hi, 1)
                        weights(br, KD * 16 + 16)

                    def merged(i):
                        act.wait_ge(m_add, i + 1)
                        src, dst = (g[:, bass.ds(i, 1)].rearrange("p a n -> p (a n)") for g in (G[:, 0], mh))
                        high(dst, src).then_inc(m_hi, 1)
                    with act.Fori(0, KD // 2 - 1) as i:
                        for b in range(2):
                            weights(b, i * 16 + (KD * 16 + 32))
                            merged(2 * i + b)

                    def out_weights(k):
                        high(wo_h(k), hraw[:, 1, k]).then_inc(wo_hi, 1)
                    act.wait_ge(wo_in, 16)
                    for b in range(2):
                        out_weights(2 * b)
                        out_weights(2 * b + 1)
                        merged(KD - 2 + b)
                    act.wait_ge(b_mm, 2 * KD)
                    for k in range(CT, KD):
                        out_weights(k)

                @block.vector
                def _(dve):
                    def weights(b, count):
                        dve.wait_ge(w_hi, count)
                        low(wl[:, b], wraw[:, b], wh[:, b]).then_inc(w_lo, 1)
                    weights(0, 1)
                    for j in range(KD // PIECE):
                        rows = slice(PIECE * j, PIECE * (j + 1))
                        dve.wait_ge(h_hi, j + 1)
                        low(hl[:, rows], hraw[:, 1, rows], hh[:, rows]).then_inc(h_lo, 1)
                        if j == 1:
                            weights(1, 2)
                    dve.wait_ge(y_hi, 1)
                    low(yl, x1[:, 0:CT], yh).then_inc(y_lo, 1)
                    with dve.Fori(0, KD - 1) as i:
                        for br in range(2):
                            weights(br, 2 * i + (br + 3))
                    weights(0, N_GATES + 1)
                    dve.wait_ge(v_hi, 1)
                    low(v_lo7[:], YTM[:], vh).then_inc(v_lo, 1)
                    weights(1, N_GATES + 2)

                    def merge(i, b):
                        m = 2 * i + b
                        g = [G[:, br, bass.ds(m, 1)].rearrange("p a n -> p (a n)") for br in range(2)]
                        for br in range(2):
                            dve.wait_ge(g_ev, N_GATES)
                            dve.wait_ge(b_mm, 2 * m + (br + 1))
                            nc.vector.tensor_tensor(g[br], g[br], flat(ps[:, 4 * b + 2 * br:4 * b + 2 * br + 2]),
                                                    ALU.mult).then_inc(mer, 1)
                        dve.wait_ge(mer, 2 * m + 2)
                        nc.vector.tensor_tensor(g[0], g[0], g[1], ALU.add).then_inc(m_add, 1)

                    def merged(m):
                        dve.wait_ge(m_hi, m + 1)
                        g = [g_[:, bass.ds(m, 1)].rearrange("p a n -> p (a n)") for g_ in (ml, G[:, 0], mh)]
                        low(*g).then_inc(m_lo, 1)

                    def out_weights(k):
                        dve.wait_ge(wo_hi, k + 1)
                        low(wo_l[:, k], hraw[:, 1, k], wo_h(k)).then_inc(wo_lo, 1)
                    with dve.Fori(0, KD // 2 - 1) as i:
                        for b in range(2):
                            merge(i, b)
                            weights(b, 2 * i + (b + N_GATES + 3))
                            merged(2 * i + b)
                    for b in range(2):
                        merge(KD // 2 - 1, b)
                        out_weights(2 * b)
                        out_weights(2 * b + 1)
                        merged(KD - 2 + b)
                    for k in range(CT, KD):
                        out_weights(k)
                    dve.wait_ge(gt_in, 16)
                    dve.wait_ge(x_in7, 16)
                    for t in range(NT):
                        dve.wait_ge(o_mm, t + 1)
                        if t >= 2:
                            dve.wait_ge(o_add, t - 1)
                        tmp = wraw[:, t % 2]
                        nc.vector.tensor_tensor(tmp, flat(ps[:, 2 * (t % 4):2 * (t % 4) + 2]),
                                                gt, ALU.mult).then_inc(o_ev, 1)
                        dve.wait_ge(o_ev, t + 1)
                        nc.vector.tensor_tensor(x1[:, t], x1[:, t], tmp, ALU.add).then_inc(o_add, 1)
        if debug is not None and last_phase == 7:
            return dump(nc, ctx, debug, x1[:].rearrange("p a b -> p (a b)"))

        with phase() as st:
            shf = sb(st, "shf", [P, D])
            scf = sb(st, "scf", [P, D])
            wr = sb(st, "wr8", [P, KD, NG + NE])
            br_ = sb(st, "br8", [P, NG + NE])
            tok_i = sb(st, "tok_i", [P, NT], i32)
            zero_i = sb(st, "zero_i", [P, NBLK + 1], i32)
            h2 = sb(st, "h2", [P, 3, D])
            junk = sb(st, "junk8", [P, D])
            h2T = sb(st, "h2T", [P, 2, KD, P])
            ss = sb(st, "ss8", [P, NT])
            lg = sb(st, "lg", [P, NT, NG + NE])
            g1 = sb(st, "g1", [P, NT, NG])
            gsum = sb(st, "gsum", [P, NT])
            e1 = sb(st, "e1", [P, NT, NE])
            e2 = sb(st, "e2", [P, NT, NE])
            hot = sb(st, "hot", [P, 2, NT, NE])
            both = sb(st, "both", [P, NT, NE])
            rank = sb(st, "rank", [P, NT, NE])
            run = sb(st, "run", [P, NT + 1, NE])
            blk = sb(st, "blk", [P, NE])
            inc = sb(st, "inc", [P, NE])
            cmp_ = sb(st, "cmp", [P, NE * (NBLK + 1)])
            m1 = sb(st, "m1", [P, 4, NT])
            tbf = sb(st, "tbf", [1, NBLK + 2])
            mods, ssq, msq, root, h2_s, h2_mid, tr, tr_ev, lmm, lg_s, dch, ge, gx, mm8, z_s, plc, tb_s, x1_out = sems(
                st, "mods", "ssq8", "msq", "root8", "h2_s", "h2_mid", "tr8", "tr_ev8", "lmm", "lg_s", "dch8", "ge",
                "gx", "mm8", "z_s", "plc", "tb_s", "x1_out")
            h2_out = slots(st, "h2_out", 3)
            h2_v = h2_dram.rearrange("(t p) d -> t p d", p=P)
            with nc.Block() as block:
                @block.sync
                def _(sp):
                    sp.dma_start(scf[:], mod_dram[:, 4 * D:5 * D].broadcast_to([P, D])).then_inc(mods, 16)
                    sp.dma_start(shf[:], mod_dram[:, 3 * D:4 * D].broadcast_to([P, D])).then_inc(mods, 16)
                    sp.dma_start(wr[:], w_router).then_inc(mods, 16)
                    sp.dma_start(br_[:], b_router.broadcast_to([P, NG + NE])).then_inc(mods, 16)
                    sp.dma_start(tok_i[:], tokens).then_inc(mods, 16)
                    sp.dma_start(x1_dram, x1[:].rearrange("p t d -> p (t d)")).then_inc(x1_out, 16)
                    for t in range(NT):
                        sp.wait_ge(h2_s, t + 1)
                        sp.dma_start(h2_v[t], h2[:, t % 3]).then_inc(h2_out[t % 3], 16)
                    sp.wait_ge(x1_out, 16)
                    for b in range(3):
                        sp.wait_ge(h2_out[b], 16 * len(range(b, NT, 3)))

                @block.gpsimd
                def _(pool):
                    nc.gpsimd.memset(zero_i[:], 0).then_inc(z_s, 1)
                    pool.wait_ge(z_s, 1)
                    pool.dma_start(slot_dram.rearrange("(p b) a -> p (b a)", p=P), zero_i[:]).then_inc(scattered, 16)
                    pool.wait_ge(scattered, 16)
                    pool.wait_ge(mods, 80)
                    pool.wait_ge(plc, 2)
                    for i in range(2):
                        for t in range(NT):
                            pool.indirect_dma_start(
                                out=slot_dram, in_=tok_i[:, t:t + 1], in_offset=None,
                                out_offset=bass.IndirectOffsetOnAxis(ap=place[:, i, t:t + 1].bitcast(u32), axis=0),
                            ).then_inc(scattered, 16)
                    pool.wait_ge(scattered, 16 + 2 * NT * 16)

                @block.scalar
                def _(act):
                    for t in range(NT):
                        if t:
                            act.wait_ge(ssq, t)
                        nc.scalar.activation(junk[:], x1[:, t], ACT.Square, accum_out=ss[:, t:t + 1]).then_inc(ssq, 1)
                    act.wait_ge(msq, 1)
                    nc.scalar.activation(ss[:], ss[:], ACT.Sqrt).then_inc(root, 1)
                    for t in range(NT):
                        for g in range(2):
                            act.wait_ge(tr, 2 * t + g + 1)
                            if t >= 2:
                                act.wait_ge(lmm, t - 1)
                            nc.scalar.activation(h2T[:, t % 2, 4 * g:4 * g + 4].rearrange("p a b -> p (a b)"),
                                                 ps[:, 2 * (t % 2) + g], ACT.Copy).then_inc(tr_ev, 1)
                    act.wait_ge(ge, 1)
                    nc.scalar.activation(g1[:], g1[:], ACT.Exp).then_inc(gx, 1)
                    act.wait_ge(ge, 2)
                    nc.scalar.activation(m1[:, 2], m1[:, 2], ACT.Exp).then_inc(gx, 1)

                @block.vector
                def _(dve):
                    V = nc.vector
                    link = Chain(dve, dch)
                    dve.wait_ge(mods, 80)
                    dve.wait_ge(ssq, NT)
                    V.tensor_scalar(ss[:], ss[:], 1.0 / D, EPS, ALU.mult, ALU.add).then_inc(msq, 1)
                    dve.wait_ge(root, 1)
                    link(V.reciprocal(ss[:], ss[:]))
                    for t in range(NT + 1):
                        if t < NT:
                            b = t % 3
                            if t >= 3:
                                dve.wait_ge(h2_out[b], 16 * (t // 3))
                                dve.wait_ge(tr, 2 * (t - 2))
                            V.scalar_tensor_tensor(h2[:, b], x1[:, t], ss[:, t:t + 1], scf[:], ALU.mult, ALU.mult)\
                             .then_inc(h2_mid, 1)
                            dve.wait_ge(h2_mid, t + 1)
                            V.tensor_tensor(h2[:, b], h2[:, b], shf[:], ALU.add).then_inc(h2_s, 1)
                        if t:
                            dve.wait_ge(lmm, t)
                            V.tensor_tensor(lg[:, t - 1], ps[:, 4 + (t - 1) % 2, 0:NG + NE], br_[:], ALU.add)\
                             .then_inc(lg_s, 1)
                    dve.wait_ge(lg_s, NT)
                    G, E = lg[:, :, 0:NG], lg[:, :, NG:]

                    def wide(ap, n):
                        return ap.unsqueeze(2).broadcast_to([P, NT, n])

                    def iota(n):
                        return C("iota")[:, 0:n].unsqueeze(1).broadcast_to([P, NT, n])

                    def first_hot(dst, vals, peak, n):
                        link(V.tensor_tensor(dst, vals, wide(peak, n), ALU.not_equal))
                        link(V.scalar_tensor_tensor(dst, dst, 1000.0, iota(n), ALU.mult, ALU.add))
                        link(V.tensor_reduce(m1[:, 3], dst, AX.X, ALU.min))
                        link(V.tensor_tensor(dst, iota(n), wide(m1[:, 3], n), ALU.is_equal))
                    link(V.tensor_reduce(gsum[:], G, AX.X, ALU.max))
                    V.tensor_tensor(g1[:], G, wide(gsum[:], NG), ALU.subtract).then_inc(ge, 1)
                    first_hot(e1[:, :, 0:NG], G, gsum[:], NG)
                    link(V.tensor_copy(both[:].rearrange("p t (g e) -> p t g e", g=NG),
                                       e1[:, :, 0:NG].unsqueeze(3).broadcast_to([P, NT, NG, EPG])))
                    link(V.tensor_tensor(e2[:], E, both[:], ALU.mult))
                    link(V.tensor_scalar(both[:], both[:], -1.0, 1e30, ALU.add, ALU.mult))
                    link(V.tensor_tensor(e2[:], e2[:], both[:], ALU.add))
                    link(V.tensor_reduce(m1[:, 0], e2[:], AX.X, ALU.max))
                    first_hot(hot[:, 0], e2[:], m1[:, 0], NE)
                    link(V.scalar_tensor_tensor(e2[:], hot[:, 0], -2e30, e2[:], ALU.mult, ALU.add))
                    link(V.tensor_reduce(m1[:, 1], e2[:], AX.X, ALU.max))
                    V.tensor_tensor(m1[:, 2], m1[:, 1], m1[:, 0], ALU.subtract).then_inc(ge, 1)
                    first_hot(hot[:, 1], e2[:], m1[:, 1], NE)
                    V.tensor_tensor(both[:], hot[:, 0], hot[:, 1], ALU.add).then_inc(ge, 1)
                    dve.wait_ge(gx, 2)
                    link(V.tensor_reduce(gsum[:], g1[:], AX.X, ALU.add))
                    link(V.tensor_scalar(m1[:, 0], m1[:, 2], 1.0, None, ALU.add))
                    link(V.tensor_tensor(gsum[:], gsum[:], m1[:, 0], ALU.mult))
                    link(V.reciprocal(top[:, 0], gsum[:]))
                    link(V.tensor_tensor(top[:, 1], top[:, 0], m1[:, 2], ALU.mult))
                    dve.wait_ge(mm8, 1)
                    link(V.memset(run[:, 0], 0.0))
                    for t in range(NT):
                        link(V.tensor_tensor(run[:, t + 1], run[:, t], ps[:, 7, t * NE:(t + 1) * NE], ALU.add))
                    link(V.tensor_tensor(rank[:], run[:, 0:NT], ps[:, 6, 0:NT * NE].rearrange("p (t e) -> p t e", t=NT),
                                         ALU.add))
                    c3 = cmp_[:, 0:NE * 8].rearrange("p (e m) -> p e m", m=8)
                    link(V.tensor_tensor(c3, run[:, NT].unsqueeze(2).broadcast_to([P, NE, 8]),
                                         C("thr").unsqueeze(1).broadcast_to([P, NE, 8]), ALU.is_gt))
                    link(V.tensor_reduce(blk[:], c3, AX.X, ALU.add))
                    link(V.tensor_tensor_scan(inc[:], C("ones")[:, 0:NE], blk[:], 0.0, ALU.mult, ALU.add))
                    link(V.tensor_tensor(blk[:], inc[:], blk[:], ALU.subtract))
                    link(V.scalar_tensor_tensor(rank[:], blk[:].unsqueeze(1).broadcast_to([P, NT, NE]), float(P),
                                                rank[:], ALU.mult, ALU.add))
                    for i in range(2):
                        link(V.tensor_tensor(e1[:], hot[:, i], rank[:], ALU.mult))
                        link(V.tensor_reduce(m1[:, i], e1[:], AX.X, ALU.add))
                        V.tensor_copy(place[:, i], m1[:, i]).then_inc(plc, 1)
                    c2 = cmp_[0:1].rearrange("p (b e) -> p b e", e=NE)
                    link(V.tensor_tensor(c2, inc[0:1].unsqueeze(1).broadcast_to([1, NBLK + 1, NE]),
                                         C("iota")[0:1].unsqueeze(2).broadcast_to([1, NBLK + 1, NE]), ALU.is_le))
                    link(V.tensor_reduce(tbf[:, 0:NBLK + 1], c2, AX.X, ALU.add))
                    link(V.tensor_scalar(tbf[:, 0:NBLK + 1], tbf[:, 0:NBLK + 1], float(NE - 1), None, ALU.min))
                    NS = NBLK // B
                    link(V.tensor_scalar(cmp_[0:1, 0:NS], C("iota")[0:1, 0:NS], float(B), None, ALU.mult))
                    link(V.tensor_tensor(cmp_[0:1, 0:NS], inc[0:1, NE - 1:NE].broadcast_to([1, NS]),
                                         cmp_[0:1, 0:NS], ALU.is_gt))
                    link(V.tensor_reduce(tbf[:, NBLK + 1:NBLK + 2], cmp_[0:1, 0:NS], AX.X, ALU.add))
                    V.tensor_copy(table[:], tbf[:]).then_inc(tb_s, 1)
                    dve.wait_ge(tb_s, 1)

                @block.tensor
                def _(pe):
                    pe.wait_ge(mods, 80)
                    for t in range(NT + 1):
                        if t < NT:
                            pe.wait_ge(h2_s, t + 1)
                            if t >= 2:
                                pe.wait_ge(tr_ev, 2 * (t - 1))
                            for g in range(2):
                                for j in range(4):
                                    k = 4 * g + j
                                    m = nc.tensor.transpose(ps[:, 2 * (t % 2) + g, j * P:(j + 1) * P],
                                                            h2[:, t % 3, k * P:(k + 1) * P], C("ident"))
                                m.then_inc(tr, 1)
                        if t:
                            u = t - 1
                            pe.wait_ge(tr_ev, 2 * t)
                            if u >= 2:
                                pe.wait_ge(lg_s, u - 1)
                            for k in range(KD):
                                m = nc.tensor.matmul(ps[:, 4 + u % 2, 0:NG + NE], h2T[:, u % 2, k], wr[:, k],
                                                     start=(k == 0), stop=(k == KD - 1))
                            m.then_inc(lmm, 1)
                    pe.wait_ge(ge, 3)
                    sel = both[:].rearrange("p t e -> p (t e)")
                    nc.tensor.matmul(ps[:, 6, 0:NT * NE], C("before"), sel, start=True, stop=True)
                    nc.tensor.matmul(ps[:, 7, 0:NT * NE], C("ones"), sel, start=True, stop=True).then_inc(mm8, 1)

        if debug is not None and last_phase == 8:
            return dump(nc, ctx, debug, x1[:].rearrange("p a b -> p (a b)"))

        xst.close()

        with phase() as st:
            gu = sb(st, "gu", [P, B, 2, KD, FE])
            dn = sb(st, "dn", [P, B, 2, D])
            idx = sb(st, "idx", [P, B], i32)
            xg = sb(st, "xg", [P, B, D])
            xT = sb(st, "xT", [P, B, KD, P])
            sg = sb(st, "sg", [P, B, FE])
            hid = sb(st, "hid", [P, B, FE])
            hidT = sb(st, "hidT", [P, B, 2, P])
            yo = YTM[:, 0:B]
            gt = sb(st, "gt9", [P, D])
            gt_in, xt_s, xt_ev, gmm, sg_s, hid_mid, hid_s, ht, ht_ev, dmm, y_ev, stored, listed = sems(
                st, "gt_in9", "xt_s", "xt_ev", "gmm", "sg_s9", "hid_mid", "hid_s", "ht", "ht_ev", "dmm", "y_ev9",
                "stored", "listed")
            gu_in, dn_in, y_out = (slots(st, n, B) for n in ("gu_in", "dn_in", "y_out9"))
            wg_v = w_e_gate[0].rearrange("e (p k) n -> e p k n", k=KD)
            wu_v = w_e_up[0].rearrange("e (p k) n -> e p k n", k=KD)
            wd_v = w_e_down[0].rearrange("e (p k) n -> e p k n", k=2)
            FREE = 2 * B + 1
            GB = (2, 3, 5)

            def steps(eng):
                return eng.value_load(table[0:1, NBLK + 1:NBLK + 2], min_val=1, max_val=NBLK // B)
            with nc.Block() as block:
                @block.sync
                def _(sp):
                    sp.dma_start(gt[:], mod_dram[:, 5 * D:6 * D].broadcast_to([P, D])).then_inc(gt_in, 16)
                    n = steps(sp)
                    with sp.Fori(0, n) as i:
                        for b in range(B):
                            e = sp.value_load(table[0:1, bass.ds(B * i + b, 1)], min_val=0, max_val=NE - 1)
                            one = lambda v: v[bass.ds(e, 1)].rearrange("a p k n -> (a p) k n")
                            m = B * i + b
                            sp.wait_ge(gmm, m + (1 - B + FREE))
                            sp.dma_start(gu[:, b, 0], one(wg_v)).then_inc(gu_in[b], 16)
                            sp.dma_start(gu[:, b, 1], one(wu_v)).then_inc(gu_in[b], 16)
                            sp.wait_ge(dmm, 2 * m + (2 - 2 * B + FREE))
                            sp.dma_start(dn[:, b], one(wd_v)).then_inc(dn_in[b], 16)

                @block.gpsimd
                def _(pool):
                    n = steps(pool)

                    def fetch(m, b, count):
                        pool.wait_ge(xt_s, 2 * m + (2 - 2 * B + FREE))
                        pool.dma_start(idx[:, b:b + 1], slot_dram[bass.ds(m * P, P), :]).then_inc(idx_in[b], 16)
                        pool.wait_ge(idx_in[b], count * 16)
                        pool.sem_inc(listed, 1)
                        pool.indirect_dma_start(
                            out=xg[:, b], out_offset=None, in_=h2_dram,
                            in_offset=bass.IndirectOffsetOnAxis(ap=idx[:, b:b + 1].bitcast(u32), axis=0))\
                            .then_inc(xg_in[b], 16)
                    fetch(0, 0, 1)
                    with pool.Fori(0, n) as i:
                        for b in range(1, B):
                            fetch(B * i + b, b, i + 1)
                        fetch(B * i + B, 0, i + 2)

                @block.tensor
                def _(pe):
                    n = steps(pe)
                    for s_ in (gmm, dmm, xt_s, ht):
                        pe.sem_inc(s_, FREE)

                    def row_transposes(m, b, count):
                        pe.wait_ge(xg_in[b], count * 16)
                        pe.wait_ge(xt_ev, 2 * m + (FREE))
                        rows = xg[:, b].rearrange("p (q k) -> p k q", k=KD)
                        for g in range(2):
                            for j in range(4):
                                last = nc.tensor.transpose(ps[:, g, j * P:(j + 1) * P], rows[:, 4 * g + j], C("ident"))
                            last.then_inc(xt_s, 1)

                    def hidden_transposes(i, b):
                        m = B * i + b
                        pe.wait_ge(hid_s, m + (1 + FREE))
                        pe.wait_ge(ht_ev, m + (FREE))
                        hrows = hid[:, b].rearrange("p (q k) -> p k q", k=2)
                        for k in range(2):
                            last = nc.tensor.transpose(ps[:, 4, k * P:(k + 1) * P], hrows[:, k], C("ident"))
                        last.then_inc(ht, 1)

                    def gate_up(i, b, ks):
                        m = B * i + b
                        if 0 in ks:
                            pe.wait_ge(xt_ev, 2 * m + (2 + FREE))
                            pe.wait_ge(gu_in[b], i * 32 + 32)
                            pe.wait_ge(hid_s, m + (1 - B + FREE))
                        for k in ks:
                            last = nc.tensor.matmul(ps[:, GB[b]], xT[:, b, k], gu[:, b, :, k],
                                                    start=(k == 0), stop=(k == KD - 1))
                        if KD - 1 in ks:
                            last.then_inc(gmm, 1)

                    def down(i, b, c_):
                        m = B * i + b
                        if c_ == 0:
                            pe.wait_ge(ht_ev, m + (1 + FREE))
                            pe.wait_ge(dn_in[b], i * 16 + 16)
                        pe.wait_ge(y_ev, 2 * m + (c_ - 1 + FREE))
                        for k in range(2):
                            last = nc.tensor.matmul(ps[:, 6 + c_], hidT[:, b, k], dn[:, b, k, c_ * 512:(c_ + 1) * 512],
                                                    start=(k == 0), stop=(k == 1))
                        last.then_inc(dmm, 1)
                    row_transposes(0, 0, 1)
                    with pe.Fori(0, n) as i:
                        gate_up(i, 0, range(0, 4))
                        row_transposes(B * i + 1, 1, i + 1)
                        gate_up(i, 0, range(4, 8))
                        gate_up(i, 1, range(0, 6))
                        hidden_transposes(i, 0)
                        row_transposes(B * i + 2, 2, i + 1)
                        gate_up(i, 1, range(6, 8))
                        down(i, 0, 0)
                        down(i, 0, 1)
                        gate_up(i, 2, range(0, 6))
                        hidden_transposes(i, 1)
                        row_transposes(B * i + B, 0, i + 2)
                        gate_up(i, 2, range(6, 8))
                        down(i, 1, 0)
                        hidden_transposes(i, 2)
                        down(i, 1, 1)
                        down(i, 2, 0)
                        down(i, 2, 1)

                @block.scalar
                def _(act):
                    n = steps(act)
                    act.sem_inc(xt_ev, FREE)
                    act.sem_inc(ht_ev, FREE)
                    for s_ in y_out:
                        act.sem_inc(s_, 16)

                    def rows_in(m, b):
                        act.wait_ge(gmm, m + (1 - B + FREE))
                        for g in range(2):
                            act.wait_ge(xt_s, 2 * m + (g + 1 + FREE))
                            nc.scalar.activation(xT[:, b, 4 * g:4 * g + 4].rearrange("p a n -> p (a n)"),
                                                 ps[:, g], ACT.Copy).then_inc(xt_ev, 1)

                    def gates(i, b):
                        act.wait_ge(gmm, B * i + (b + 1 + FREE))
                        nc.scalar.activation(sg[:, b], ps[:, GB[b], 0:FE], ACT.Sigmoid).then_inc(sg_s, 1)

                    def hidden_out(i, b):
                        act.wait_ge(ht, B * i + (b + 1 + FREE))
                        nc.scalar.activation(hidT[:, b].rearrange("p a n -> p (a n)"), ps[:, 4, 0:2 * P], ACT.Copy)\
                          .then_inc(ht_ev, 1)

                    def store(i, b):
                        act.wait_ge(y_ev, 2 * B * i + (2 * b + 2 + FREE))
                        act.dma_start(y_dram[bass.ds((B * i + b) * P, P), :], yo[:, b]).then_inc(y_out[b], 16)
                    rows_in(0, 0)
                    with act.Fori(0, n) as i:
                        rows_in(B * i + 1, 1)
                        gates(i, 0)
                        hidden_out(i, 0)
                        rows_in(B * i + 2, 2)
                        gates(i, 1)
                        store(i, 0)
                        hidden_out(i, 1)
                        rows_in(B * i + B, 0)
                        gates(i, 2)
                        hidden_out(i, 2)
                        store(i, 1)
                        store(i, 2)
                    for b in range(B):
                        act.wait_ge(y_out[b], n * 16 + 16)
                    act.sem_inc(stored, 1)

                @block.vector
                def _(dve):
                    n = steps(dve)
                    dve.sem_inc(hid_s, FREE)
                    dve.sem_inc(y_ev, FREE)
                    dve.wait_ge(gt_in, 16)

                    def hidden(i, b):
                        m = B * i + b
                        dve.wait_ge(sg_s, m + 1)
                        dve.wait_ge(ht, m + (1 - B + FREE))
                        nc.vector.tensor_tensor(sg[:, b], sg[:, b], ps[:, GB[b], 0:FE], ALU.mult).then_inc(hid_mid, 1)
                        dve.wait_ge(hid_mid, m + 1)
                        nc.vector.tensor_tensor(hid[:, b], sg[:, b], ps[:, GB[b], FE:2 * FE], ALU.mult)\
                          .then_inc(hid_s, 1)

                    def rows_out(i, b):
                        m = B * i + b
                        dve.wait_ge(y_out[b], i * 16 + 16)
                        for c_ in range(2):
                            cols = slice(c_ * 512, (c_ + 1) * 512)
                            dve.wait_ge(dmm, 2 * m + (c_ + 1 + FREE))
                            nc.vector.tensor_tensor(yo[:, b, cols], ps[:, 6 + c_], gt[:, cols], ALU.mult)\
                              .then_inc(y_ev, 1)
                    with dve.Fori(0, n) as i:
                        hidden(i, 0)
                        hidden(i, 1)
                        rows_out(i, 0)
                        hidden(i, 2)
                        rows_out(i, 1)
                        rows_out(i, 2)

        with phase() as st:
            rows = sb(st, "rows", [P, 2 * NT, D])
            x1 = sb(st, "x1b", [P, NT, D])
            x1_in = slots(st, "x1_in", NT)
            x1_v = x1_dram.rearrange("p (t d) -> p t d", t=NT)
            acc, acc2, = sems(st, "acc", "acc2")
            o_out = sem(st, "o_out")
            out_v = out[0].rearrange("(t p) d -> t p d", p=P)
            with nc.Block() as block:
                @block.gpsimd
                def _(pool):
                    for t in range(NT):
                        for i in range(2):
                            pool.indirect_dma_start(
                                out=rows[:, 2 * t + i], out_offset=None, in_=y_dram,
                                in_offset=bass.IndirectOffsetOnAxis(ap=place[:, i, t:t + 1].bitcast(u32), axis=0))\
                                .then_inc(r_in[2 * t + i], 16)

                @block.vector
                def _(dve):
                    for t in range(NT):
                        dve.wait_ge(x1_in[t], 16)
                        for i in range(2):
                            dve.wait_ge(r_in[2 * t + i], 16)
                            if i:
                                dve.wait_ge(acc, 2 * t + 1)
                            nc.vector.scalar_tensor_tensor(x1[:, t], rows[:, 2 * t + i], top[:, i, t:t + 1], x1[:, t],
                                                           ALU.mult, ALU.add).then_inc(acc, 1)

                @block.sync
                def _(sp):
                    for t in range(NT):
                        sp.dma_start(x1[:, t], x1_v[:, t]).then_inc(x1_in[t], 16)
                    for t in range(NT):
                        sp.wait_ge(acc, 2 * t + 2)
                        sp.dma_start(out_v[t], x1[:, t]).then_inc(o_out, 16)
                    sp.wait_ge(o_out, 16 * NT)


def dump(nc, ctx, debug, ap):
    with nc.semaphore("dbg") as s, nc.Block() as block:
        @block.sync
        def _(sp):
            sp.dma_start(debug, ap).then_inc(s, 16)
            sp.wait_ge(s, 16)


OUT_SHAPE = (1, SEQ, D)


def kernel(**inputs):
    import concourse.bacc as bacc
    from concourse.bass_utils import run_bass_kernel_spmd

    arrays = lay_out(inputs)
    nc = bacc.Bacc("TRN2", target_bir_lowering=False, num_devices=1)
    args = {n: nc.dram_tensor(n, a.shape, mybir.dt.from_np(a.dtype), kind="ExternalInput").ap()
            for n, a in arrays.items()}
    out = nc.dram_tensor("out", OUT_SHAPE, f32, kind="ExternalOutput").ap()
    build(nc, **args, out=out)
    r = run_bass_kernel_spmd(nc, [arrays], core_ids=[0])
    return r.results[0]["out"]
```
